# Optimizing a Trainium2 kernel written in Bass

```python
import math
import jax
import jax.numpy as jnp
from jax import lax
import numpy as np

D_MODEL = 1024
BATCH = 1
SEQ = 256
DEPTH = 2

GRID_W = 64
CTX_LEN = 256
QBLK = 128
EPS = 1e-6
NEG_INF = -1e30
ROPE_DIM = 64
ROPE_BASE = 10000.0
N_MOD = 9
FFN_DIM = 2816
FFN_RES = 0.5
N_BRANCH = 3

DIFF_D = 64
DIFF_HEADS = D_MODEL // (2 * DIFF_D)
DIFF_V = 2 * DIFF_D
WIN_HEAD_DIM = 64
WIN_Q_HEADS = D_MODEL // WIN_HEAD_DIM
WIN_KV_HEADS = WIN_Q_HEADS // 4
WIN_GROUP = WIN_Q_HEADS // WIN_KV_HEADS
WINDOW = 128
WIN_SCALE = WIN_HEAD_DIM ** -0.5
MLA_HEADS = D_MODEL // 128
MLA_Q_RANK = 384
MLA_KV_RANK = 256
MLA_NOPE = 128
MLA_ROPE = ROPE_DIM
MLA_V = 128
MLA_SCALE = (MLA_NOPE + MLA_ROPE) ** -0.5

MIX_SPLITS = (
    DIFF_HEADS * 2 * DIFF_D,
    DIFF_HEADS * 2 * DIFF_D,
    DIFF_HEADS * DIFF_V,
    WIN_Q_HEADS * WIN_HEAD_DIM,
    WIN_KV_HEADS * WIN_HEAD_DIM,
    WIN_KV_HEADS * WIN_HEAD_DIM,
    MLA_Q_RANK,
    MLA_KV_RANK,
    MLA_ROPE,
    N_BRANCH * D_MODEL,
)
MIX_IN = sum(MIX_SPLITS)
MIX_CUTS = tuple(int(v) for v in np.cumsum(MIX_SPLITS)[:-1])

kernel_name = 'hybrid_diffusion_parallel_branch_block'

def rms_norm(x, g):
    xf = x.astype(jnp.float32)
    y = xf * lax.rsqrt(jnp.mean(xf * xf, axis=-1, keepdims=True) + EPS)
    return (y * g.astype(jnp.float32)).astype(x.dtype)

def modulate(x, shift, scale):
    return x * (1 + scale) + shift

def swiglu(x, w_in, w_out):
    a, b = jnp.split(x @ w_in, 2, axis=-1)
    return (jax.nn.silu(a) * b) @ w_out

def ffn_sublayer(t, shift, scale, gate, g_pre, g_post, w_in, w_out):
    y = swiglu(modulate(rms_norm(t, g_pre), shift, scale), w_in, w_out)
    return t + FFN_RES * gate * rms_norm(y, g_post)

def axial_rope_tables(n):
    rows = n // GRID_W
    row = jnp.repeat(jnp.arange(rows), GRID_W).astype(jnp.float32)
    col = jnp.tile(jnp.arange(GRID_W), rows).astype(jnp.float32)
    quarter = ROPE_DIM // 4
    inv_freq = 1.0 / (ROPE_BASE ** (jnp.arange(quarter, dtype=jnp.float32) / quarter))
    ang_r = row[:, None] * inv_freq
    ang_c = col[:, None] * inv_freq
    return (jnp.cos(ang_r), jnp.sin(ang_r), jnp.cos(ang_c), jnp.sin(ang_c))

def apply_rope2d(x, tabs):
    cr, sr, cc, sc = (t.reshape((1, t.shape[0]) + (1,) * (x.ndim - 3) + (t.shape[1],)) for t in tabs)
    xf = x.astype(jnp.float32)
    r1, r2, c1, c2 = jnp.split(xf, 4, axis=-1)
    out = jnp.concatenate([r1 * cr - r2 * sr, r2 * cr + r1 * sr,
                           c1 * cc - c2 * sc, c2 * cc + c1 * sc], axis=-1)
    return out.astype(x.dtype)

def maybe_rope(t, tabs):
    return t if tabs is None else apply_rope2d(t, tabs)

def project(hm, w_in):
    return jnp.split(hm @ w_in, MIX_CUTS, axis=-1)

def mixer_kv(parts, kv_norm_g, w_ukv, tabs):
    B, N = parts[0].shape[:2]
    a_k = maybe_rope(parts[1].reshape(B, N, DIFF_HEADS, 2, DIFF_D), tabs)
    a_v = parts[2].reshape(B, N, DIFF_HEADS, DIFF_V)
    b_k = maybe_rope(parts[4].reshape(B, N, WIN_KV_HEADS, WIN_HEAD_DIM), tabs)
    b_v = parts[5].reshape(B, N, WIN_KV_HEADS, WIN_HEAD_DIM)
    kv = (rms_norm(parts[7], kv_norm_g) @ w_ukv).reshape(B, N, MLA_HEADS, MLA_NOPE + MLA_V)
    c_kr = maybe_rope(parts[8], tabs)
    return (a_k, a_v, b_k, b_v, kv[..., :MLA_NOPE], c_kr, kv[..., MLA_NOPE:])

def mixer_q(parts, q_norm_g, w_uq, tabs):
    B, N = parts[0].shape[:2]
    a_q = maybe_rope(parts[0].reshape(B, N, DIFF_HEADS, 2, DIFF_D), tabs)
    b_q = maybe_rope(parts[3].reshape(B, N, WIN_KV_HEADS, WIN_GROUP, WIN_HEAD_DIM), tabs)
    q = (rms_norm(parts[6], q_norm_g) @ w_uq).reshape(B, N, MLA_HEADS, MLA_NOPE + MLA_ROPE)
    return (a_q, b_q, q[..., :MLA_NOPE], maybe_rope(q[..., MLA_NOPE:], tabs))

def diff_attend(q, k, v, lam):
    s = jnp.einsum('bqhnd,bkhnd->bhnqk', q, k, preferred_element_type=jnp.float32) / math.sqrt(DIFF_D)
    p = jax.nn.softmax(s, axis=-1)
    a = p[:, :, 0] - lam * p[:, :, 1]
    return jnp.einsum('bhqk,bkhe->bqhe', a.astype(v.dtype), v)

def sink_attend(q, segments, sink):
    B, Q = q.shape[:2]
    scores = []
    for k, v, mask in segments:
        s = jnp.einsum('bqhgd,bkhd->bhgqk', q, k, preferred_element_type=jnp.float32) * WIN_SCALE
        scores.append(s if mask is None else jnp.where(mask, s, NEG_INF))
    sink_col = jnp.broadcast_to(sink.astype(jnp.float32).reshape(1, WIN_KV_HEADS, WIN_GROUP, 1, 1),
                                (B, WIN_KV_HEADS, WIN_GROUP, Q, 1))
    p = jax.nn.softmax(jnp.concatenate(scores + [sink_col], axis=-1), axis=-1)
    outs = []
    start = 0
    for k, v, _ in segments:
        n = k.shape[1]
        outs.append(jnp.einsum('bhgqk,bkhd->bqhgd', p[..., start:start + n].astype(v.dtype), v))
        start += n
    return sum(outs[1:], outs[0])

def mla_attend(q_nope, q_rope, k_nope, k_rope, v):
    s = (jnp.einsum('bqhd,bkhd->bhqk', q_nope, k_nope, preferred_element_type=jnp.float32)
         + jnp.einsum('bqhr,bkr->bhqk', q_rope, k_rope, preferred_element_type=jnp.float32)) * MLA_SCALE
    p = jax.nn.softmax(s, axis=-1)
    return jnp.einsum('bhqk,bkhd->bqhd', p.astype(v.dtype), v)

def sweep_query_blocks(attend, qs, extra=()):
    S = qs[0].shape[1]
    nblk = S // QBLK
    blocks = tuple(jnp.moveaxis(q.reshape((q.shape[0], nblk, QBLK) + q.shape[2:]), 1, 0) for q in qs)
    out = lax.map(lambda xs: attend(*xs), blocks + tuple(extra))
    out = jnp.moveaxis(out, 0, 1)
    return out.reshape((out.shape[0], S) + out.shape[3:])

def band_blocks(t):
    B, S = t.shape[:2]
    nblk = S // QBLK
    tp = jnp.pad(t, [(0, 0), (QBLK, QBLK)] + [(0, 0)] * (t.ndim - 2))
    tp = tp.reshape((B, nblk + 2, QBLK) + t.shape[2:])
    band = jnp.concatenate([tp[:, :-2], tp[:, 1:-1], tp[:, 2:]], axis=2)
    return jnp.moveaxis(band, 1, 0)

def mix_latent(q, kv_lat, kv_ctx, lam, sink, band_mask, key_valid):
    a_q, b_q, c_qn, c_qr = q
    a_k, a_v, b_k, b_v, c_kn, c_kr, c_v = kv_lat
    ca_k, ca_v, cb_k, cb_v, cc_kn, cc_kr, cc_v = kv_ctx
    cat = lambda u, w: jnp.concatenate([u, w], axis=1)
    ka, va = cat(a_k, ca_k), cat(a_v, ca_v)
    ya = sweep_query_blocks(lambda qb: diff_attend(qb, ka, va, lam), (a_q,))
    yb = sweep_query_blocks(
        lambda qb, kb, vb, kvd: sink_attend(qb, ((kb, vb, band_mask & kvd[None, :]), (cb_k, cb_v, None)), sink),
        (b_q,), (band_blocks(b_k), band_blocks(b_v), key_valid))
    kn, kr, vc = cat(c_kn, cc_kn), cat(c_kr, cc_kr), cat(c_v, cc_v)
    yc = sweep_query_blocks(lambda qn, qr: mla_attend(qn, qr, kn, kr, vc), (c_qn, c_qr))
    return ya, yb, yc

def mix_context(q, kv_ctx, lam, sink):
    a_q, b_q, c_qn, c_qr = q
    a_k, a_v, b_k, b_v, c_kn, c_kr, c_v = kv_ctx
    ya = diff_attend(a_q, a_k, a_v, lam)
    yb = sink_attend(b_q, ((b_k, b_v, None),), sink)
    yc = mla_attend(c_qn, c_qr, c_kn, c_kr, c_v)
    return ya, yb, yc

def merge_branches(ya, yb, yc, gates, subln_g, lambda_init, branch_w, w_out):
    B, N = ya.shape[:2]
    ya = (rms_norm(ya, subln_g) * (1.0 - lambda_init)).reshape(B, N, DIFF_HEADS * DIFF_V)
    yb = yb.reshape(B, N, WIN_Q_HEADS * WIN_HEAD_DIM)
    yc = yc.reshape(B, N, MLA_HEADS * MLA_V)
    ga, gb, gc = jnp.split(jax.nn.sigmoid(gates), N_BRANCH, axis=-1)
    merged = ga * (ya @ branch_w[0]) + gb * (yb @ branch_w[1]) + gc * (yc @ branch_w[2])
    return merged @ w_out

def setup_inputs(seed: int = 0) -> dict:
    key = jax.random.key(seed)
    ks = jax.random.split(key, 19)
    nrm = lambda k, shape, scale: scale * jax.random.normal(k, shape, jnp.float32)
    return {
        'x': nrm(ks[0], (BATCH, SEQ, D_MODEL), 1.0),
        'c': nrm(ks[1], (BATCH, D_MODEL), 1.0),
        'ctx': nrm(ks[2], (BATCH, CTX_LEN, D_MODEL), 1.0),
        'c_ctx': nrm(ks[3], (D_MODEL,), 1.0),
        'ada_w': nrm(ks[4], (DEPTH, D_MODEL, N_MOD * D_MODEL), 0.3 * D_MODEL ** -0.5),
        'ada_b': nrm(ks[5], (DEPTH, N_MOD * D_MODEL), 0.02),
        'norm_g': 1.0 + nrm(ks[6], (DEPTH, 6, D_MODEL), 0.02),
        'ffn_w_in': nrm(ks[7], (DEPTH, 2, D_MODEL, 2 * FFN_DIM), D_MODEL ** -0.5),
        'ffn_w_out': nrm(ks[8], (DEPTH, 2, FFN_DIM, D_MODEL), FFN_DIM ** -0.5),
        'mix_w_in': nrm(ks[9], (DEPTH, D_MODEL, MIX_IN), D_MODEL ** -0.5),
        'diff_lambda': nrm(ks[10], (DEPTH, 4, DIFF_D), 0.1),
        'diff_subln_g': 1.0 + nrm(ks[11], (DEPTH, DIFF_V), 0.02),
        'win_sink': nrm(ks[12], (DEPTH, WIN_Q_HEADS), 0.5),
        'mla_q_norm_g': 1.0 + nrm(ks[13], (DEPTH, MLA_Q_RANK), 0.02),
        'mla_kv_norm_g': 1.0 + nrm(ks[14], (DEPTH, MLA_KV_RANK), 0.02),
        'mla_w_uq': nrm(ks[15], (DEPTH, MLA_Q_RANK, MLA_HEADS * (MLA_NOPE + MLA_ROPE)), MLA_Q_RANK ** -0.5),
        'mla_w_ukv': nrm(ks[16], (DEPTH, MLA_KV_RANK, MLA_HEADS * (MLA_NOPE + MLA_V)), MLA_KV_RANK ** -0.5),
        'branch_w': nrm(ks[17], (DEPTH, N_BRANCH, D_MODEL, D_MODEL), D_MODEL ** -0.5),
        'mix_w_out': nrm(ks[18], (DEPTH, D_MODEL, D_MODEL), D_MODEL ** -0.5),
    }

def reference(x, c, ctx, c_ctx, ada_w, ada_b, norm_g, ffn_w_in, ffn_w_out, mix_w_in,
              diff_lambda, diff_subln_g, win_sink, mla_q_norm_g, mla_kv_norm_g,
              mla_w_uq, mla_w_ukv, branch_w, mix_w_out):
    B, S, _ = x.shape
    tabs = axial_rope_tables(S)
    nblk = S // QBLK
    qq = jnp.arange(QBLK)[:, None]
    kk = jnp.arange(3 * QBLK)[None, :]
    band_mask = jnp.abs(kk - QBLK - qq) <= WINDOW
    kpos = jnp.arange(nblk)[:, None] * QBLK - QBLK + kk
    key_valid = (kpos >= 0) & (kpos < S)
    silu_c = jax.nn.silu(c)[:, None, :]
    silu_cc = jax.nn.silu(c_ctx)
    h = ctx
    for l in range(DEPTH):
        last = l == DEPTH - 1
        lambda_init = 0.8 - 0.6 * math.exp(-0.3 * l)
        mx = jnp.split(silu_c @ ada_w[l] + ada_b[l], N_MOD, axis=-1)
        mc = jnp.split(silu_cc @ ada_w[l] + ada_b[l], N_MOD, axis=-1)
        g = norm_g[l]
        dl = diff_lambda[l].astype(jnp.float32)
        lam = jnp.exp(jnp.sum(dl[0] * dl[1])) - jnp.exp(jnp.sum(dl[2] * dl[3])) + lambda_init
        x = ffn_sublayer(x, mx[0], mx[1], mx[2], g[0], g[1], ffn_w_in[l, 0], ffn_w_out[l, 0])
        h = ffn_sublayer(h, mc[0], mc[1], mc[2], g[0], g[1], ffn_w_in[l, 0], ffn_w_out[l, 0])
        px = project(modulate(rms_norm(x, g[2]), mx[3], mx[4]), mix_w_in[l])
        pc = project(modulate(rms_norm(h, g[2]), mc[3], mc[4]), mix_w_in[l])
        kv_x = mixer_kv(px, mla_kv_norm_g[l], mla_w_ukv[l], tabs)
        kv_c = mixer_kv(pc, mla_kv_norm_g[l], mla_w_ukv[l], None)
        q_x = mixer_q(px, mla_q_norm_g[l], mla_w_uq[l], tabs)
        ya, yb, yc = mix_latent(q_x, kv_x, kv_c, lam, win_sink[l], band_mask, key_valid)
        y = merge_branches(ya, yb, yc, px[9], diff_subln_g[l], lambda_init, branch_w[l], mix_w_out[l])
        x = x + mx[5] * rms_norm(y, g[3])
        if not last:
            q_c = mixer_q(pc, mla_q_norm_g[l], mla_w_uq[l], None)
            ca, cb, cc = mix_context(q_c, kv_c, lam, win_sink[l])
            yh = merge_branches(ca, cb, cc, pc[9], diff_subln_g[l], lambda_init, branch_w[l], mix_w_out[l])
            h = h + mc[5] * rms_norm(yh, g[3])
            h = ffn_sublayer(h, mc[6], mc[7], mc[8], g[4], g[5], ffn_w_in[l, 1], ffn_w_out[l, 1])
        x = ffn_sublayer(x, mx[6], mx[7], mx[8], g[4], g[5], ffn_w_in[l, 1], ffn_w_out[l, 1])
    return x


_drawn_inputs = setup_inputs


def setup_inputs(seed=0):
    import zlib

    import numpy as np

    out = dict(_drawn_inputs(seed))
    spreads = {}
    factors = {'norm_g': 5.389,
     'diff_lambda': 5.383,
     'diff_subln_g': 8.0,
     'win_sink': 8.0,
     'mla_q_norm_g': 8.0,
     'mla_kv_norm_g': 8.0}
    for name, (base, spread) in spreads.items():
        noise = np.random.default_rng([zlib.crc32(name.encode()), seed]).standard_normal(out[name].shape)
        drawn = base * np.exp(spread * noise) if base else spread * noise
        out[name] = jnp.asarray(drawn.astype(out[name].dtype))
    for name, factor in factors.items():
        out[name] = (out[name] * factor).astype(out[name].dtype)
    return out
```

```python
from contextlib import ExitStack

import numpy as np

import concourse.bass as bass
from concourse import mybir

F32 = mybir.dt.float32
F32R = mybir.dt.float32r
ALU = mybir.AluOpType
ACT = mybir.ActivationFunctionType
AX_X = mybir.AxisListType.X

P = 128
D = 1024
KC = D // P
S = 256
T = 512
LAYERS = 2
FFN = 2816
FC = FFN // P
N_MOD = 9
GRID_W = 64
ROPE = 64
EPS = 1e-6
NEG = -1e30
WINDOW = 128
Q_RANK, KV_RANK = 384, 256
QC, KVC = Q_RANK // P, KV_RANK // P
HEAD_SCALE = 64 ** -0.5
MLA_SCALE = (128 + 64) ** -0.5
LN_EXP = "natural_log_exp_and_others"
SILU = "silu_and_others"
SIGMOID = "sigmoid_and_others"

RAW = 4
SPLIT = 2
BANKS = 4
STAT, ADA_BANK = 5, 6
GROUP = 1024
ADA_RING = 2


class Idx:

    def __init__(self, c, step, i):
        self.c, self.step, self.i = c, step, i

    def plus(self, k):
        return Idx(self.c + k, self.step, self.i)

    def val(self, extra=0):
        if isinstance(self.i, int):
            return self.c + self.i * self.step + extra
        return self.i * self.step + (self.c + extra)

    def ring(self, size):
        if isinstance(self.i, int):
            return (self.c + self.i * self.step) % size
        assert self.step % size == 0
        return self.c % size

    def lap(self, size, extra=0):
        if isinstance(self.i, int):
            return (self.c + self.i * self.step) // size + extra
        assert self.step % size == 0
        return self.i * (self.step // size) + (self.c // size + extra)


def wait(eng, sem, value):
    if isinstance(value, int) and value <= 0:
        return
    eng.wait_ge(sem, value)


class Phase:

    def __init__(self, kind, layer, src=None, tokens=None, first=0, iters=0, groups=0, tiles=0, adds=None,
                 sub=None, post=None, pre=None, fill1=(), fill2=(), per_tile=1, dst=None, cols=0, x=None,
                 kpg=0, mode=None, blocks=0, nq=0, r=0):
        self.kind, self.layer, self.src, self.tokens, self.first = kind, layer, src, tokens, first
        self.iters, self.groups, self.tiles, self.adds = iters, groups, tiles, dict(adds or {})
        self.sub, self.post, self.pre, self.fill1, self.fill2 = sub, post, pre, fill1, fill2
        self.per_tile, self.dst, self.cols, self.x, self.kpg = per_tile, dst, cols, x, kpg
        self.mode, self.blocks, self.nq, self.r = mode, blocks, nq, r
        self.peel_first = self.peel_last = False


def make_plan():
    plan = []

    def add(kind, layer, **kw):
        plan.append(Phase(kind, layer=layer, **kw))

    def norm(layer, post, pre, tokens, fill1=(), fill2=()):
        adds = {"stat": bool(post) + bool(pre), "inv": bool(post) + bool(pre), "ada": len(fill1) + len(fill2)}
        if post:
            adds["x"] = KC
        if pre:
            adds.update(sq=KC, acc=KC, scaled=KC, xhi=KC, xlo=KC)
        add("norm", layer, post=post, pre=pre, tokens=tokens, fill1=fill1, fill2=fill2, adds=adds)

    norm(0, None, (0, 0), T, [(0, 0), (0, 1)], [(0, 2)])
    fills = [
        ([(0, 3), (0, 4), (0, 5)], [(0, 6), (0, 7)]),
        ([(0, 8), (1, 0)], [(1, 1)]),
        ([(1, 2), (1, 3)], [(1, 4)]),
        ([(1, 5), (1, 6)], [(1, 7)]),
        ([(1, 8)], []),
        ([], []),
    ]
    for layer in range(LAYERS):
        last = layer == LAYERS - 1
        nq = S if last else T

        def ffn(sub, tokens):
            add("ffn_in", layer, sub=sub, tokens=tokens, iters=FC // 2, groups=4, tiles=4,
                adds={"ghi": FC, "glo": FC})
            add("y", layer, src="ffn_out", sub=sub, tokens=tokens, iters=KC // 4, groups=12, tiles=4,
                per_tile=3, adds={"sq": KC, "acc": KC})

        ffn(0, T)
        norm(layer, (layer, 0), (layer, 1), T, *fills[3 * layer])
        if last:
            add("rope", layer, src="qk_a", dst="q", first=0, tokens=nq, iters=2, groups=4, tiles=4,
                adds={"rope": 8})
            add("rope", layer, src="qk_a", dst="k", first=8, tokens=T, iters=2, groups=4, tiles=4,
                adds={"rope": 8})
        else:
            add("rope", layer, src="qk_a", dst="qk", first=0, tokens=T, iters=4, groups=4, tiles=4,
                adds={"rope": 16})
        add("v", layer, src="v_a", cols=512, x="x", kpg=2, iters=2, groups=4, tiles=4)
        add("attn", layer, mode="a", blocks=8, nq=nq)
        add("merge", layer, r=0, tokens=nq, iters=4, groups=4, tiles=4)
        add("rope", layer, src="qk_b", dst="q", first=0, tokens=nq, iters=2, groups=4, tiles=4,
            adds={"rope": 8})
        add("rope", layer, src="qk_b", dst="k", first=8, tokens=T, iters=1, groups=2, tiles=2,
            adds={"rope": 2})
        add("v", layer, src="v_b", cols=256, x="x", kpg=4, iters=1, groups=2, tiles=4)
        add("attn", layer, mode="b", blocks=8, nq=nq)
        add("merge", layer, r=1, tokens=nq, iters=4, groups=4, tiles=4, adds={"m": KC})
        add("plain", layer, src="c_lat", dst="lat", tokens=T, iters=1, groups=QC + KVC, tiles=QC + KVC)
        add("rope", layer, src="c_lat", dst="kr", first=QC + KVC, tokens=T, iters=1, groups=1, tiles=1,
            adds={"rope": 1})
        add("latnorm", layer, adds={"lsq": QC + KVC, "stat": QC + KVC, "inv": 2, "lt": QC + KVC,
                                    "lhi": QC + KVC, "llo": QC + KVC})
        add("plain", layer, src="uq", dst="qn", tokens=nq, iters=1, groups=4, tiles=8)
        add("rope", layer, src="uq", dst="qr", first=8, tokens=nq, iters=1, groups=2, tiles=4,
            adds={"rope": 4})
        add("plain", layer, src="uk", dst="kn", tokens=T, iters=1, groups=2, tiles=8)
        add("v", layer, src="uv", cols=512, x="lat", kpg=2, iters=2, groups=1, tiles=4)
        add("attn", layer, mode="c", blocks=4, nq=nq)
        add("merge", layer, r=2, tokens=nq, iters=4, groups=4, tiles=4, adds={"m": KC})
        add("msplit", layer, tokens=nq, adds={"mhi": KC, "mlo": KC})
        add("y", layer, src="wo", sub=1, tokens=nq, iters=2, groups=4, tiles=4, per_tile=1,
            adds={"sq": KC, "acc": KC})
        norm(layer, (layer, 1), (layer, 2), nq, *fills[3 * layer + 1])
        ffn(2, nq)
        norm(layer, (layer, 2), None if last else (layer + 1, 0), nq, *fills[3 * layer + 2])

    at = {}
    g = n = 0
    for ph in plan:
        ph.g, ph.n, ph.at = g, n, dict(at)
        g += ph.groups * ph.iters
        n += ph.tiles * ph.iters
        if ph.kind == "attn":
            qts = list(range(ph.nq // P))
            ph.units = [(b, qt) for b in range(ph.blocks) for qt in qts]
            ph.per_block = len(qts)
            u = len(ph.units)
            ph.adds = {"score": u, "bias": u, "exp": u, "prob": u, "turned": u, "pt": u, "pv": u,
                       "yhi": ph.blocks, "ylo": ph.blocks}
            if ph.mode == "a":
                ph.adds.update(asq=ph.blocks, stat=ph.blocks, inv=ph.blocks, ynorm=ph.blocks)
        for k, v in ph.adds.items():
            at[k] = at.get(k, 0) + v
    products = [ph for ph in plan if ph.iters]
    products[0].peel_first = True
    next(ph for ph in products if ph.kind == "rope").peel_first = True
    products[-1].peel_last = True
    return plan, g


def build(nc, io, out):
    plan, all_groups = make_plan()
    lambda_init = [0.8 - 0.6 * float(np.exp(-0.3 * l)) for l in range(LAYERS)]

    with ExitStack() as ctx:
        def sb(name, shape, dt=F32):
            return ctx.enter_context(nc.sbuf_tensor(name, shape, dt))

        x = sb("x", [P, KC, T])
        work = sb("work", [P, KC, T])
        xhi = sb("xhi", [P, KC, T], F32R)
        xlo = sb("xlo", [P, KC, T], F32R)
        raw = sb("raw", [P, RAW, GROUP])
        whi = sb("whi", [P, SPLIT, GROUP], F32R)
        wlo = sb("wlo", [P, SPLIT, GROUP], F32R)
        ada = sb("ada", [P, ADA_RING, GROUP])
        cos = sb("cos", [P, S])
        sin = sb("sin", [P, S])
        ident = sb("ident", [P, P])
        mask = sb("mask", [P, 2, P])
        ones = sb("ones", [P, P])
        inv = sb("inv", [P, T])
        tmp = sb("tmp", [P, 2, T])
        acc = sb("acc", [P, T])
        mods = sb("mods", [P, LAYERS, N_MOD, KC, 2])
        ada_b = sb("ada_b", [P, LAYERS, N_MOD, KC, 2])
        norm_g = sb("norm_g", [P, LAYERS, 6, KC, 2])
        cvec = sb("cvec", [P, KC, 2])
        subg = sb("subg", [P, LAYERS])
        lat_g = sb("lat_g", [P, LAYERS, QC + KVC])
        dlam = sb("dlam", [64, LAYERS, 4])
        dprod = sb("dprod", [64, LAYERS, 2])
        elam = sb("elam", [P, LAYERS, 2])
        lam = sb("lam", [P, LAYERS])
        nsink = sb("nsink", [P, LAYERS, 16])
        sink = sb("sink", [P, LAYERS, 16])
        eps = sb("eps", [P, 1])
        mx = sb("mx", [P, 2, 2])
        nb = sb("nb", [P, 2, 2])
        sd = sb("sd", [P, 2, 2])
        se = sb("se", [P, 2, 2])
        sm = sb("sm", [P, 2, 2])
        rc = sb("rc", [P, 2, 2])

        arena_bytes = 2 * FC * T * 4
        arena_at = (nc.sbuf_usable_end - arena_bytes) // 32 * 32
        assert nc.sbuf_base <= arena_at, (nc.sbuf_base, arena_at)

        def at(name, shape, offset, dt=F32):
            assert offset + int(np.prod(shape[1:])) * 4 <= arena_bytes, name
            return nc.alloc_sbuf_tensor_at(name, shape, dt, offset=arena_at + offset)

        KB = 1024
        ghi = at("ghi", [P, FC, T], 0, F32R)
        glo = at("glo", [P, FC, T], FC * T * 4, F32R)
        qk = at("qk", [P, 16, T], 0)
        q = qk[:, 0:8, :]
        k = qk[:, 8:16, :]
        yhi = at("yhi", [P, 8, T], 0, F32R)
        v = at("v", [P, 4, D], 32 * KB)
        ylo = at("ylo", [P, 8, T], 48 * KB, F32R)
        lat = at("lat", [P, QC + KVC, T], 78 * KB)
        lhi = at("lhi", [P, QC + KVC, T], 48 * KB, F32R)
        llo = at("llo", [P, QC + KVC, T], 58 * KB, F32R)
        qr = at("qr", [P, 4, T], 68 * KB)
        kr = at("kr", [P, T], 76 * KB)
        sub_v = at("sub_v", [P, T], 68 * KB)
        prob = at("prob", [P, 2, 2, T], 78 * KB)

        ps = ctx.enter_context(nc.psum_tensor("ps", [P, 8, 512], F32))

        def sem(name):
            return ctx.enter_context(nc.semaphore(name))

        raw_loaded = [sem(f"raw_loaded{s}") for s in range(RAW)]
        ada_loaded = [sem(f"ada_loaded{s}") for s in range(ADA_RING)]
        x_loaded = sem("x_loaded")
        c_loaded = sem("c_loaded")
        consts_loaded = sem("consts_loaded")
        consts_made = sem("consts_made")
        silu_c = sem("silu_c")
        hi_ready = sem("hi_ready")
        lo_ready = sem("lo_ready")
        group_used = sem("group_used")
        bank_free = [sem(f"bank_free{b}") for b in range(BANKS)]
        ada_used = sem("ada_used")
        ada_evac = sem("ada_evac")
        done = {name: sem(f"{name}_done") for name in (
            "ghi", "glo", "sq", "acc", "stat", "inv", "x", "scaled", "xhi", "xlo", "rope", "m", "mhi",
            "mlo", "lsq", "lt", "lhi", "llo", "score", "bias", "exp", "prob", "turned", "pt", "pv",
            "yhi", "ylo", "asq", "ynorm", "refined")}
        rope_mul = sem("rope_mul")
        acc_zero = sem("acc_zero")
        lam_sum = sem("lam_sum")
        lam_exp = sem("lam_exp")
        dve_step = sem("dve_step")
        act_step = sem("act_step")
        stored = sem("stored")

        block = ctx.enter_context(nc.Block())

        def run(eng, ph, body, begin=0):
            first = 1 if ph.peel_first else begin
            last = 1 if ph.peel_last else 0
            if ph.iters == 1 or ph.groups % RAW:
                for i in range(begin, ph.iters):
                    body(i)
                return
            for i in range(begin, first):
                body(i)
            if ph.iters - first - last > 1:
                with eng.Fori(first, ph.iters - last) as i:
                    body(i)
            else:
                for i in range(first, ph.iters - last):
                    body(i)
            for i in range(ph.iters - last, ph.iters):
                body(i)

        def base(ph, name):
            return ph.at.get(name, 0)

        def streams(tokens):
            return range(tokens // S)

        def sl(s):
            return slice(s * S, (s + 1) * S)

        def source(ph, i, j):
            w = io[ph.src or ph.kind][ph.layer]

            def pick(ap, index):
                if isinstance(index, int):
                    return ap[index]
                return ap[bass.ds(index, 1)].rearrange("o p n -> (o p) n")

            if ph.kind == "ffn_in":
                return pick(w[ph.sub // 2], i * 4 + j), GROUP
            if ph.kind == "merge":
                return pick(w[ph.r], i * 4 + j), GROUP
            if ph.src == "ffn_out":
                tile, part = divmod(j, 3)
                n = GROUP if part < 2 else (FC - 16) * P
                return pick(w[ph.sub // 2], i * 4 + tile)[:, part * GROUP:part * GROUP + n], n
            first = 4 if (ph.src, ph.kind) == ("uq", "rope") else ph.first
            n = w.shape[-1]
            return pick(w, i * ph.groups + (first + j)), n

        def last_group(ph, i, j):
            if ph.kind == "v":
                own = ph.groups - 1
            elif ph.src == "ffn_out":
                own = 3 * j + 2
            else:
                own = j * ph.groups // ph.tiles
            return Idx(ph.g + own, ph.groups, i)

        def bank(ph, i, j):
            return Idx(ph.n + j, ph.tiles, i)

        def tiles_before(ph, b):
            return (ph.n - b + BANKS - 1) // BANKS

        def chunk(t, c, tokens):
            if isinstance(c.i, int):
                return t[:, c.val(), 0:tokens]
            return t[:, bass.ds(c.val(), 1), 0:tokens].rearrange("p o n -> p (o n)")

        def split_ahead(split, ph, i, j):
            per_group = ph.tiles // ph.groups
            if j % per_group == 0:
                split(Idx(ph.g + j // per_group + 1, ph.groups, i))

        def rope_dst(ph, i, j, cols):
            if ph.dst == "kr":
                return kr[:, cols]
            t = {"q": q, "k": k, "qk": qk, "qr": qr}[ph.dst]
            if isinstance(i, int):
                return t[:, i * ph.tiles + j, cols]
            return t[:, bass.ds(i * ph.tiles + j, 1), cols].rearrange("p o n -> p (o n)")

        ada_order = [lm for ph in plan if ph.kind == "norm" for lm in (*ph.fill1, *ph.fill2)]
        ada_number = {lm: n for n, lm in enumerate(ada_order)}
        assert sorted(ada_order) == [(l, m) for l in range(LAYERS) for m in range(N_MOD)]

        def refine(dve, step, dst, bank_, tokens, width, scratch):
            vs, sq = (t[:, 0:tokens] for t in scratch)
            dve.tensor_scalar(vs, ps[:, bank_, 0:tokens], 1.0 / width, EPS, ALU.mult, ALU.add)\
               .then_inc(done["refined"], 1)
            step(dve.tensor_tensor(sq, dst, dst, ALU.mult))
            step(dve.scalar_tensor_tensor(sq, sq, -0.5, vs, ALU.mult, ALU.mult))
            step(dve.scalar_tensor_tensor(dst, sq, 1.5, dst, ALU.add, ALU.mult))

        def last_unit(ph, b):
            return (b + 1) * ph.per_block - 1

        def keys(qt):
            return 0 if qt < S // P else S // P

        def act_attention(act, ph, inverse):
            units, nq = ph.units, ph.nq
            scale = MLA_SCALE if ph.mode == "c" else HEAD_SCALE

            def exp(u):
                e, nk = u % 2, T - keys(units[u][1]) * P
                act.wait_ge(done["bias"], base(ph, "bias") + u + 1)
                wait(act, done["turned"], base(ph, "turned") + u - 1 if u >= 2 else 0)
                if ph.mode == "b":
                    act.activation(se[:, e, :], sd[:, e, :], ACT.Exp)
                for n in range(2):
                    last = act.activation(prob[:, e, n, 0:nk], ps[:, 2 * e + n, 0:nk], ACT.Exp,
                                          bias=nb[:, e, n:n + 1], scale=scale, accum_out=sm[:, e, n:n + 1])
                last.then_inc(done["exp"], 1)

            def turned_copy(u):
                nk = T - keys(units[u][1]) * P
                act.wait_ge(done["turned"], base(ph, "turned") + u + 1)
                if ph.mode == "a":
                    wait(act, done["pv"], base(ph, "pv") + u - 1 if u >= 2 else 0)
                    act.activation(tmp[:, u % 2, 0:nk], ps[:, 4, 0:nk], ACT.Copy).then_inc(done["pt"], 1)
                else:
                    wait(act, done["pv"], base(ph, "pv") + u if u else 0)
                    for n in range(2):
                        last = act.activation(tmp[:, n, 0:nk], ps[:, 4 + n, 0:nk], ACT.Copy)
                    last.then_inc(done["pt"], 1)

            exp(0)
            for s in range(len(units) + 3):
                for b in range(ph.blocks):
                    if ph.mode == "a" and s == last_unit(ph, b) + 3:
                        act.wait_ge(done["ynorm"], base(ph, "ynorm") + b + 1)
                        act.activation(yhi[:, b, 0:nq], acc[:, 0:nq], ACT.Copy).then_inc(done["yhi"], 1)
                    if ph.mode != "a" and s == last_unit(ph, b) + 2:
                        act.wait_ge(done["pv"], base(ph, "pv") + last_unit(ph, b) + 1)
                        for n in range(2):
                            if ph.mode == "b":
                                half = slice(64 * n, 64 * n + 64)
                                last = act.activation(yhi[half, b, 0:nq], ps[half, 6 + n, 0:nq], ACT.Copy)
                            else:
                                last = act.activation(yhi[:, 2 * b + n, 0:nq], ps[:, 6 + n, 0:nq], ACT.Copy)
                        last.then_inc(done["yhi"], 1)
                if s + 1 < len(units):
                    exp(s + 1)
                if s < len(units):
                    turned_copy(s)
                for b in range(ph.blocks):
                    if ph.mode == "a" and s == last_unit(ph, b) + 1:
                        act.wait_ge(done["pv"], base(ph, "pv") + last_unit(ph, b) + 1)
                        wait(act, done["ylo"], base(ph, "ylo") + b)
                        act.activation(acc[:, 0:nq], ps[:, 6 + b % 2, 0:nq], ACT.Square).then_inc(done["asq"], 1)
                    if ph.mode == "a" and s == last_unit(ph, b) + 2:
                        inverse(inv[:, 0:nq], STAT, nq, P, base(ph, "stat") + b + 1)

        def dve_attention(dve, ph, step):
            units, nq, l = ph.units, ph.nq, ph.layer
            scale = MLA_SCALE if ph.mode == "c" else HEAD_SCALE

            def biases(u):
                b, qt = units[u]
                e, nk = u % 2, T - keys(qt) * P
                dve.wait_ge(done["score"], base(ph, "score") + u + 1)
                step(dve.tensor_reduce(mx[:, e, :], ps[:, 2 * e:2 * e + 2, 0:nk], AX_X, ALU.max, negate=True))
                if ph.mode == "b":
                    negs = nsink[:, l, 2 * b:2 * b + 2]
                    step(dve.scalar_tensor_tensor(nb[:, e, :], mx[:, e, :], scale, negs, ALU.mult, ALU.min))
                    dve.tensor_tensor(sd[:, e, :], sink[:, l, 2 * b:2 * b + 2], nb[:, e, :], ALU.add)\
                       .then_inc(done["bias"], 1)
                else:
                    dve.tensor_scalar(nb[:, e, :], mx[:, e, :], scale, None, ALU.mult).then_inc(done["bias"], 1)

            def normalize(u):
                e, nk = u % 2, T - keys(units[u][1]) * P
                dve.wait_ge(done["exp"], base(ph, "exp") + u + 1)
                if ph.mode == "b":
                    step(dve.tensor_tensor(sm[:, e, :], sm[:, e, :], se[:, e, :], ALU.add))
                step(dve.reciprocal(rc[:, e, :], sm[:, e, :]))
                p0, p1 = prob[:, e, 0, 0:nk], prob[:, e, 1, 0:nk]
                if ph.mode == "a":
                    step(dve.tensor_scalar(p1, p1, rc[:, e, 1:2], lam[:, l:l + 1], ALU.mult, ALU.mult))
                    dve.scalar_tensor_tensor(p0, p0, rc[:, e, 0:1], p1, ALU.mult, ALU.subtract)\
                       .then_inc(done["prob"], 1)
                else:
                    dve.tensor_scalar(p0, p0, rc[:, e, 0:1], None, ALU.mult)
                    dve.tensor_scalar(p1, p1, rc[:, e, 1:2], None, ALU.mult).then_inc(done["prob"], 1)

            biases(0)
            for s in range(len(units) + 3):
                for b in range(ph.blocks):
                    if ph.mode != "a" and s == last_unit(ph, b) + 2:
                        dve.wait_ge(done["yhi"], base(ph, "yhi") + b + 1)
                        for n in range(2):
                            if ph.mode == "b":
                                half = slice(64 * n, 64 * n + 64)
                                dst, hi, src = ylo[half, b, 0:nq], yhi[half, b, 0:nq], ps[half, 6 + n, 0:nq]
                            else:
                                c = 2 * b + n
                                dst, hi, src = ylo[:, c, 0:nq], yhi[:, c, 0:nq], ps[:, 6 + n, 0:nq]
                            last = dve.tensor_tensor(dst, src, hi.bitcast(F32), ALU.subtract)
                        last.then_inc(done["ylo"], 1)
                if s < len(units):
                    normalize(s)
                if s + 1 < len(units):
                    biases(s + 1)
                for b in range(ph.blocks):
                    if ph.mode == "a" and s == last_unit(ph, b) + 2:
                        dve.wait_ge(done["inv"], base(ph, "inv") + b + 1)
                        refine(dve, step, inv[:, 0:nq], STAT, nq, P, (sub_v, acc))
                        dve.scalar_tensor_tensor(acc[:, 0:nq], ps[:, 6 + b % 2, 0:nq], subg[:, l:l + 1],
                                                 inv[:, 0:nq], ALU.mult, ALU.mult).then_inc(done["ynorm"], 1)

        def pe_attention(pe, ph):
            units = ph.units
            for b in range(BANKS):
                pe.wait_ge(bank_free[b], tiles_before(ph, b))
            pe.wait_ge(done["rope"], base(ph, "rope"))
            wait(pe, done["refined"], base(ph, "inv"))
            wait(pe, done["pt"], base(ph, "pt"))
            wait(pe, ada_evac, base(ph, "ada"))

            def scores(u):
                b, qt = units[u]
                e, kc = u % 2, keys(units[u][1])
                nk = T - kc * P
                cols, ks = slice(qt * P, (qt + 1) * P), slice(kc * P, T)
                wait(pe, done["exp"], base(ph, "exp") + u - 1 if u >= 2 else 0)
                for n in range(2):
                    o = ps[:, 2 * e + n, 0:nk]
                    half = slice(64 * n, 64 * n + 64)
                    if ph.mode == "c":
                        pe.matmul(o, q[:, 2 * b + n, cols], k[:, 2 * b + n, ks], start=True, stop=False)
                        last = pe.matmul(o, qr[half, b, cols], kr[half, ks], start=False, stop=True)
                    else:
                        kb = b if ph.mode == "a" else b // 4
                        masked = ph.mode == "b" and kc == 0
                        last = pe.matmul(o, q[half, b, cols], k[half, kb, ks], start=True, stop=not masked)
                        if masked:
                            other = (1 - qt) * P
                            last = pe.matmul(ps[:, 2 * e + n, other:other + P], ident[:, :], mask[:, qt, :],
                                             start=False, stop=True)
                last.then_inc(done["score"], 1)

            def turn(u):
                e, nk = u % 2, T - keys(units[u][1]) * P
                pe.wait_ge(done["prob"], base(ph, "prob") + u + 1)
                wait(pe, done["pt"], base(ph, "pt") + u if u else 0)
                for n in range(1 if ph.mode == "a" else 2):
                    for c in range(nk // P):
                        cs = slice(c * P, (c + 1) * P)
                        last = pe.transpose(ps[:, 4 + n, cs], prob[:, e, n, cs], ident[:, :])
                last.then_inc(done["turned"], 1)

            def weighted(u):
                b, qt = units[u]
                kc0 = keys(qt)
                pe.wait_ge(done["pt"], base(ph, "pt") + u + 1)
                if qt == 0:
                    if ph.mode == "a":
                        wait(pe, done["ynorm"], base(ph, "ynorm") + b - 1 if b >= 2 else base(ph, "ynorm"))
                        wait(pe, done["ylo"], base(ph, "ylo") if b < 2 else 0)
                    else:
                        wait(pe, done["ylo"], base(ph, "ylo") + b)
                for n in range(1 if ph.mode == "a" else 2):
                    if ph.mode == "a":
                        to, pt, vc = 6 + b % 2, u % 2, b
                    elif ph.mode == "b":
                        to, pt, vc = 6 + n, n, b // 4
                    else:
                        to, pt, vc = 6 + n, n, 2 * b + n
                    for kc in range(kc0, T // P):
                        last = pe.matmul(ps[:, to, qt * P:(qt + 1) * P], v[:, kc, vc * P:(vc + 1) * P],
                                         tmp[:, pt, (kc - kc0) * P:(kc - kc0 + 1) * P],
                                         start=kc == kc0, stop=kc == T // P - 1)
                last.then_inc(done["pv"], 1)

            scores(0)
            for s in range(len(units) + 3):
                if s + 1 < len(units):
                    scores(s + 1)
                if s < len(units):
                    turn(s)
                if 1 <= s <= len(units):
                    weighted(s - 1)
                for b in range(ph.blocks):
                    if ph.mode == "a" and s == last_unit(ph, b) + 2:
                        pe.wait_ge(done["asq"], base(ph, "asq") + b + 1)
                        wait(pe, done["refined"], base(ph, "inv") + b)
                        pe.matmul(ps[:, STAT, 0:ph.nq], ones[:, :], acc[:, 0:ph.nq], start=True, stop=True)\
                          .then_inc(done["stat"], 1)

        def pool_attention(pool, ph):
            for b in range(ph.blocks):
                pool.wait_ge(done["yhi"], base(ph, "yhi") + b + 1)
                pool.tensor_tensor(ylo[:, b, 0:ph.nq], acc[:, 0:ph.nq], yhi[:, b, 0:ph.nq].bitcast(F32),
                                   ALU.subtract).then_inc(done["ylo"], 1)

        @block.sync
        def _(sp):
            sp.dma_start(x[:, :, :], io["x"]).then_inc(x_loaded, 16)
            sp.dma_start(cvec[:, :, :], io["cvec"]).then_inc(c_loaded, 16)

            def ada_loads(fill):
                for l, m in fill:
                    number = ada_number[(l, m)]

                    def body(i):
                        for j in range(ADA_RING):
                            b = Idx(number * KC + j, ADA_RING, i)
                            wait(sp, ada_used, b.val(1 - ADA_RING))
                            index = i * ADA_RING + (m * KC + j)
                            src = io["ada_w"][l]
                            src = src[index] if isinstance(index, int) else \
                                src[bass.ds(index, 1)].rearrange("o p n -> (o p) n")
                            sp.dma_start(ada[:, b.ring(ADA_RING), :], src)\
                                .then_inc(ada_loaded[b.ring(ADA_RING)], 16)

                    if number == 0:
                        for i in range(KC // ADA_RING):
                            body(i)
                    else:
                        with sp.Fori(0, KC // ADA_RING) as i:
                            body(i)

            def group_loads(ph, i):
                for j in range(ph.groups):
                    g = Idx(ph.g + j, ph.groups, i)
                    wait(sp, lo_ready, g.val(1 - RAW))
                    src, n = source(ph, i, j)
                    sp.dma_start(raw[:, g.ring(RAW), 0:n], src).then_inc(raw_loaded[g.ring(RAW)], 16)

            ahead = False
            for ph, following in zip(plan, plan[1:] + [None]):
                if ph.kind == "norm":
                    ahead = following is not None
                    if ahead:
                        assert following.groups == RAW
                        group_loads(following, 0)
                    ada_loads(ph.fill1)
                    ada_loads(ph.fill2)
                if ph.iters:
                    run(sp, ph, lambda i, ph=ph: group_loads(ph, i), begin=1 if ahead else 0)
                    ahead = False
            sp.wait_ge(done["x"], base(plan[-1], "x") + KC)
            sp.dma_start(out, x[:, :, 0:S]).then_inc(stored, 16)
            sp.wait_ge(stored, 16)

        @block.gpsimd
        def _(pool):
            small = [(ada_b, "ada_b"), (norm_g, "norm_g"), (cos, "cos"), (sin, "sin"), (ident, "ident"),
                     (mask, "mask"), (subg, "subg"), (lat_g, "lat_g"), (dlam, "dlam")]
            for dst, name in small:
                pool.dma_start(dst[tuple([slice(None)] * len(dst.shape))], io[name]).then_inc(consts_loaded, 16)
            pool.dma_start(sink[:, :, :].rearrange("p l n -> p (l n)"),
                           io["sink"].to_broadcast([P, LAYERS * 16])).then_inc(consts_loaded, 16)

            def add_square(n, number, tokens):
                pool.wait_ge(done["sq"], n.val(1))
                wait(pool, done["acc"], n.val())
                pool.tensor_tensor(acc[:, 0:tokens], acc[:, 0:tokens], tmp[:, number, 0:tokens], ALU.add)\
                    .then_inc(done["acc"], 1)

            zeros = 0
            ropes = 0
            for ph in plan:
                if ph.kind == "norm" and ph.pre:
                    wait(pool, done["stat"], base(ph, "stat") + (1 if ph.post else 0))
                    pool.memset(acc[:, :], 0.0).then_inc(acc_zero, 1)
                    zeros += 1
                    pool.wait_ge(acc_zero, zeros)
                    for c in range(KC):
                        add_square(Idx(base(ph, "sq") + c, 0, 0), c % 2, ph.tokens)
                if ph.kind == "y":
                    pool.wait_ge(done["stat"], base(ph, "stat"))
                    if "ylo" in ph.at:
                        pool.wait_ge(done["ylo"], base(ph, "ylo"))
                    pool.memset(acc[:, :], 0.0).then_inc(acc_zero, 1)
                    zeros += 1
                    pool.wait_ge(acc_zero, zeros)

                    def body(i, ph=ph):
                        for j in range(ph.tiles):
                            add_square(Idx(base(ph, "sq") + j, ph.tiles, i), j % 2, ph.tokens)

                    run(pool, ph, body)
                if ph.kind == "attn" and ph.mode == "a":
                    pool_attention(pool, ph)
                if ph.kind == "rope":
                    def body(i, ph=ph):
                        for j in range(ph.tiles):
                            n = Idx(ph.n + j, ph.tiles, i)
                            r = Idx(base(ph, "rope") + j, ph.tiles, i)
                            pool.wait_ge(bank_free[n.ring(BANKS)], n.lap(BANKS, 1))
                            wait(pool, done["rope"], r.val(-1))
                            pool.tensor_tensor(acc[:, r.ring(2) * S:(r.ring(2) + 1) * S],
                                               tmp[:, r.ring(2), 0:S], cos[:, :], ALU.mult).then_inc(rope_mul, 1)

                    if base(ph, "rope") == 0:
                        pool.wait_ge(consts_loaded, 160)
                    run(pool, ph, body)

        @block.scalar
        def _(act):
            steps = 0
            table = [None]

            def use_table(name):
                if table[0] != name:
                    act.preload_act_table_set(name)
                    table[0] = name

            def split_hi(g):
                if isinstance(g.i, int) and g.val() >= all_groups:
                    return
                act.wait_ge(raw_loaded[g.ring(RAW)], g.lap(RAW, 1) * 16)
                wait(act, group_used, g.val(1 - SPLIT))
                act.activation(whi[:, g.ring(SPLIT), :], raw[:, g.ring(RAW), :], ACT.Copy).then_inc(hi_ready, 1)

            def inverse(dst, bank, tokens, width, stat):
                nonlocal steps
                act.wait_ge(done["stat"], stat)
                act.activation(dst, ps[:, bank, 0:tokens], ACT.Ln, bias=eps[:, 0:1], scale=1.0 / width)\
                   .then_inc(act_step, 1)
                steps += 1
                act.wait_ge(act_step, steps)
                act.activation(dst, dst, ACT.Exp, scale=-0.5).then_inc(done["inv"], 1)

            def square(src, number, tokens, n):
                wait(act, done["acc"], n.val(-1))
                act.activation(tmp[:, number, 0:tokens], src, ACT.Square).then_inc(done["sq"], 1)

            use_table(SILU)
            act.wait_ge(c_loaded, 16)
            act.activation(cvec[:, :, :], cvec[:, :, :], ACT.Silu).then_inc(silu_c, 1)
            use_table(LN_EXP)
            act.wait_ge(consts_made, 1)
            act.wait_ge(lam_sum, 1)
            act.activation(elam[:, :, :], ps[:, STAT, 0:2 * LAYERS].rearrange("p (l n) -> p l n", n=2), ACT.Exp)\
               .then_inc(lam_exp, 1)
            split_hi(Idx(0, 0, 0))

            for ph in plan:
                tk = ph.tokens
                if ph.kind == "norm":
                    if ph.post:
                        inverse(inv[:, 0:tk], STAT, tk, D, base(ph, "stat") + 1)
                    if ph.pre:
                        for c in range(KC):
                            if ph.post:
                                act.wait_ge(done["x"], base(ph, "x") + c + 1)
                            elif c == 0:
                                act.wait_ge(x_loaded, 16)
                            square(x[:, c, 0:tk], c % 2, tk, Idx(base(ph, "sq") + c, 0, 0))
                        inverse(inv[:, 0:tk], STAT, tk, D, base(ph, "stat") + (2 if ph.post else 1))
                        l, sub = ph.pre
                        for c in range(KC):
                            act.wait_ge(done["scaled"], base(ph, "scaled") + c + 1)
                            for s in streams(tk):
                                last = act.activation(xhi[:, c, sl(s)], work[:, c, sl(s)], ACT.Identity,
                                                      bias=mods[:, l, 3 * sub, c, s:s + 1])
                            last.then_inc(done["xhi"], 1)
                elif ph.kind == "ffn_in":
                    use_table(SILU)

                    def body(i, ph=ph, tk=tk):
                        for j in range(2):
                            g = Idx(ph.g + 2 * j, ph.groups, i)
                            n = Idx(ph.n + 2 * j, ph.tiles, i)
                            p = Idx(base(ph, "ghi") + j, 2, i)
                            split_hi(g.plus(1))
                            split_hi(g.plus(2))
                            a, b = n, n.plus(1)
                            act.wait_ge(group_used, last_group(ph, i, 2 * j).val(1))
                            act.activation(tmp[:, 0, 0:tk], ps[:, a.ring(BANKS), 0:tk], ACT.Silu)\
                               .then_inc(bank_free[a.ring(BANKS)], 1)
                            act.wait_ge(bank_free[b.ring(BANKS)], b.lap(BANKS, 1))
                            act.activation(chunk(ghi, Idx(j, 2, i), tk), tmp[:, 1, 0:tk], ACT.Copy)\
                               .then_inc(done["ghi"], 1)

                    run(act, ph, body)
                elif ph.kind == "y":
                    use_table(LN_EXP)
                    if ph.src == "ffn_out":
                        act.wait_ge(done["glo"], base(ph, "glo"))

                    def body(i, ph=ph, tk=tk):
                        for j in range(ph.tiles):
                            g = Idx(ph.g + ph.per_tile * j, ph.groups, i)
                            n = Idx(ph.n + j, ph.tiles, i)
                            for t in range(ph.per_tile):
                                split_hi(g.plus(1 + t))
                            act.wait_ge(group_used, last_group(ph, i, j).val(1))
                            square(ps[:, n.ring(BANKS), 0:tk], j % 2, tk,
                                   Idx(base(ph, "sq") + j, ph.tiles, i))
                            act.activation(chunk(work, Idx(j, ph.tiles, i), tk), ps[:, n.ring(BANKS), 0:tk],
                                           ACT.Copy).then_inc(bank_free[n.ring(BANKS)], 1)

                    run(act, ph, body)
                elif ph.kind == "rope":
                    for b in range(BANKS):
                        act.wait_ge(bank_free[b], tiles_before(ph, b))
                    wait(act, done["m"], base(ph, "m"))

                    def body(i, ph=ph, tk=tk):
                        for j in range(ph.tiles):
                            split_ahead(split_hi, ph, i, j)
                            n = Idx(ph.n + j, ph.tiles, i)
                            r = Idx(base(ph, "rope") + j, ph.tiles, i)
                            act.wait_ge(group_used, last_group(ph, i, j).val(1))
                            wait(act, done["rope"], r.val(-1))
                            last = act.activation(tmp[:, r.ring(2), 0:S], ps[:, n.ring(BANKS), 0:S], ACT.Copy)
                            if tk == T:
                                last = act.activation(rope_dst(ph, i, j, slice(S, T)),
                                                      ps[:, n.ring(BANKS), S:T], ACT.Copy)
                            last.then_inc(bank_free[n.ring(BANKS)], 1)

                    run(act, ph, body)
                elif ph.kind == "plain":
                    i = 0
                    for j in range(ph.tiles):
                        split_ahead(split_hi, ph, i, j)
                        n = bank(ph, i, j)
                        act.wait_ge(group_used, last_group(ph, i, j).val(1))
                        dst = {"lat": lat, "qn": q, "kn": k}[ph.dst]
                        act.activation(dst[:, j, 0:tk], ps[:, n.ring(BANKS), 0:tk], ACT.Copy)\
                           .then_inc(bank_free[n.ring(BANKS)], 1)
                elif ph.kind == "v":
                    def body(i, ph=ph):
                        for j in range(ph.groups):
                            split_hi(Idx(ph.g + j + 1, ph.groups, i))
                        for t in range(ph.tiles):
                            n = bank(ph, i, t)
                            act.wait_ge(group_used, last_group(ph, i, t).val(1))
                            col = i * ph.cols
                            dst = v[:, t, col:col + ph.cols] if isinstance(i, int) else \
                                v[:, t, bass.ds(col, ph.cols)]
                            act.activation(dst, ps[:, n.ring(BANKS), 0:ph.cols], ACT.Copy)\
                               .then_inc(bank_free[n.ring(BANKS)], 1)

                    run(act, ph, body)
                elif ph.kind == "merge":
                    use_table(SIGMOID)

                    def body(i, ph=ph, tk=tk):
                        for j in range(2):
                            g = Idx(ph.g + 2 * j, ph.groups, i)
                            gate = Idx(ph.n + 2 * j, ph.tiles, i)
                            split_hi(g.plus(1))
                            split_hi(g.plus(2))
                            act.wait_ge(group_used, last_group(ph, i, 2 * j).val(1))
                            before = gate.plus(-1)
                            if j or not (isinstance(i, int) and i == 0):
                                act.wait_ge(bank_free[before.ring(BANKS)], before.lap(BANKS, 1))
                            act.activation(tmp[:, 0, 0:tk], ps[:, gate.ring(BANKS), 0:tk], ACT.Sigmoid)\
                               .then_inc(bank_free[gate.ring(BANKS)], 1)

                    run(act, ph, body)
                elif ph.kind == "msplit":
                    for c in range(KC):
                        act.wait_ge(done["m"], base(ph, "m") - KC + c + 1)
                        if c == 0:
                            act.wait_ge(group_used, ph.g)
                        act.activation(yhi[:, c, 0:tk], work[:, c, 0:tk], ACT.Copy).then_inc(done["mhi"], 1)
                elif ph.kind == "latnorm":
                    use_table(LN_EXP)
                    for c in range(QC + KVC):
                        if c == 0:
                            act.wait_ge(done["rope"], base(ph, "rope"))
                        if c >= 2:
                            act.wait_ge(done["stat"], base(ph, "stat") + c - 1)
                        act.activation(tmp[:, c % 2, :], lat[:, c, :], ACT.Square).then_inc(done["lsq"], 1)
                    inverse(inv[:, :], 4, T, Q_RANK, base(ph, "stat") + QC)
                    inverse(acc[:, :], 5, T, KV_RANK, base(ph, "stat") + QC + KVC)
                    for c in range(QC + KVC):
                        act.wait_ge(done["lt"], base(ph, "lt") + c + 1)
                        act.activation(lhi[:, c, :], lat[:, c, :], ACT.Copy).then_inc(done["lhi"], 1)
                elif ph.kind == "attn":
                    use_table(LN_EXP)
                    act_attention(act, ph, inverse)

        @block.vector
        def _(dve):
            steps = 0

            def split_lo(g):
                if isinstance(g.i, int) and g.val() >= all_groups:
                    return
                dve.wait_ge(hi_ready, g.val(1))
                dve.tensor_tensor(wlo[:, g.ring(SPLIT), :], raw[:, g.ring(RAW), :],
                                  whi[:, g.ring(SPLIT), :].bitcast(F32), ALU.subtract).then_inc(lo_ready, 1)

            def step(ins):
                nonlocal steps
                ins.then_inc(dve_step, 1)
                steps += 1
                dve.wait_ge(dve_step, steps)

            def ada_evacuate(fill):
                for l, m in fill:
                    number = ada_number[(l, m)]
                    dst = mods[:, l, m, :, :]
                    dve.wait_ge(ada_used, KC * (number + 1))
                    src = ps[:, ADA_BANK + number % 2, 0:2 * KC].rearrange("p (c n) -> p c n", n=2)
                    add = dve.tensor_tensor(dst, src, ada_b[:, l, m, :, :], ALU.add)
                    sub, part = divmod(m, 3)
                    if part == 0:
                        add.then_inc(ada_evac, 1)
                        continue
                    step(add)
                    g = norm_g[:, l, 2 * sub + part - 1, :, :]
                    factor, op = (1.0, ALU.add) if part == 1 else (1.0 if sub == 1 else 0.5, ALU.mult)
                    dve.scalar_tensor_tensor(dst, dst, factor, g, op, ALU.mult).then_inc(ada_evac, 1)

            dve.memset(ones[:, :], 1.0).then_inc(consts_made, 1)
            dve.memset(eps[:, :], EPS).then_inc(consts_made, 1)
            dve.wait_ge(consts_loaded, 160)
            for l in range(LAYERS):
                for n in range(2):
                    dve.tensor_tensor(dprod[:, l, n:n + 1], dlam[:, l, 2 * n:2 * n + 1],
                                      dlam[:, l, 2 * n + 1:2 * n + 2], ALU.mult).then_inc(consts_made, 1)
            for l in range(LAYERS):
                step(dve.tensor_scalar(subg[:, l:l + 1], subg[:, l:l + 1], 1.0 - lambda_init[l], None, ALU.mult))
            step(dve.tensor_scalar(nsink[:, :, :], sink[:, :, :], -1.0, None, ALU.mult))
            dve.wait_ge(lam_exp, 1)
            for l in range(LAYERS):
                step(dve.scalar_tensor_tensor(lam[:, l:l + 1], elam[:, l, 0:1], lambda_init[l], elam[:, l, 1:2],
                                              ALU.add, ALU.subtract))
            split_lo(Idx(0, 0, 0))

            for ph in plan:
                tk = ph.tokens
                if ph.kind == "norm":
                    if ph.post:
                        l, sub = ph.post
                        dve.wait_ge(done["inv"], base(ph, "inv") + 1)
                        refine(dve, step, inv[:, 0:tk], STAT, tk, D, (tmp[:, 0, :], tmp[:, 1, :]))
                        dve.wait_ge(ada_evac, ada_number[(l, 3 * sub + 2)] + 1)

                        def gated(c):
                            for s in streams(tk):
                                last = dve.scalar_tensor_tensor(
                                    work[:, c, sl(s)], work[:, c, sl(s)], mods[:, l, 3 * sub + 2, c, s:s + 1],
                                    inv[:, sl(s)], ALU.mult, ALU.mult)
                            last.then_inc(dve_step, 1)

                        gated(0)
                        for c in range(KC):
                            if c + 1 < KC:
                                gated(c + 1)
                            dve.wait_ge(dve_step, steps + c + 1)
                            dve.tensor_tensor(x[:, c, 0:tk], x[:, c, 0:tk], work[:, c, 0:tk], ALU.add)\
                               .then_inc(done["x"], 1)
                        steps += KC
                    ada_evacuate(ph.fill1)
                    if ph.pre:
                        l, sub = ph.pre
                        dve.wait_ge(done["inv"], base(ph, "inv") + (2 if ph.post else 1))
                        refine(dve, step, inv[:, 0:tk], STAT, tk, D, (tmp[:, 0, :], tmp[:, 1, :]))
                        dve.wait_ge(ada_evac, ada_number[(l, 3 * sub + 1)] + 1)

                        def scaled(c):
                            for s in streams(tk):
                                last = dve.scalar_tensor_tensor(
                                    work[:, c, sl(s)], x[:, c, sl(s)], mods[:, l, 3 * sub + 1, c, s:s + 1],
                                    inv[:, sl(s)], ALU.mult, ALU.mult)
                            last.then_inc(done["scaled"], 1)

                        scaled(0)
                        for c in range(KC):
                            if c + 1 < KC:
                                scaled(c + 1)
                            dve.wait_ge(done["xhi"], base(ph, "xhi") + c + 1)
                            for s in streams(tk):
                                last = dve.scalar_tensor_tensor(
                                    xlo[:, c, sl(s)], work[:, c, sl(s)], mods[:, l, 3 * sub, c, s:s + 1],
                                    xhi[:, c, sl(s)].bitcast(F32), ALU.add, ALU.subtract)
                            last.then_inc(done["xlo"], 1)
                    ada_evacuate(ph.fill2)
                elif ph.kind == "ffn_in":
                    def body(i, ph=ph, tk=tk):
                        for j in range(2):
                            g = Idx(ph.g + 2 * j, ph.groups, i)
                            a, b = bank(ph, i, 2 * j), bank(ph, i, 2 * j + 1)
                            p = Idx(base(ph, "ghi") + j, 2, i)
                            split_lo(g.plus(1))
                            split_lo(g.plus(2))
                            dve.wait_ge(bank_free[a.ring(BANKS)], a.lap(BANKS, 1))
                            dve.wait_ge(group_used, last_group(ph, i, 2 * j + 1).val(1))
                            dve.tensor_tensor(tmp[:, 1, 0:tk], tmp[:, 0, 0:tk], ps[:, b.ring(BANKS), 0:tk],
                                              ALU.mult).then_inc(bank_free[b.ring(BANKS)], 1)
                            dve.wait_ge(done["ghi"], p.val(1))
                            c = Idx(j, 2, i)
                            dve.tensor_tensor(chunk(glo, c, tk), tmp[:, 1, 0:tk], chunk(ghi, c, tk).bitcast(F32),
                                              ALU.subtract).then_inc(done["glo"], 1)

                    run(dve, ph, body)
                elif ph.kind == "y":
                    def body(i, ph=ph):
                        for j in range(ph.groups):
                            split_lo(Idx(ph.g + j + 1, ph.groups, i))

                    run(dve, ph, body)
                elif ph.kind == "rope":
                    start = steps

                    def body(i, ph=ph, start=start):
                        for j in range(ph.tiles):
                            split_ahead(split_lo, ph, i, j)
                            n = bank(ph, i, j)
                            r = Idx(base(ph, "rope") + j, ph.tiles, i)
                            st = Idx(start + 2 * j, 2 * ph.tiles, i)
                            a = tmp[:, r.ring(2), 0:S]
                            b = tmp[:, r.ring(2), S:T]
                            dve.wait_ge(bank_free[n.ring(BANKS)], n.lap(BANKS, 1))
                            dve.stream_shuffle(b, a, [(m + 16) % 32 for m in range(32)]).then_inc(dve_step, 1)
                            dve.wait_ge(dve_step, st.val(1))
                            dve.tensor_tensor(b, b, sin[:, :], ALU.mult).then_inc(dve_step, 1)
                            dve.wait_ge(dve_step, st.val(2))
                            dve.wait_ge(rope_mul, r.val(1))
                            dve.tensor_tensor(rope_dst(ph, i, j, slice(0, S)),
                                              acc[:, r.ring(2) * S:(r.ring(2) + 1) * S], b, ALU.add)\
                               .then_inc(done["rope"], 1)

                    for i in range(ph.iters):
                        body(i)
                    steps += 2 * ph.tiles * ph.iters
                elif ph.kind == "plain":
                    for j in range(ph.tiles):
                        split_ahead(split_lo, ph, 0, j)
                elif ph.kind == "v":
                    def body(i, ph=ph):
                        for j in range(ph.groups):
                            split_lo(Idx(ph.g + j + 1, ph.groups, i))

                    run(dve, ph, body)
                elif ph.kind == "merge":
                    def body(i, ph=ph, tk=tk):
                        for j in range(2):
                            g = Idx(ph.g + 2 * j, ph.groups, i)
                            a, b = bank(ph, i, 2 * j), bank(ph, i, 2 * j + 1)
                            split_lo(g.plus(1))
                            split_lo(g.plus(2))
                            dve.wait_ge(bank_free[a.ring(BANKS)], a.lap(BANKS, 1))
                            dve.wait_ge(group_used, last_group(ph, i, 2 * j + 1).val(1))
                            c = Idx(j, 2, i)
                            dst = chunk(work, c, tk) if ph.r == 0 else tmp[:, 1, 0:tk]
                            dve.tensor_tensor(dst, tmp[:, 0, 0:tk], ps[:, b.ring(BANKS), 0:tk], ALU.mult)\
                               .then_inc(bank_free[b.ring(BANKS)], 1)
                            if ph.r:
                                dve.wait_ge(bank_free[b.ring(BANKS)], b.lap(BANKS, 1))
                                dve.tensor_tensor(chunk(work, c, tk), chunk(work, c, tk), tmp[:, 1, 0:tk], ALU.add)\
                                   .then_inc(done["m"], 1)

                    run(dve, ph, body)
                elif ph.kind == "msplit":
                    for c in range(KC):
                        dve.wait_ge(done["mhi"], base(ph, "mhi") + c + 1)
                        dve.tensor_tensor(ylo[:, c, 0:tk], work[:, c, 0:tk], yhi[:, c, 0:tk].bitcast(F32),
                                          ALU.subtract).then_inc(done["mlo"], 1)
                elif ph.kind == "latnorm":
                    dve.wait_ge(done["inv"], base(ph, "inv") + 2)
                    refine(dve, step, inv[:, :], 4, T, Q_RANK, (tmp[:, 0, :], tmp[:, 1, :]))
                    refine(dve, step, acc[:, :], 5, T, KV_RANK, (tmp[:, 0, :], tmp[:, 1, :]))

                    def normed(c):
                        dve.scalar_tensor_tensor(lat[:, c, :], lat[:, c, :], lat_g[:, ph.layer, c:c + 1],
                                                 (inv if c < QC else acc)[:, :], ALU.mult, ALU.mult)\
                           .then_inc(done["lt"], 1)

                    normed(0)
                    for c in range(QC + KVC):
                        if c + 1 < QC + KVC:
                            normed(c + 1)
                        dve.wait_ge(done["lhi"], base(ph, "lhi") + c + 1)
                        dve.tensor_tensor(llo[:, c, :], lat[:, c, :], lhi[:, c, :].bitcast(F32), ALU.subtract)\
                           .then_inc(done["llo"], 1)
                elif ph.kind == "attn":
                    dve_attention(dve, ph, step)

        @block.tensor
        def _(pe):
            def ada_products(fill, ph):
                for l, m in fill:
                    number = ada_number[(l, m)]
                    wait(pe, ada_evac, number - 1)
                    pe.wait_ge(silu_c, 1)
                    for name in ("yhi", "ylo", "ynorm"):
                        wait(pe, done[name], base(ph, name))

                    def body(i):
                        for j in range(ADA_RING):
                            b = Idx(number * KC + j, ADA_RING, i)
                            pe.wait_ge(ada_loaded[b.ring(ADA_RING)], b.lap(ADA_RING, 1) * 16)
                            col = (i * ADA_RING + j) * 2
                            out = ps[:, ADA_BANK + number % 2, col:col + 2] if isinstance(col, int) else \
                                ps[:, ADA_BANK + number % 2, bass.ds(col, 2)]
                            for c in range(KC):
                                last = pe.matmul(out, ada[:, b.ring(ADA_RING), c * P:(c + 1) * P], cvec[:, c, :],
                                                 start=c == 0, stop=c == KC - 1)
                            last.then_inc(ada_used, 1)

                    with pe.Fori(0, KC // ADA_RING) as i:
                        body(i)

            def stat(ph, before):
                wait(pe, done["refined"], base(ph, "inv") + before)
                wait(pe, done["pt"], base(ph, "pt"))
                pe.matmul(ps[:, STAT, 0:ph.tokens], ones[:, :], acc[:, 0:ph.tokens], start=True, stop=True)\
                  .then_inc(done["stat"], 1)

            def group_pieces(ph, j):
                if ph.src == "ffn_out":
                    tile, part = divmod(j, 3)
                    n = KC if part < 2 else FC - 2 * KC
                    return [(tile, KC * part + c, c * P, part == 0 and c == 0, part == 2 and c == n - 1)
                            for c in range(n)]
                per, depth = ph.tiles // ph.groups, {"uq": QC, "uk": KVC}.get(ph.src, KC)
                return [(per * j + t, c, (t * depth + c) * P, c == 0, c == depth - 1)
                        for t in range(per) for c in range(depth)]

            def moving(ph, tile):
                tk, j = ph.tokens, tile
                if ph.kind == "merge" and j % 2:
                    return yhi, ylo, 0, "ylo", None
                if ph.src == "ffn_out":
                    return ghi, glo, 0, "glo", FC
                if ph.src == "wo":
                    return yhi, ylo, 0, "mlo", KC
                if ph.src == "uq":
                    return lhi, llo, 0, "llo", QC + KVC
                if ph.src == "uk":
                    return lhi, llo, QC, "llo", QC + KVC
                return xhi, xlo, 0, "xlo", KC

            def group_products(ph, i, j):
                g = Idx(ph.g + j, ph.groups, i)
                s = g.ring(SPLIT)
                pieces = group_pieces(ph, j)
                tk = ph.tokens
                for tile, c, col, start, stop in pieces:
                    hi, lo, first, ready, chunks = moving(ph, tile)
                    n = bank(ph, i, tile)
                    if start:
                        wait(pe, bank_free[n.ring(BANKS)], n.lap(BANKS))
                    if tile == 0 or (ph.kind == "merge" and tile == 1 and c == 0):
                        pe.wait_ge(done[ready], base(ph, ready) if chunks is None else
                                   base(ph, ready) - chunks + first + c + 1)
                    if (tile, c) == pieces[0][:2]:
                        pe.wait_ge(hi_ready, g.val(1))
                    o = ps[:, n.ring(BANKS), 0:tk]
                    w = whi[:, s, col:col + P]
                    pe.matmul(o, w, hi[:, first + c, 0:tk], start=start, stop=False)
                    pe.matmul(o, w, lo[:, first + c, 0:tk], start=False, stop=False)
                pe.wait_ge(lo_ready, g.val(1))
                for tile, c, col, start, stop in pieces:
                    hi, lo, first, _, _ = moving(ph, tile)
                    n = bank(ph, i, tile)
                    last = pe.matmul(ps[:, n.ring(BANKS), 0:tk], wlo[:, s, col:col + P], hi[:, first + c, 0:tk],
                                     start=False, stop=stop)
                last.then_inc(group_used, 1)

            def token_products(ph, i, j):
                g = Idx(ph.g + j, ph.groups, i)
                s = g.ring(SPLIT)
                hi, lo, first = (lhi, llo, QC) if ph.x == "lat" else (xhi, xlo, 0)
                pe.wait_ge(hi_ready, g.val(1))
                for low in range(2):
                    if low:
                        pe.wait_ge(lo_ready, g.val(1))
                    for t in range(T // P):
                        n = bank(ph, i, t)
                        if j == 0 and not low:
                            wait(pe, bank_free[n.ring(BANKS)], n.lap(BANKS))
                        o = ps[:, n.ring(BANKS), 0:ph.cols]
                        for c in range(ph.kpg):
                            kc = first + j * ph.kpg + c
                            cols = slice(c * ph.cols, (c + 1) * ph.cols)
                            tokens = slice(t * P, (t + 1) * P)
                            if low:
                                last = pe.matmul(o, hi[:, kc, tokens], wlo[:, s, cols], start=False,
                                                 stop=j == ph.groups - 1 and c == ph.kpg - 1)
                            else:
                                pe.matmul(o, hi[:, kc, tokens], whi[:, s, cols], start=j == 0 and c == 0,
                                          stop=False)
                                pe.matmul(o, lo[:, kc, tokens], whi[:, s, cols], start=False, stop=False)
                last.then_inc(group_used, 1)

            pe.wait_ge(consts_made, 2 + 2 * LAYERS)
            pe.matmul(ps[:, STAT, 0:2 * LAYERS], ones[0:64, :], dprod[:, :, :].rearrange("p l n -> p (l n)"),
                      start=True, stop=True).then_inc(lam_sum, 1)
            pe.wait_ge(lam_exp, 1)

            for ph in plan:
                if ph.kind == "norm":
                    if ph.post:
                        pe.wait_ge(done["acc"], base(ph, "acc"))
                        stat(ph, 0)
                    ada_products(ph.fill1, ph)
                    if ph.pre:
                        pe.wait_ge(done["acc"], base(ph, "acc") + KC)
                        stat(ph, 1 if ph.post else 0)
                    ada_products(ph.fill2, ph)
                elif ph.kind == "latnorm":
                    wait(pe, done["pt"], base(ph, "pt"))
                    wait(pe, done["refined"], base(ph, "inv"))
                    for c in range(QC + KVC):
                        pe.wait_ge(done["lsq"], base(ph, "lsq") + c + 1)
                        pe.matmul(ps[:, 4 if c < QC else 5, :], ones[:, :], tmp[:, c % 2, :],
                                  start=c in (0, QC), stop=c in (QC - 1, QC + KVC - 1)).then_inc(done["stat"], 1)
                elif ph.kind == "attn":
                    pe_attention(pe, ph)
                elif ph.iters:
                    wait(pe, done["exp"], base(ph, "exp"))
                    if ph.kind == "v":
                        def body(i, ph=ph):
                            for j in range(ph.groups):
                                token_products(ph, i, j)
                    else:
                        def body(i, ph=ph):
                            for j in range(ph.groups):
                                group_products(ph, i, j)

                    run(pe, ph, body)



def blocked(w):
    *lead, k, m = w.shape
    n = len(lead)
    w = w.reshape(*lead, k // P, P, m // P, P)
    w = w.transpose(*range(n), n + 2, n + 1, n, n + 3)
    return w.reshape(*lead, m // P, P, k)


def by_rows(w, cols, kpg):
    l, k, m = w.shape
    w = w.reshape(l, k // P // kpg, kpg, P, m // cols, cols)
    return w.transpose(0, 4, 1, 3, 2, 5).reshape(l, -1, P, kpg * cols)


def layout(x, c, ctx, c_ctx, ada_w, ada_b, norm_g, ffn_w_in, ffn_w_out, mix_w_in, diff_lambda, diff_subln_g,
           win_sink, mla_q_norm_g, mla_kv_norm_g, mla_w_uq, mla_w_ukv, branch_w, mix_w_out):
    L = LAYERS
    a = {}
    a["x"] = np.concatenate([x[0], ctx[0]], 0).T.reshape(KC, P, T).transpose(1, 0, 2)
    a["cvec"] = np.stack([c[0], c_ctx], -1).reshape(KC, P, 2).transpose(1, 0, 2)
    a["ada_w"] = blocked(ada_w)
    a["ada_b"] = np.repeat(ada_b.reshape(L, N_MOD, KC, P).transpose(3, 0, 1, 2)[..., None], 2, -1)
    a["norm_g"] = np.repeat(norm_g.reshape(L, 6, KC, P).transpose(3, 0, 1, 2)[..., None], 2, -1)
    ab = blocked(ffn_w_in).reshape(L, 2, 2, FC, P, D).transpose(0, 1, 3, 2, 4, 5)
    a["ffn_in"] = ab.reshape(L, 2, 2 * FC, P, D)
    a["ffn_out"] = blocked(ffn_w_out)
    cuts = np.cumsum([D, D, D, D, 256, 256, Q_RANK, KV_RANK, ROPE])
    aq, ak, av, bq, bk, bv, cq, ckv, ckr, gates = np.split(mix_w_in, cuts, axis=-1)
    a["qk_a"] = np.concatenate([blocked(aq), blocked(ak)], 1)
    a["v_a"] = by_rows(av, 512, 2)
    bq = bq.reshape(L, D, 2, 2, 4, 64).transpose(0, 1, 2, 4, 3, 5).reshape(L, D, D)
    a["qk_b"] = np.concatenate([blocked(bq), blocked(bk)], 1)
    a["v_b"] = by_rows(bv, 256, 4)
    a["c_lat"] = np.concatenate([blocked(cq), blocked(ckv), blocked(np.concatenate([ckr, ckr], -1))], 1)
    uq = mla_w_uq.reshape(L, Q_RANK, 8, 192)
    uq = np.concatenate([uq[..., :128].reshape(L, Q_RANK, D), uq[..., 128:].reshape(L, Q_RANK, 512)], -1)
    a["uq"] = blocked(uq).reshape(L, 6, 2, P, Q_RANK).transpose(0, 1, 3, 2, 4).reshape(L, 6, P, 2 * Q_RANK)
    ukv = mla_w_ukv.reshape(L, KV_RANK, 8, 256)
    uk = blocked(ukv[..., :128].reshape(L, KV_RANK, D))
    a["uk"] = uk.reshape(L, 2, 4, P, KV_RANK).transpose(0, 1, 3, 2, 4).reshape(L, 2, P, 4 * KV_RANK)
    a["uv"] = by_rows(ukv[..., 128:].reshape(L, KV_RANK, D), 512, 2)
    bw = branch_w.reshape(L, 3, D, D)
    win = bw[:, 1].reshape(L, 2, 2, 4, 64, D).transpose(0, 1, 3, 2, 4, 5).reshape(L, D, D)
    bw = np.stack([bw[:, 0], win, bw[:, 2]], 1)
    gates = gates.reshape(L, D, 3, D).transpose(0, 2, 1, 3)
    a["merge"] = np.stack([blocked(gates), blocked(bw)], 3).reshape(L, 3, 2 * KC, P, D)
    a["wo"] = blocked(mix_w_out)
    a["subg"] = diff_subln_g.T
    lat_g = np.concatenate([mla_q_norm_g, mla_kv_norm_g], -1)
    a["lat_g"] = lat_g.reshape(L, QC + KVC, P).transpose(2, 0, 1)
    a["dlam"] = diff_lambda.transpose(2, 0, 1)
    a["sink"] = win_sink.reshape(L, 2, 2, 4).transpose(0, 1, 3, 2).reshape(1, L * 16)

    token = np.arange(S)
    quarter = ROPE // 4
    freq = (1.0 / (np.float32(10000.0) ** (np.arange(quarter, dtype=np.float32) / np.float32(quarter))))
    freq = freq.astype(np.float32)
    row, col = (token // GRID_W).astype(np.float32), (token % GRID_W).astype(np.float32)
    angles = np.concatenate([freq[:, None] * row] * 2 + [freq[:, None] * col] * 2, 0).astype(np.float32)
    sign = np.where(np.arange(ROPE) // quarter % 2 == 0, -1.0, 1.0)[:, None].astype(np.float32)
    a["cos"] = np.concatenate([np.cos(angles)] * 2, 0).astype(np.float32)
    a["sin"] = np.concatenate([np.sin(angles) * sign] * 2, 0).astype(np.float32)
    a["ident"] = np.eye(P, dtype=np.float32)
    i = np.arange(P)
    later, earlier = i[None, :] > i[:, None], i[None, :] < i[:, None]
    a["mask"] = np.where(np.stack([later, earlier], 1), np.float32(NEG), np.float32(0.0)).astype(np.float32)
    return {name: np.ascontiguousarray(t) for name, t in a.items()}


def kernel(**inputs):
    import concourse.bacc as bacc
    from concourse.bass_utils import run_bass_kernel_spmd

    arrays = layout(**{name: np.asarray(t) for name, t in inputs.items()})
    nc = bacc.Bacc("TRN2", target_bir_lowering=False, num_devices=1)
    io = {name: nc.dram_tensor(f"in_{name}", t.shape, F32, kind="ExternalInput").ap()
          for name, t in arrays.items()}
    out = nc.dram_tensor("out", (P, KC, S), F32, kind="ExternalOutput").ap()
    build(nc, io, out)
    r = run_bass_kernel_spmd(nc, [{f"in_{name}": t for name, t in arrays.items()}], core_ids=[0])
    y = r.results[0]["out"]
    return y.transpose(2, 1, 0).reshape(1, S, D)
```

```python
from contextlib import ExitStack

import numpy as np

import concourse.bass as bass
from concourse import mybir

F32 = mybir.dt.float32
F32R = mybir.dt.float32r
ALU = mybir.AluOpType
ACT = mybir.ActivationFunctionType
AX_X = mybir.AxisListType.X

P = 128
D = 1024
KC = D // P
S = 256
T = 512
LAYERS = 2
FFN = 2816
FC = FFN // P
N_MOD = 9
GRID_W = 64
ROPE = 64
EPS = 1e-6
NEG = -1e30
WINDOW = 128
Q_RANK, KV_RANK = 384, 256
QC, KVC = Q_RANK // P, KV_RANK // P
HEAD_SCALE = 64 ** -0.5
MLA_SCALE = (128 + 64) ** -0.5
LN_EXP = "natural_log_exp_and_others"
SILU = "silu_and_others"
SIGMOID = "sigmoid_and_others"

RAW = 4
SPLIT = 2
BANKS = 4
STAT, ADA_BANK = 5, 6
GROUP = 1024
FIRST_ADA = 2
ADA_PAIR = 2
ADA_RING = 2


class Idx:

    def __init__(self, c, step, i):
        self.c, self.step, self.i = c, step, i

    def plus(self, k):
        return Idx(self.c + k, self.step, self.i)

    def val(self, extra=0):
        if isinstance(self.i, int):
            return self.c + self.i * self.step + extra
        return self.i * self.step + (self.c + extra)

    def ring(self, size):
        if isinstance(self.i, int):
            return (self.c + self.i * self.step) % size
        assert self.step % size == 0
        return self.c % size

    def lap(self, size, extra=0):
        if isinstance(self.i, int):
            return (self.c + self.i * self.step) // size + extra
        assert self.step % size == 0
        return self.i * (self.step // size) + (self.c // size + extra)


def wait(eng, sem, value):
    if isinstance(value, int) and value <= 0:
        return
    eng.wait_ge(sem, value)


class Phase:

    def __init__(self, kind, layer, src=None, tokens=None, first=0, iters=0, groups=0, tiles=0, adds=None,
                 sub=None, post=None, pre=None, vectors=(), per_tile=1, dst=None, cols=0, x=None,
                 kpg=0, mode=None, blocks=0, nq=0, r=0):
        self.kind, self.layer, self.src, self.tokens, self.first = kind, layer, src, tokens, first
        self.iters, self.groups, self.tiles, self.adds = iters, groups, tiles, dict(adds or {})
        self.sub, self.post, self.pre, self.vectors = sub, post, pre, vectors
        self.per_tile, self.dst, self.cols, self.x, self.kpg = per_tile, dst, cols, x, kpg
        self.mode, self.blocks, self.nq, self.r = mode, blocks, nq, r
        self.peel_first = self.peel_last = False


def make_plan():
    plan = []

    def add(kind, layer, **kw):
        plan.append(Phase(kind, layer=layer, **kw))

    def norm(layer, post, pre, tokens):
        adds = {"stat": bool(post) + bool(pre), "inv": bool(post) + bool(pre)}
        if post:
            adds["x"] = KC
        if pre:
            adds.update(sq=KC, acc=KC, scaled=KC, xhi=KC, xlo=KC)
        add("norm", layer, post=post, pre=pre, tokens=tokens, adds=adds)

    norm(0, None, (0, 0), T)
    vectors = {
        (0, 0): [(0, 2), (0, 3), (0, 4), (0, 5), (0, 6), (0, 7)],
        (0, 2): [(0, 8), (1, 0), (1, 1), (1, 2)],
        (1, 0): [(1, 3), (1, 4), (1, 5), (1, 6), (1, 7)],
        (1, 2): [(1, 8)],
    }
    for layer in range(LAYERS):
        last = layer == LAYERS - 1
        nq = S if last else T

        def ffn(sub, tokens):
            made = vectors[(layer, sub)]
            add("ffn_in", layer, sub=sub, tokens=tokens, iters=FC // 2, groups=4, tiles=4, vectors=made,
                adds={"ghi": FC, "glo": FC, "made": sum(m % 3 > 0 for _, m in made)})
            add("y", layer, src="ffn_out", sub=sub, tokens=tokens, iters=KC // 4, groups=12, tiles=4,
                per_tile=3, adds={"sq": KC, "acc": KC})

        ffn(0, T)
        norm(layer, (layer, 0), (layer, 1), T)
        if last:
            add("rope", layer, src="qk_a", dst="q", first=0, tokens=nq, iters=2, groups=4, tiles=4,
                adds={"rope": 8})
            add("rope", layer, src="qk_a", dst="k", first=8, tokens=T, iters=2, groups=4, tiles=4,
                adds={"rope": 8})
        else:
            add("rope", layer, src="qk_a", dst="qk", first=0, tokens=T, iters=4, groups=4, tiles=4,
                adds={"rope": 16})
        add("v", layer, src="v_a", cols=512, x="x", kpg=2, iters=2, groups=4, tiles=4)
        add("attn", layer, mode="a", blocks=8, nq=nq)
        add("merge", layer, r=0, tokens=nq, iters=4, groups=4, tiles=4)
        add("rope", layer, src="qk_b", dst="q", first=0, tokens=nq, iters=2, groups=4, tiles=4,
            adds={"rope": 8})
        add("rope", layer, src="qk_b", dst="k", first=8, tokens=T, iters=1, groups=2, tiles=2,
            adds={"rope": 2})
        add("v", layer, src="v_b", cols=256, x="x", kpg=4, iters=1, groups=2, tiles=4)
        add("attn", layer, mode="b", blocks=8, nq=nq)
        add("merge", layer, r=1, tokens=nq, iters=4, groups=4, tiles=4, adds={"m": KC})
        add("plain", layer, src="c_lat", dst="lat", tokens=T, iters=1, groups=QC + KVC, tiles=QC + KVC)
        add("rope", layer, src="c_lat", dst="kr", first=QC + KVC, tokens=T, iters=1, groups=1, tiles=1,
            adds={"rope": 1})
        add("latnorm", layer, adds={"lsq": QC + KVC, "stat": QC + KVC, "inv": 2, "lt": QC + KVC,
                                    "lhi": QC + KVC, "llo": QC + KVC})
        add("plain", layer, src="uq", dst="qn", tokens=nq, iters=1, groups=4, tiles=8)
        add("rope", layer, src="uq", dst="qr", first=8, tokens=nq, iters=1, groups=2, tiles=4,
            adds={"rope": 4})
        add("plain", layer, src="uk", dst="kn", tokens=T, iters=1, groups=2, tiles=8)
        add("v", layer, src="uv", cols=512, x="lat", kpg=2, iters=2, groups=1, tiles=4)
        add("attn", layer, mode="c", blocks=4, nq=nq)
        add("merge", layer, r=2, tokens=nq, iters=4, groups=4, tiles=4, adds={"m": KC})
        add("msplit", layer, tokens=nq, adds={"mhi": KC, "mlo": KC})
        add("y", layer, src="wo", sub=1, tokens=nq, iters=2, groups=4, tiles=4, per_tile=1,
            adds={"sq": KC, "acc": KC})
        norm(layer, (layer, 1), (layer, 2), nq)
        ffn(2, nq)
        norm(layer, (layer, 2), None if last else (layer + 1, 0), nq)

    at = {}
    g = n = 0
    for ph in plan:
        ph.g, ph.n, ph.at = g, n, dict(at)
        g += ph.groups * ph.iters
        n += ph.tiles * ph.iters
        if ph.kind == "attn":
            qts = list(range(ph.nq // P))
            ph.units = [(b, qt) for b in range(ph.blocks) for qt in qts]
            ph.per_block = len(qts)
            u = len(ph.units)
            ph.adds = {"score": u, "bias": u, "exp": u, "prob": u, "turned": u, "pt": u, "pv": u,
                       "yhi": ph.blocks, "ylo": ph.blocks}
            if ph.mode == "a":
                ph.adds.update(asq=ph.blocks, stat=ph.blocks, inv=ph.blocks, ynorm=ph.blocks)
        for k, v in ph.adds.items():
            at[k] = at.get(k, 0) + v
    products = [ph for ph in plan if ph.iters]
    products[0].peel_first = True
    next(ph for ph in products if ph.kind == "rope").peel_first = True
    products[-1].peel_last = True
    return plan, g


def build(nc, io, silu_rows, out):
    plan, all_groups = make_plan()
    lambda_init = [0.8 - 0.6 * float(np.exp(-0.3 * l)) for l in range(LAYERS)]

    with ExitStack() as ctx:
        def sb(name, shape, dt=F32):
            return ctx.enter_context(nc.sbuf_tensor(name, shape, dt))

        x = sb("x", [P, KC, T])
        work = sb("work", [P, KC, T])
        xhi = sb("xhi", [P, KC, T], F32R)
        xlo = sb("xlo", [P, KC, T], F32R)
        raw = sb("raw", [P, RAW, GROUP])
        whi = sb("whi", [P, SPLIT, GROUP], F32R)
        wlo = sb("wlo", [P, SPLIT, GROUP], F32R)
        ada = sb("ada", [P, ADA_RING, D])
        cos = sb("cos", [P, S])
        sin = sb("sin", [P, S])
        ident = sb("ident", [P, P])
        mask = sb("mask", [P, 2, P])
        ones = sb("ones", [P, P])
        inv = sb("inv", [P, T])
        tmp = sb("tmp", [P, 2, T])
        acc = sb("acc", [P, T])
        mods = sb("mods", [P, LAYERS, N_MOD, KC, 2])
        ada_b = sb("ada_b", [P, LAYERS, N_MOD, KC, 2])
        norm_g = sb("norm_g", [P, LAYERS, 6, KC, 2])
        cvec = sb("cvec", [P, KC, 2])
        subg = sb("subg", [P, LAYERS])
        lat_g = sb("lat_g", [P, LAYERS, QC + KVC])
        dlam = sb("dlam", [64, LAYERS, 4])
        dprod = sb("dprod", [64, LAYERS, 2])
        elam = sb("elam", [P, LAYERS, 2])
        lam = sb("lam", [P, LAYERS])
        nsink = sb("nsink", [P, LAYERS, 16])
        sink = sb("sink", [P, LAYERS, 16])
        eps = sb("eps", [P, 1])
        mx = sb("mx", [P, 2, 2])
        nb = sb("nb", [P, 2, 2])
        sd = sb("sd", [P, 2, 2])
        se = sb("se", [P, 2, 2])
        sm = sb("sm", [P, 2, 2])
        rc = sb("rc", [P, 2, 2])

        arena_bytes = 2 * FC * T * 4
        arena_at = (nc.sbuf_usable_end - arena_bytes) // 32 * 32
        assert nc.sbuf_base <= arena_at, (nc.sbuf_base, arena_at)

        def at(name, shape, offset, dt=F32):
            assert offset + int(np.prod(shape[1:])) * 4 <= arena_bytes, name
            return nc.alloc_sbuf_tensor_at(name, shape, dt, offset=arena_at + offset)

        KB = 1024
        shift_w = at("shift_w", [P, KC, D], 0)
        scale_w = at("scale_w", [P, KC, D], 32 * KB)
        ghi = at("ghi", [P, FC, T], 0, F32R)
        glo = at("glo", [P, FC, T], FC * T * 4, F32R)
        qk = at("qk", [P, 16, T], 0)
        q = qk[:, 0:8, :]
        k = qk[:, 8:16, :]
        yhi = at("yhi", [P, 8, T], 0, F32R)
        v = at("v", [P, 4, D], 32 * KB)
        ylo = at("ylo", [P, 8, T], 48 * KB, F32R)
        lat = at("lat", [P, QC + KVC, T], 78 * KB)
        lhi = at("lhi", [P, QC + KVC, T], 48 * KB, F32R)
        llo = at("llo", [P, QC + KVC, T], 58 * KB, F32R)
        qr = at("qr", [P, 4, T], 68 * KB)
        kr = at("kr", [P, T], 76 * KB)
        sub_v = at("sub_v", [P, T], 68 * KB)
        prob = at("prob", [P, 2, 2, T], 78 * KB)

        ps = ctx.enter_context(nc.psum_tensor("ps", [P, 8, 512], F32))

        def sem(name):
            return ctx.enter_context(nc.semaphore(name))

        raw_loaded = [sem(f"raw_loaded{s}") for s in range(RAW)]
        shift_w_loaded = [sem(f"shift_w_loaded{s}") for s in range(KC // ADA_PAIR)]
        scale_w_loaded = [sem(f"scale_w_loaded{s}") for s in range(KC // ADA_PAIR)]
        ada_loaded = [sem(f"ada_loaded{s}") for s in range(ADA_RING)]
        x_loaded = sem("x_loaded")
        c_loaded = sem("c_loaded")
        consts_loaded = sem("consts_loaded")
        consts_made = sem("consts_made")
        silu_c = sem("silu_c")
        silu_rows_made = sem("silu_rows_made")
        silu_rows_stored = sem("silu_rows_stored")
        c_all_loaded = sem("c_all_loaded")
        c_spread = sem("c_spread")
        hi_ready = sem("hi_ready")
        lo_ready = sem("lo_ready")
        group_used = sem("group_used")
        bank_free = [sem(f"bank_free{b}") for b in range(BANKS)]
        first_shift = sem("first_shift")
        ada_dot = sem("ada_dot")
        done = {name: sem(f"{name}_done") for name in (
            "ghi", "glo", "sq", "acc", "stat", "inv", "x", "scaled", "xhi", "xlo", "rope", "m", "mhi",
            "mlo", "lsq", "lt", "lhi", "llo", "score", "bias", "exp", "prob", "turned", "pt", "pv",
            "yhi", "ylo", "asq", "ynorm", "refined", "made")}
        rope_mul = sem("rope_mul")
        acc_zero = sem("acc_zero")
        lam_sum = sem("lam_sum")
        lam_exp = sem("lam_exp")
        dve_step = sem("dve_step")
        act_step = sem("act_step")
        stored = sem("stored")

        block = ctx.enter_context(nc.Block())

        def run(eng, ph, body):
            first = 1 if ph.peel_first else 0
            last = 1 if ph.peel_last else 0
            if ph.iters == 1 or ph.groups % RAW:
                for i in range(ph.iters):
                    body(i)
                return
            for i in range(first):
                body(i)
            if ph.iters - first - last > 1:
                with eng.Fori(first, ph.iters - last) as i:
                    body(i)
            else:
                for i in range(first, ph.iters - last):
                    body(i)
            for i in range(ph.iters - last, ph.iters):
                body(i)

        def base(ph, name):
            return ph.at.get(name, 0)

        def streams(tokens):
            return range(tokens // S)

        def sl(s):
            return slice(s * S, (s + 1) * S)

        def source(ph, i, j):
            w = io[ph.src or ph.kind][ph.layer]

            def pick(ap, index):
                if isinstance(index, int):
                    return ap[index]
                return ap[bass.ds(index, 1)].rearrange("o p n -> (o p) n")

            if ph.kind == "ffn_in":
                return pick(w[ph.sub // 2], i * 4 + j), GROUP
            if ph.kind == "merge":
                return pick(w[ph.r], i * 4 + j), GROUP
            if ph.src == "ffn_out":
                tile, part = divmod(j, 3)
                n = GROUP if part < 2 else (FC - 16) * P
                return pick(w[ph.sub // 2], i * 4 + tile)[:, part * GROUP:part * GROUP + n], n
            first = 4 if (ph.src, ph.kind) == ("uq", "rope") else ph.first
            n = w.shape[-1]
            return pick(w, i * ph.groups + (first + j)), n

        def last_group(ph, i, j):
            if ph.kind == "v":
                own = ph.groups - 1
            elif ph.src == "ffn_out":
                own = 3 * j + 2
            else:
                own = j * ph.groups // ph.tiles
            return Idx(ph.g + own, ph.groups, i)

        def bank(ph, i, j):
            return Idx(ph.n + j, ph.tiles, i)

        def tiles_before(ph, b):
            return (ph.n - b + BANKS - 1) // BANKS

        def chunk(t, c, tokens):
            if isinstance(c.i, int):
                return t[:, c.val(), 0:tokens]
            return t[:, bass.ds(c.val(), 1), 0:tokens].rearrange("p o n -> p (o n)")

        def split_ahead(split, ph, i, j):
            per_group = ph.tiles // ph.groups
            if j % per_group == 0:
                split(Idx(ph.g + j // per_group + 1, ph.groups, i))

        def rope_dst(ph, i, j, cols):
            if ph.dst == "kr":
                return kr[:, cols]
            t = {"q": q, "k": k, "qk": qk, "qr": qr}[ph.dst]
            if isinstance(i, int):
                return t[:, i * ph.tiles + j, cols]
            return t[:, bass.ds(i * ph.tiles + j, 1), cols].rearrange("p o n -> p (o n)")

        ada_order = [lm for ph in plan for lm in ph.vectors]
        assert ada_order == [divmod(n, N_MOD) for n in range(FIRST_ADA, LAYERS * N_MOD)]

        c_all = work[:, 0:4, :].rearrange("p c n -> p (c n)")
        products = work[:, 4:8, :].rearrange("p (s c) n -> p s (c n)", s=2)
        mods_flat = mods[:, :, :, :, :].rearrange("p l m c s -> p (l m c s)")
        ada_b_flat = ada_b[:, :, :, :, :].rearrange("p l m c s -> p (l m c s)")

        def scale_or_gate(eng, l, m):
            sub, part = divmod(m, 3)
            g = norm_g[:, l, 2 * sub + part - 1, :, :]
            factor, op = (1.0, ALU.add) if part == 1 else (1.0 if sub == 1 else 0.5, ALU.mult)
            dst = mods[:, l, m, :, :]
            return eng.scalar_tensor_tensor(dst, dst, factor, g, op, ALU.mult)

        def refine(dve, step, dst, bank_, tokens, width, scratch):
            vs, sq = (t[:, 0:tokens] for t in scratch)
            dve.tensor_scalar(vs, ps[:, bank_, 0:tokens], 1.0 / width, EPS, ALU.mult, ALU.add)\
               .then_inc(done["refined"], 1)
            step(dve.tensor_tensor(sq, dst, dst, ALU.mult))
            step(dve.scalar_tensor_tensor(sq, sq, -0.5, vs, ALU.mult, ALU.mult))
            step(dve.scalar_tensor_tensor(dst, sq, 1.5, dst, ALU.add, ALU.mult))

        def last_unit(ph, b):
            return (b + 1) * ph.per_block - 1

        def keys(qt):
            return 0 if qt < S // P else S // P

        def turns(ph):
            return 1 if ph.mode == "a" else 2

        def turned(ph, u, n):
            if ph.mode == "a":
                return tmp[:, u % 2, :]
            return (acc, inv)[n][:, :] if u % 2 else tmp[:, n, :]

        def act_attention(act, ph, inverse):
            units, nq = ph.units, ph.nq
            scale = MLA_SCALE if ph.mode == "c" else HEAD_SCALE

            def exp(u):
                e, nk = u % 2, T - keys(units[u][1]) * P
                act.wait_ge(done["bias"], base(ph, "bias") + u + 1)
                wait(act, done["turned"], base(ph, "turned") + u - 1 if u >= 2 else 0)
                if ph.mode == "b":
                    act.activation(se[:, e, :], sd[:, e, :], ACT.Exp)
                for n in range(2):
                    last = act.activation(prob[:, e, n, 0:nk], ps[:, 2 * e + n, 0:nk], ACT.Exp,
                                          bias=nb[:, e, n:n + 1], scale=scale, accum_out=sm[:, e, n:n + 1])
                last.then_inc(done["exp"], 1)

            def turned_copy(u):
                nk = T - keys(units[u][1]) * P
                act.wait_ge(done["turned"], base(ph, "turned") + u + 1)
                wait(act, done["pv"], base(ph, "pv") + u - 1 if u >= 2 else 0)
                for n in range(turns(ph)):
                    last = act.activation(turned(ph, u, n)[:, 0:nk], ps[:, 4 + n, 0:nk], ACT.Copy)
                last.then_inc(done["pt"], 1)

            exp(0)
            exp(1)
            for s in range(len(units) + 4):
                for b in range(ph.blocks):
                    if ph.mode == "a" and s == last_unit(ph, b) + 4:
                        act.wait_ge(done["ynorm"], base(ph, "ynorm") + b + 1)
                        act.activation(yhi[:, b, 0:nq], acc[:, 0:nq], ACT.Copy).then_inc(done["yhi"], 1)
                    if ph.mode != "a" and s == last_unit(ph, b) + 2:
                        act.wait_ge(done["pv"], base(ph, "pv") + last_unit(ph, b) + 1)
                        for n in range(2):
                            if ph.mode == "b":
                                half = slice(64 * n, 64 * n + 64)
                                last = act.activation(yhi[half, b, 0:nq], ps[half, 6 + n, 0:nq], ACT.Copy)
                            else:
                                last = act.activation(yhi[:, 2 * b + n, 0:nq], ps[:, 6 + n, 0:nq], ACT.Copy)
                        last.then_inc(done["yhi"], 1)
                if s < len(units):
                    turned_copy(s)
                for b in range(ph.blocks):
                    if ph.mode == "a" and s == last_unit(ph, b) + 2:
                        act.wait_ge(done["pv"], base(ph, "pv") + last_unit(ph, b) + 1)
                        wait(act, done["ylo"], base(ph, "ylo") + b)
                        act.activation(acc[:, 0:nq], ps[:, 6 + b % 2, 0:nq], ACT.Square).then_inc(done["asq"], 1)
                    if ph.mode == "a" and s == last_unit(ph, b) + 3:
                        inverse(inv[:, 0:nq], STAT, nq, P, base(ph, "stat") + b + 1)
                if s + 2 < len(units):
                    exp(s + 2)

        def dve_attention(dve, ph, step):
            units, nq, l = ph.units, ph.nq, ph.layer
            scale = MLA_SCALE if ph.mode == "c" else HEAD_SCALE

            def biases(u):
                b, qt = units[u]
                e, nk = u % 2, T - keys(qt) * P
                dve.wait_ge(done["score"], base(ph, "score") + u + 1)
                step(dve.tensor_reduce(mx[:, e, :], ps[:, 2 * e:2 * e + 2, 0:nk], AX_X, ALU.max, negate=True))
                if ph.mode == "b":
                    negs = nsink[:, l, 2 * b:2 * b + 2]
                    step(dve.scalar_tensor_tensor(nb[:, e, :], mx[:, e, :], scale, negs, ALU.mult, ALU.min))
                    dve.tensor_tensor(sd[:, e, :], sink[:, l, 2 * b:2 * b + 2], nb[:, e, :], ALU.add)\
                       .then_inc(done["bias"], 1)
                else:
                    dve.tensor_scalar(nb[:, e, :], mx[:, e, :], scale, None, ALU.mult).then_inc(done["bias"], 1)

            def normalize(u):
                e, nk = u % 2, T - keys(units[u][1]) * P
                dve.wait_ge(done["exp"], base(ph, "exp") + u + 1)
                if ph.mode == "b":
                    step(dve.tensor_tensor(sm[:, e, :], sm[:, e, :], se[:, e, :], ALU.add))
                step(dve.reciprocal(rc[:, e, :], sm[:, e, :]))
                p0, p1 = prob[:, e, 0, 0:nk], prob[:, e, 1, 0:nk]
                if ph.mode == "a":
                    step(dve.tensor_scalar(p1, p1, rc[:, e, 1:2], lam[:, l:l + 1], ALU.mult, ALU.mult))
                    dve.scalar_tensor_tensor(p0, p0, rc[:, e, 0:1], p1, ALU.mult, ALU.subtract)\
                       .then_inc(done["prob"], 1)
                else:
                    dve.tensor_scalar(p0, p0, rc[:, e, 0:1], None, ALU.mult)
                    dve.tensor_scalar(p1, p1, rc[:, e, 1:2], None, ALU.mult).then_inc(done["prob"], 1)

            biases(0)
            biases(1)
            normalize(0)
            for s in range(len(units) + 4):
                for b in range(ph.blocks):
                    if ph.mode != "a" and s == last_unit(ph, b) + 2:
                        dve.wait_ge(done["yhi"], base(ph, "yhi") + b + 1)
                        for n in range(2):
                            if ph.mode == "b":
                                half = slice(64 * n, 64 * n + 64)
                                dst, hi, src = ylo[half, b, 0:nq], yhi[half, b, 0:nq], ps[half, 6 + n, 0:nq]
                            else:
                                c = 2 * b + n
                                dst, hi, src = ylo[:, c, 0:nq], yhi[:, c, 0:nq], ps[:, 6 + n, 0:nq]
                            last = dve.tensor_tensor(dst, src, hi.bitcast(F32), ALU.subtract)
                        last.then_inc(done["ylo"], 1)
                if s + 1 < len(units):
                    normalize(s + 1)
                if s + 2 < len(units):
                    biases(s + 2)
                for b in range(ph.blocks):
                    if ph.mode == "a" and s == last_unit(ph, b) + 3:
                        dve.wait_ge(done["inv"], base(ph, "inv") + b + 1)
                        refine(dve, step, inv[:, 0:nq], STAT, nq, P, (sub_v, acc))
                        dve.scalar_tensor_tensor(acc[:, 0:nq], ps[:, 6 + b % 2, 0:nq], subg[:, l:l + 1],
                                                 inv[:, 0:nq], ALU.mult, ALU.mult).then_inc(done["ynorm"], 1)

        def pe_attention(pe, ph):
            units = ph.units
            for b in range(BANKS):
                pe.wait_ge(bank_free[b], tiles_before(ph, b))
            pe.wait_ge(done["rope"], base(ph, "rope"))
            wait(pe, done["refined"], base(ph, "inv"))
            wait(pe, done["pt"], base(ph, "pt"))

            def scores(u):
                b, qt = units[u]
                e, kc = u % 2, keys(units[u][1])
                nk = T - kc * P
                cols, ks = slice(qt * P, (qt + 1) * P), slice(kc * P, T)
                wait(pe, done["exp"], base(ph, "exp") + u - 1 if u >= 2 else 0)
                for n in range(2):
                    o = ps[:, 2 * e + n, 0:nk]
                    half = slice(64 * n, 64 * n + 64)
                    if ph.mode == "c":
                        pe.matmul(o, q[:, 2 * b + n, cols], k[:, 2 * b + n, ks], start=True, stop=False)
                        last = pe.matmul(o, qr[half, b, cols], kr[half, ks], start=False, stop=True)
                    else:
                        kb = b if ph.mode == "a" else b // 4
                        masked = ph.mode == "b" and kc == 0
                        last = pe.matmul(o, q[half, b, cols], k[half, kb, ks], start=True, stop=not masked)
                        if masked:
                            other = (1 - qt) * P
                            last = pe.matmul(ps[:, 2 * e + n, other:other + P], ident[:, :], mask[:, qt, :],
                                             start=False, stop=True)
                last.then_inc(done["score"], 1)

            def turn(u):
                e, nk = u % 2, T - keys(units[u][1]) * P
                pe.wait_ge(done["prob"], base(ph, "prob") + u + 1)
                wait(pe, done["pt"], base(ph, "pt") + u if u else 0)
                for n in range(turns(ph)):
                    for c in range(nk // P):
                        cs = slice(c * P, (c + 1) * P)
                        last = pe.transpose(ps[:, 4 + n, cs], prob[:, e, n, cs], ident[:, :])
                last.then_inc(done["turned"], 1)

            def weighted(u):
                b, qt = units[u]
                kc0 = keys(qt)
                pe.wait_ge(done["pt"], base(ph, "pt") + u + 1)
                if qt == 0:
                    if ph.mode == "a":
                        wait(pe, done["ynorm"], base(ph, "ynorm") + b - 1 if b >= 2 else base(ph, "ynorm"))
                        wait(pe, done["ylo"], base(ph, "ylo") if b < 2 else 0)
                    else:
                        wait(pe, done["ylo"], base(ph, "ylo") + b)
                for n in range(turns(ph)):
                    to = 6 + (b % 2 if ph.mode == "a" else n)
                    vc = {"a": b, "b": b // 4, "c": 2 * b + n}[ph.mode]
                    for kc in range(kc0, T // P):
                        last = pe.matmul(ps[:, to, qt * P:(qt + 1) * P], v[:, kc, vc * P:(vc + 1) * P],
                                         turned(ph, u, n)[:, (kc - kc0) * P:(kc - kc0 + 1) * P],
                                         start=kc == kc0, stop=kc == T // P - 1)
                last.then_inc(done["pv"], 1)

            scores(0)
            scores(1)
            for s in range(len(units) + 3):
                if s < len(units):
                    turn(s)
                if s + 2 < len(units):
                    scores(s + 2)
                if 1 <= s <= len(units):
                    weighted(s - 1)
                for b in range(ph.blocks):
                    if ph.mode == "a" and s == last_unit(ph, b) + 2:
                        pe.wait_ge(done["asq"], base(ph, "asq") + b + 1)
                        wait(pe, done["refined"], base(ph, "inv") + b)
                        pe.matmul(ps[:, STAT, 0:ph.nq], ones[:, :], acc[:, 0:ph.nq], start=True, stop=True)\
                          .then_inc(done["stat"], 1)

        def pool_attention(pool, ph):
            for b in range(ph.blocks):
                pool.wait_ge(done["yhi"], base(ph, "yhi") + b + 1)
                pool.tensor_tensor(ylo[:, b, 0:ph.nq], acc[:, 0:ph.nq], yhi[:, b, 0:ph.nq].bitcast(F32),
                                   ALU.subtract).then_inc(done["ylo"], 1)

        @block.sync
        def _(sp):
            sp.dma_start(cvec[:, :, :], io["cvec"]).then_inc(c_loaded, 16)
            sp.dma_start(c_all[:, :], io["c_rows"].to_broadcast([P, 2 * D])).then_inc(c_all_loaded, 16)

            def first_pair(pair):
                some = slice(pair * ADA_PAIR, (pair + 1) * ADA_PAIR)
                sp.dma_start(shift_w[:, some, :], io["shift_w"][pair]).then_inc(shift_w_loaded[pair], 16)
                sp.dma_start(scale_w[:, some, :], io["scale_w"][pair]).then_inc(scale_w_loaded[pair], 16)

            first_pair(0)
            small = [(ada_b, "ada_b"), (norm_g, "norm_g"), (dlam, "dlam"), (subg, "subg"), (lat_g, "lat_g"),
                     (cos, "cos"), (sin, "sin"), (ident, "ident"), (mask, "mask")]
            for dst, name in small:
                sp.dma_start(dst[tuple([slice(None)] * len(dst.shape))], io[name]).then_inc(consts_loaded, 16)
            sp.dma_start(sink[:, :, :].rearrange("p l n -> p (l n)"),
                         io["sink"].to_broadcast([P, LAYERS * 16])).then_inc(consts_loaded, 16)
            sp.dma_start(x[:, :, :], io["x"]).then_inc(x_loaded, 16)
            for pair in range(1, KC // ADA_PAIR):
                first_pair(pair)
            sp.wait_ge(silu_rows_made, 1)
            sp.dma_start(silu_rows, c_all[0:1, :]).then_inc(silu_rows_stored, 16)

            def group_loads(ph, i):
                for j in range(ph.groups):
                    g = Idx(ph.g + j, ph.groups, i)
                    wait(sp, lo_ready, g.val(1 - RAW))
                    src, n = source(ph, i, j)
                    sp.dma_start(raw[:, g.ring(RAW), 0:n], src).then_inc(raw_loaded[g.ring(RAW)], 16)

            for ph in plan:
                if ph.iters:
                    run(sp, ph, lambda i, ph=ph: group_loads(ph, i))
            sp.wait_ge(done["x"], base(plan[-1], "x") + KC)
            sp.dma_start(out, x[:, :, 0:S]).then_inc(stored, 16)
            sp.wait_ge(stored, 16)

        @block.gpsimd
        def _(pool):
            def add_square(n, number, tokens):
                pool.wait_ge(done["sq"], n.val(1))
                wait(pool, done["acc"], n.val())
                pool.tensor_tensor(acc[:, 0:tokens], acc[:, 0:tokens], tmp[:, number, 0:tokens], ALU.add)\
                    .then_inc(done["acc"], 1)

            def load_ada(block):
                index = block.val()
                src = io["ada_rows"][index] if isinstance(index, int) else \
                    io["ada_rows"][bass.ds(index, 1)].rearrange("o p n -> (o p) n")
                slot = block.ring(ADA_RING)
                pool.dma_start(ada[:, slot, :], src).then_inc(ada_loaded[slot], 16)

            def feed_modulation_vectors(ph):
                pool.wait_ge(done["xlo"], base(ph, "xlo"))
                pool.wait_ge(silu_rows_stored, 16)
                pool.dma_start(c_all[:, :], silu_rows.to_broadcast([P, 2 * D])).then_inc(c_spread, 16)
                first = ada_order.index(ph.vectors[0]) * KC

                def body(i):
                    for j in range(ADA_RING):
                        block = Idx(first + j, ADA_RING, i)
                        pool.wait_ge(ada_dot, Idx(2 * (first + j + 1), 2 * ADA_RING, i).val())
                        load_ada(block.plus(ADA_RING))

                pairs = len(ph.vectors) * KC // ADA_RING
                final = ph.vectors[-1] == ada_order[-1]
                with pool.Fori(0, pairs - final) as i:
                    body(i)

            for j in range(ADA_RING):
                load_ada(Idx(j, 0, 0))
            zeros = 0
            for ph in plan:
                if ph.vectors:
                    feed_modulation_vectors(ph)
                if ph.kind == "norm" and ph.pre:
                    wait(pool, done["stat"], base(ph, "stat") + (1 if ph.post else 0))
                    pool.memset(acc[:, :], 0.0).then_inc(acc_zero, 1)
                    zeros += 1
                    pool.wait_ge(acc_zero, zeros)
                    for c in range(KC):
                        add_square(Idx(base(ph, "sq") + c, 0, 0), c % 2, ph.tokens)
                if ph.kind == "y":
                    pool.wait_ge(done["stat"], base(ph, "stat"))
                    if "ylo" in ph.at:
                        pool.wait_ge(done["ylo"], base(ph, "ylo"))
                    pool.memset(acc[:, :], 0.0).then_inc(acc_zero, 1)
                    zeros += 1
                    pool.wait_ge(acc_zero, zeros)

                    def body(i, ph=ph):
                        for j in range(ph.tiles):
                            add_square(Idx(base(ph, "sq") + j, ph.tiles, i), j % 2, ph.tokens)

                    run(pool, ph, body)
                if ph.kind == "attn" and ph.mode == "a":
                    pool_attention(pool, ph)
                if ph.kind == "rope":
                    def body(i, ph=ph):
                        for j in range(ph.tiles):
                            n = Idx(ph.n + j, ph.tiles, i)
                            r = Idx(base(ph, "rope") + j, ph.tiles, i)
                            pool.wait_ge(bank_free[n.ring(BANKS)], n.lap(BANKS, 1))
                            wait(pool, done["rope"], r.val(-1))
                            pool.tensor_tensor(acc[:, r.ring(2) * S:(r.ring(2) + 1) * S],
                                               tmp[:, r.ring(2), 0:S], cos[:, :], ALU.mult).then_inc(rope_mul, 1)

                    if base(ph, "rope") == 0:
                        pool.wait_ge(consts_loaded, 160)
                    run(pool, ph, body)

        @block.scalar
        def _(act):
            steps = 0
            table = [None]

            def use_table(name):
                if table[0] != name:
                    act.preload_act_table_set(name)
                    table[0] = name

            def split_hi(g):
                if isinstance(g.i, int) and g.val() >= all_groups:
                    return
                act.wait_ge(raw_loaded[g.ring(RAW)], g.lap(RAW, 1) * 16)
                wait(act, group_used, g.val(1 - SPLIT))
                act.activation(whi[:, g.ring(SPLIT), :], raw[:, g.ring(RAW), :], ACT.Copy).then_inc(hi_ready, 1)

            def inverse(dst, bank, tokens, width, stat):
                nonlocal steps
                act.wait_ge(done["stat"], stat)
                act.activation(dst, ps[:, bank, 0:tokens], ACT.Ln, bias=eps[:, 0:1], scale=1.0 / width)\
                   .then_inc(act_step, 1)
                steps += 1
                act.wait_ge(act_step, steps)
                act.activation(dst, dst, ACT.Exp, scale=-0.5).then_inc(done["inv"], 1)

            def square(src, number, tokens, n):
                wait(act, done["acc"], n.val(-1))
                act.activation(tmp[:, number, 0:tokens], src, ACT.Square).then_inc(done["sq"], 1)

            use_table(SILU)
            act.wait_ge(c_loaded, 16)
            act.activation(cvec[:, :, :], cvec[:, :, :], ACT.Silu).then_inc(silu_c, 1)
            act.wait_ge(c_all_loaded, 16)
            act.activation(c_all[:, :], c_all[:, :], ACT.Silu).then_inc(silu_rows_made, 1)
            use_table(LN_EXP)
            act.wait_ge(consts_made, 2)

            for ph in plan:
                tk = ph.tokens
                if ph.kind == "norm":
                    if ph.post:
                        inverse(inv[:, 0:tk], STAT, tk, D, base(ph, "stat") + 1)
                    if ph.pre:
                        for c in range(KC):
                            if ph.post:
                                act.wait_ge(done["x"], base(ph, "x") + c + 1)
                            elif c == 0:
                                act.wait_ge(x_loaded, 16)
                            square(x[:, c, 0:tk], c % 2, tk, Idx(base(ph, "sq") + c, 0, 0))
                        if not ph.post:
                            split_hi(Idx(0, 0, 0))
                        inverse(inv[:, 0:tk], STAT, tk, D, base(ph, "stat") + (2 if ph.post else 1))
                        l, sub = ph.pre
                        for c in range(KC):
                            act.wait_ge(done["scaled"], base(ph, "scaled") + c + 1)
                            for s in streams(tk):
                                last = act.activation(xhi[:, c, sl(s)], work[:, c, sl(s)], ACT.Identity,
                                                      bias=mods[:, l, 3 * sub, c, s:s + 1])
                            last.then_inc(done["xhi"], 1)
                    if not ph.post:
                        act.wait_ge(lam_sum, 1)
                        act.activation(elam[:, :, :], ps[:, STAT, 0:2 * LAYERS].rearrange("p (l n) -> p l n", n=2),
                                       ACT.Exp).then_inc(lam_exp, 1)
                elif ph.kind == "ffn_in":
                    use_table(SILU)

                    def body(i, ph=ph, tk=tk):
                        for j in range(2):
                            g = Idx(ph.g + 2 * j, ph.groups, i)
                            n = Idx(ph.n + 2 * j, ph.tiles, i)
                            p = Idx(base(ph, "ghi") + j, 2, i)
                            split_hi(g.plus(1))
                            split_hi(g.plus(2))
                            a, b = n, n.plus(1)
                            act.wait_ge(group_used, last_group(ph, i, 2 * j).val(1))
                            act.activation(tmp[:, 0, 0:tk], ps[:, a.ring(BANKS), 0:tk], ACT.Silu)\
                               .then_inc(bank_free[a.ring(BANKS)], 1)
                            act.wait_ge(bank_free[b.ring(BANKS)], b.lap(BANKS, 1))
                            act.activation(chunk(ghi, Idx(j, 2, i), tk), tmp[:, 1, 0:tk], ACT.Copy)\
                               .then_inc(done["ghi"], 1)

                    run(act, ph, body)
                elif ph.kind == "y":
                    use_table(LN_EXP)
                    if ph.src == "ffn_out":
                        act.wait_ge(done["glo"], base(ph, "glo"))
                        act.wait_ge(done["made"], base(ph, "made"))

                    def body(i, ph=ph, tk=tk):
                        for j in range(ph.tiles):
                            g = Idx(ph.g + ph.per_tile * j, ph.groups, i)
                            n = Idx(ph.n + j, ph.tiles, i)
                            for t in range(ph.per_tile):
                                split_hi(g.plus(1 + t))
                            act.wait_ge(group_used, last_group(ph, i, j).val(1))
                            square(ps[:, n.ring(BANKS), 0:tk], j % 2, tk,
                                   Idx(base(ph, "sq") + j, ph.tiles, i))
                            act.activation(chunk(work, Idx(j, ph.tiles, i), tk), ps[:, n.ring(BANKS), 0:tk],
                                           ACT.Copy).then_inc(bank_free[n.ring(BANKS)], 1)

                    run(act, ph, body)
                elif ph.kind == "rope":
                    for b in range(BANKS):
                        act.wait_ge(bank_free[b], tiles_before(ph, b))
                    wait(act, done["m"], base(ph, "m"))

                    def body(i, ph=ph, tk=tk):
                        for j in range(ph.tiles):
                            split_ahead(split_hi, ph, i, j)
                            n = Idx(ph.n + j, ph.tiles, i)
                            r = Idx(base(ph, "rope") + j, ph.tiles, i)
                            act.wait_ge(group_used, last_group(ph, i, j).val(1))
                            wait(act, done["rope"], r.val(-1))
                            last = act.activation(tmp[:, r.ring(2), 0:S], ps[:, n.ring(BANKS), 0:S], ACT.Copy)
                            if tk == T:
                                last = act.activation(rope_dst(ph, i, j, slice(S, T)),
                                                      ps[:, n.ring(BANKS), S:T], ACT.Copy)
                            last.then_inc(bank_free[n.ring(BANKS)], 1)

                    run(act, ph, body)
                elif ph.kind == "plain":
                    i = 0
                    for j in range(ph.tiles):
                        split_ahead(split_hi, ph, i, j)
                        n = bank(ph, i, j)
                        act.wait_ge(group_used, last_group(ph, i, j).val(1))
                        dst = {"lat": lat, "qn": q, "kn": k}[ph.dst]
                        act.activation(dst[:, j, 0:tk], ps[:, n.ring(BANKS), 0:tk], ACT.Copy)\
                           .then_inc(bank_free[n.ring(BANKS)], 1)
                elif ph.kind == "v":
                    def body(i, ph=ph):
                        for j in range(ph.groups):
                            split_hi(Idx(ph.g + j + 1, ph.groups, i))
                        for t in range(ph.tiles):
                            n = bank(ph, i, t)
                            act.wait_ge(group_used, last_group(ph, i, t).val(1))
                            col = i * ph.cols
                            dst = v[:, t, col:col + ph.cols] if isinstance(i, int) else \
                                v[:, t, bass.ds(col, ph.cols)]
                            act.activation(dst, ps[:, n.ring(BANKS), 0:ph.cols], ACT.Copy)\
                               .then_inc(bank_free[n.ring(BANKS)], 1)

                    run(act, ph, body)
                elif ph.kind == "merge":
                    use_table(SIGMOID)

                    def body(i, ph=ph, tk=tk):
                        for j in range(2):
                            g = Idx(ph.g + 2 * j, ph.groups, i)
                            gate = Idx(ph.n + 2 * j, ph.tiles, i)
                            split_hi(g.plus(1))
                            split_hi(g.plus(2))
                            act.wait_ge(group_used, last_group(ph, i, 2 * j).val(1))
                            before = gate.plus(-1)
                            if j or not (isinstance(i, int) and i == 0):
                                act.wait_ge(bank_free[before.ring(BANKS)], before.lap(BANKS, 1))
                            act.activation(tmp[:, 0, 0:tk], ps[:, gate.ring(BANKS), 0:tk], ACT.Sigmoid)\
                               .then_inc(bank_free[gate.ring(BANKS)], 1)

                    run(act, ph, body)
                elif ph.kind == "msplit":
                    for c in range(KC):
                        act.wait_ge(done["m"], base(ph, "m") - KC + c + 1)
                        if c == 0:
                            act.wait_ge(group_used, ph.g)
                        act.activation(yhi[:, c, 0:tk], work[:, c, 0:tk], ACT.Copy).then_inc(done["mhi"], 1)
                elif ph.kind == "latnorm":
                    use_table(LN_EXP)
                    for c in range(QC + KVC):
                        if c == 0:
                            act.wait_ge(done["rope"], base(ph, "rope"))
                        if c >= 2:
                            act.wait_ge(done["stat"], base(ph, "stat") + c - 1)
                        act.activation(tmp[:, c % 2, :], lat[:, c, :], ACT.Square).then_inc(done["lsq"], 1)
                    inverse(inv[:, :], 4, T, Q_RANK, base(ph, "stat") + QC)
                    inverse(acc[:, :], 5, T, KV_RANK, base(ph, "stat") + QC + KVC)
                    for c in range(QC + KVC):
                        act.wait_ge(done["lt"], base(ph, "lt") + c + 1)
                        act.activation(lhi[:, c, :], lat[:, c, :], ACT.Copy).then_inc(done["lhi"], 1)
                elif ph.kind == "attn":
                    use_table(LN_EXP)
                    act_attention(act, ph, inverse)

        @block.vector
        def _(dve):
            steps = 0

            def split_lo(g):
                if isinstance(g.i, int) and g.val() >= all_groups:
                    return
                dve.wait_ge(hi_ready, g.val(1))
                dve.tensor_tensor(wlo[:, g.ring(SPLIT), :], raw[:, g.ring(RAW), :],
                                  whi[:, g.ring(SPLIT), :].bitcast(F32), ALU.subtract).then_inc(lo_ready, 1)

            def step(ins):
                nonlocal steps
                ins.then_inc(dve_step, 1)
                steps += 1
                dve.wait_ge(dve_step, steps)

            def first_modulations():
                dve.wait_ge(silu_rows_made, 1)
                for block in range(KC):
                    if block % ADA_PAIR == 0:
                        dve.wait_ge(scale_w_loaded[block // ADA_PAIR], 16)
                    for s in range(2):
                        step(dve.scalar_tensor_tensor(products[:, s, :], scale_w[:, block, :], 1.0,
                                                      c_all[:, s * D:(s + 1) * D], ALU.mult, ALU.mult,
                                                      accum_out=mods[:, 0, 1, block, s:s + 1]))
                dve.wait_ge(consts_loaded, 160)
                step(dve.tensor_tensor(mods[:, 0, 1, :, :], mods[:, 0, 1, :, :], ada_b[:, 0, 1, :, :], ALU.add))
                step(scale_or_gate(dve, 0, 1))
                dve.wait_ge(first_shift, 1)
                src = ps[:, ADA_BANK, 0:2 * KC].rearrange("p (c n) -> p c n", n=2)
                step(dve.tensor_tensor(mods[:, 0, 0, :, :], src, ada_b[:, 0, 0, :, :], ALU.add))

            spreads = 0

            def ada_block(block):
                slot = block.ring(ADA_RING)
                dve.wait_ge(c_spread, 16 * spreads)
                dve.wait_ge(ada_loaded[slot], block.lap(ADA_RING, 1) * 16)
                for s in range(2):
                    dot = Idx(2 * block.c + s, 2 * block.step, block.i)
                    wait(dve, ada_dot, dot.val(-1))
                    to = dot.val(2 * FIRST_ADA * KC)
                    to = mods_flat[:, to:to + 1] if isinstance(to, int) else mods_flat[:, bass.ds(to, 1)]
                    dve.scalar_tensor_tensor(products[:, s, :], ada[:, slot, :], 1.0, c_all[:, s * D:(s + 1) * D],
                                             ALU.mult, ALU.mult, accum_out=to).then_inc(ada_dot, 1)

            def blocks_per_body(ph):
                left, counts = len(ph.vectors) * KC, []
                for n in range(ph.iters):
                    bodies = ph.iters - n
                    even = left // bodies // ADA_RING * ADA_RING
                    counts.append(min(left, max(even, ADA_RING)))
                    left -= counts[-1]
                assert not left
                return counts

            def finish_vectors(ph):
                first = ada_order.index(ph.vectors[0]) * KC
                last = first + len(ph.vectors) * KC
                dve.wait_ge(ada_dot, 2 * last)
                span = slice(2 * (FIRST_ADA * KC + first), 2 * (FIRST_ADA * KC + last))
                step(dve.tensor_tensor(mods_flat[:, span], mods_flat[:, span], ada_b_flat[:, span], ALU.add))
                for l, m in ph.vectors:
                    if m % 3:
                        scale_or_gate(dve, l, m).then_inc(done["made"], 1)

            dve.memset(ones[:, :], 1.0).then_inc(consts_made, 1)
            dve.memset(eps[:, :], EPS).then_inc(consts_made, 1)
            first_modulations()
            for l in range(LAYERS):
                for n in range(2):
                    dve.tensor_tensor(dprod[:, l, n:n + 1], dlam[:, l, 2 * n:2 * n + 1],
                                      dlam[:, l, 2 * n + 1:2 * n + 2], ALU.mult).then_inc(consts_made, 1)
            for l in range(LAYERS):
                step(dve.tensor_scalar(subg[:, l:l + 1], subg[:, l:l + 1], 1.0 - lambda_init[l], None, ALU.mult))
            step(dve.tensor_scalar(nsink[:, :, :], sink[:, :, :], -1.0, None, ALU.mult))


            for ph in plan:
                tk = ph.tokens
                if ph.kind == "norm":
                    if ph.post:
                        l, sub = ph.post
                        dve.wait_ge(done["inv"], base(ph, "inv") + 1)
                        refine(dve, step, inv[:, 0:tk], STAT, tk, D, (tmp[:, 0, :], tmp[:, 1, :]))
                        dve.wait_ge(done["made"], base(ph, "made"))

                        def gated(c):
                            for s in streams(tk):
                                last = dve.scalar_tensor_tensor(
                                    work[:, c, sl(s)], work[:, c, sl(s)], mods[:, l, 3 * sub + 2, c, s:s + 1],
                                    inv[:, sl(s)], ALU.mult, ALU.mult)
                            last.then_inc(dve_step, 1)

                        gated(0)
                        for c in range(KC):
                            if c + 1 < KC:
                                gated(c + 1)
                            dve.wait_ge(dve_step, steps + c + 1)
                            dve.tensor_tensor(x[:, c, 0:tk], x[:, c, 0:tk], work[:, c, 0:tk], ALU.add)\
                               .then_inc(done["x"], 1)
                        steps += KC
                    if ph.pre:
                        l, sub = ph.pre
                        if not ph.post:
                            split_lo(Idx(0, 0, 0))
                        dve.wait_ge(done["inv"], base(ph, "inv") + (2 if ph.post else 1))
                        refine(dve, step, inv[:, 0:tk], STAT, tk, D, (tmp[:, 0, :], tmp[:, 1, :]))

                        def scaled(c):
                            for s in streams(tk):
                                last = dve.scalar_tensor_tensor(
                                    work[:, c, sl(s)], x[:, c, sl(s)], mods[:, l, 3 * sub + 1, c, s:s + 1],
                                    inv[:, sl(s)], ALU.mult, ALU.mult)
                            last.then_inc(done["scaled"], 1)

                        scaled(0)
                        for c in range(KC):
                            if c + 1 < KC:
                                scaled(c + 1)
                            dve.wait_ge(done["xhi"], base(ph, "xhi") + c + 1)
                            for s in streams(tk):
                                last = dve.scalar_tensor_tensor(
                                    xlo[:, c, sl(s)], work[:, c, sl(s)], mods[:, l, 3 * sub, c, s:s + 1],
                                    xhi[:, c, sl(s)].bitcast(F32), ALU.add, ALU.subtract)
                            last.then_inc(done["xlo"], 1)
                    if not ph.post:
                        dve.wait_ge(lam_exp, 1)
                        for l in range(LAYERS):
                            step(dve.scalar_tensor_tensor(lam[:, l:l + 1], elam[:, l, 0:1], lambda_init[l],
                                                          elam[:, l, 1:2], ALU.add, ALU.subtract))
                elif ph.kind == "ffn_in":
                    def body(i, count, first, ph=ph, tk=tk):
                        for j in range(2):
                            g = Idx(ph.g + 2 * j, ph.groups, i)
                            a, b = bank(ph, i, 2 * j), bank(ph, i, 2 * j + 1)
                            p = Idx(base(ph, "ghi") + j, 2, i)
                            split_lo(g.plus(1))
                            split_lo(g.plus(2))
                            dve.wait_ge(bank_free[a.ring(BANKS)], a.lap(BANKS, 1))
                            dve.wait_ge(group_used, last_group(ph, i, 2 * j + 1).val(1))
                            dve.tensor_tensor(tmp[:, 1, 0:tk], tmp[:, 0, 0:tk], ps[:, b.ring(BANKS), 0:tk],
                                              ALU.mult).then_inc(bank_free[b.ring(BANKS)], 1)
                            for n in range(count // 2):
                                ada_block(Idx(first + j * count // 2 + n, count, i))
                            dve.wait_ge(done["ghi"], p.val(1))
                            c = Idx(j, 2, i)
                            dve.tensor_tensor(chunk(glo, c, tk), tmp[:, 1, 0:tk], chunk(ghi, c, tk).bitcast(F32),
                                              ALU.subtract).then_inc(done["glo"], 1)

                    counts = blocks_per_body(ph)
                    spreads += 1
                    start, block = 0, ada_order.index(ph.vectors[0]) * KC
                    while start < ph.iters:
                        end = start + 1
                        while end < ph.iters and counts[end] == counts[start] and not (ph.peel_first and start == 0):
                            end += 1
                        count = counts[start]
                        if end - start > 1:
                            with dve.Fori(start, end) as i:
                                body(i, count, block - start * count)
                        else:
                            body(start, count, block - start * count)
                        block += (end - start) * count
                        start = end
                    finish_vectors(ph)
                elif ph.kind == "y":
                    def body(i, ph=ph):
                        for j in range(ph.groups):
                            split_lo(Idx(ph.g + j + 1, ph.groups, i))

                    run(dve, ph, body)
                elif ph.kind == "rope":
                    start = steps

                    def body(i, ph=ph, start=start):
                        for j in range(ph.tiles):
                            split_ahead(split_lo, ph, i, j)
                            n = bank(ph, i, j)
                            r = Idx(base(ph, "rope") + j, ph.tiles, i)
                            st = Idx(start + 2 * j, 2 * ph.tiles, i)
                            a = tmp[:, r.ring(2), 0:S]
                            b = tmp[:, r.ring(2), S:T]
                            dve.wait_ge(bank_free[n.ring(BANKS)], n.lap(BANKS, 1))
                            dve.stream_shuffle(b, a, [(m + 16) % 32 for m in range(32)]).then_inc(dve_step, 1)
                            dve.wait_ge(dve_step, st.val(1))
                            dve.tensor_tensor(b, b, sin[:, :], ALU.mult).then_inc(dve_step, 1)
                            dve.wait_ge(dve_step, st.val(2))
                            dve.wait_ge(rope_mul, r.val(1))
                            dve.tensor_tensor(rope_dst(ph, i, j, slice(0, S)),
                                              acc[:, r.ring(2) * S:(r.ring(2) + 1) * S], b, ALU.add)\
                               .then_inc(done["rope"], 1)

                    for i in range(ph.iters):
                        body(i)
                    steps += 2 * ph.tiles * ph.iters
                elif ph.kind == "plain":
                    for j in range(ph.tiles):
                        split_ahead(split_lo, ph, 0, j)
                elif ph.kind == "v":
                    def body(i, ph=ph):
                        for j in range(ph.groups):
                            split_lo(Idx(ph.g + j + 1, ph.groups, i))

                    run(dve, ph, body)
                elif ph.kind == "merge":
                    def body(i, ph=ph, tk=tk):
                        for j in range(2):
                            g = Idx(ph.g + 2 * j, ph.groups, i)
                            a, b = bank(ph, i, 2 * j), bank(ph, i, 2 * j + 1)
                            split_lo(g.plus(1))
                            split_lo(g.plus(2))
                            dve.wait_ge(bank_free[a.ring(BANKS)], a.lap(BANKS, 1))
                            dve.wait_ge(group_used, last_group(ph, i, 2 * j + 1).val(1))
                            c = Idx(j, 2, i)
                            dst = chunk(work, c, tk) if ph.r == 0 else tmp[:, 1, 0:tk]
                            dve.tensor_tensor(dst, tmp[:, 0, 0:tk], ps[:, b.ring(BANKS), 0:tk], ALU.mult)\
                               .then_inc(bank_free[b.ring(BANKS)], 1)
                            if ph.r:
                                dve.wait_ge(bank_free[b.ring(BANKS)], b.lap(BANKS, 1))
                                dve.tensor_tensor(chunk(work, c, tk), chunk(work, c, tk), tmp[:, 1, 0:tk], ALU.add)\
                                   .then_inc(done["m"], 1)

                    run(dve, ph, body)
                elif ph.kind == "msplit":
                    for c in range(KC):
                        dve.wait_ge(done["mhi"], base(ph, "mhi") + c + 1)
                        dve.tensor_tensor(ylo[:, c, 0:tk], work[:, c, 0:tk], yhi[:, c, 0:tk].bitcast(F32),
                                          ALU.subtract).then_inc(done["mlo"], 1)
                elif ph.kind == "latnorm":
                    dve.wait_ge(done["inv"], base(ph, "inv") + 2)
                    refine(dve, step, inv[:, :], 4, T, Q_RANK, (tmp[:, 0, :], tmp[:, 1, :]))
                    refine(dve, step, acc[:, :], 5, T, KV_RANK, (tmp[:, 0, :], tmp[:, 1, :]))

                    def normed(c):
                        dve.scalar_tensor_tensor(lat[:, c, :], lat[:, c, :], lat_g[:, ph.layer, c:c + 1],
                                                 (inv if c < QC else acc)[:, :], ALU.mult, ALU.mult)\
                           .then_inc(done["lt"], 1)

                    normed(0)
                    for c in range(QC + KVC):
                        if c + 1 < QC + KVC:
                            normed(c + 1)
                        dve.wait_ge(done["lhi"], base(ph, "lhi") + c + 1)
                        dve.tensor_tensor(llo[:, c, :], lat[:, c, :], lhi[:, c, :].bitcast(F32), ALU.subtract)\
                           .then_inc(done["llo"], 1)
                elif ph.kind == "attn":
                    dve_attention(dve, ph, step)

        @block.tensor
        def _(pe):
            def shift_products():
                pe.wait_ge(silu_c, 1)
                for block in range(KC):
                    if block % ADA_PAIR == 0:
                        pe.wait_ge(shift_w_loaded[block // ADA_PAIR], 16)
                    for c in range(KC):
                        last = pe.matmul(ps[:, ADA_BANK, 2 * block:2 * block + 2],
                                         shift_w[:, block, c * P:(c + 1) * P], cvec[:, c, :],
                                         start=c == 0, stop=c == KC - 1)
                last.then_inc(first_shift, 1)

            def stat(ph, before):
                wait(pe, done["refined"], base(ph, "inv") + before)
                wait(pe, done["pt"], base(ph, "pt"))
                pe.matmul(ps[:, STAT, 0:ph.tokens], ones[:, :], acc[:, 0:ph.tokens], start=True, stop=True)\
                  .then_inc(done["stat"], 1)

            def group_pieces(ph, j):
                if ph.src == "ffn_out":
                    tile, part = divmod(j, 3)
                    n = KC if part < 2 else FC - 2 * KC
                    return [(tile, KC * part + c, c * P, part == 0 and c == 0, part == 2 and c == n - 1)
                            for c in range(n)]
                per, depth = ph.tiles // ph.groups, {"uq": QC, "uk": KVC}.get(ph.src, KC)
                return [(per * j + t, c, (t * depth + c) * P, c == 0, c == depth - 1)
                        for t in range(per) for c in range(depth)]

            def moving(ph, tile):
                tk, j = ph.tokens, tile
                if ph.kind == "merge" and j % 2:
                    return yhi, ylo, 0, "ylo", None
                if ph.src == "ffn_out":
                    return ghi, glo, 0, "glo", FC
                if ph.src == "wo":
                    return yhi, ylo, 0, "mlo", KC
                if ph.src == "uq":
                    return lhi, llo, 0, "llo", QC + KVC
                if ph.src == "uk":
                    return lhi, llo, QC, "llo", QC + KVC
                return xhi, xlo, 0, "xlo", KC

            def group_products(ph, i, j):
                g = Idx(ph.g + j, ph.groups, i)
                s = g.ring(SPLIT)
                pieces = group_pieces(ph, j)
                tk = ph.tokens
                for tile, c, col, start, stop in pieces:
                    hi, lo, first, ready, chunks = moving(ph, tile)
                    n = bank(ph, i, tile)
                    if start:
                        wait(pe, bank_free[n.ring(BANKS)], n.lap(BANKS))
                    if tile == 0 or (ph.kind == "merge" and tile == 1 and c == 0):
                        pe.wait_ge(done[ready], base(ph, ready) if chunks is None else
                                   base(ph, ready) - chunks + first + c + 1)
                    if (tile, c) == pieces[0][:2]:
                        pe.wait_ge(hi_ready, g.val(1))
                    o = ps[:, n.ring(BANKS), 0:tk]
                    w = whi[:, s, col:col + P]
                    pe.matmul(o, w, hi[:, first + c, 0:tk], start=start, stop=False)
                    pe.matmul(o, w, lo[:, first + c, 0:tk], start=False, stop=False)
                pe.wait_ge(lo_ready, g.val(1))
                for tile, c, col, start, stop in pieces:
                    hi, lo, first, _, _ = moving(ph, tile)
                    n = bank(ph, i, tile)
                    last = pe.matmul(ps[:, n.ring(BANKS), 0:tk], wlo[:, s, col:col + P], hi[:, first + c, 0:tk],
                                     start=False, stop=stop)
                last.then_inc(group_used, 1)

            def token_products(ph, i, j):
                g = Idx(ph.g + j, ph.groups, i)
                s = g.ring(SPLIT)
                hi, lo, first = (lhi, llo, QC) if ph.x == "lat" else (xhi, xlo, 0)
                pe.wait_ge(hi_ready, g.val(1))
                for low in range(2):
                    if low:
                        pe.wait_ge(lo_ready, g.val(1))
                    for t in range(T // P):
                        n = bank(ph, i, t)
                        if j == 0 and not low:
                            wait(pe, bank_free[n.ring(BANKS)], n.lap(BANKS))
                        o = ps[:, n.ring(BANKS), 0:ph.cols]
                        for c in range(ph.kpg):
                            kc = first + j * ph.kpg + c
                            cols = slice(c * ph.cols, (c + 1) * ph.cols)
                            tokens = slice(t * P, (t + 1) * P)
                            if low:
                                last = pe.matmul(o, hi[:, kc, tokens], wlo[:, s, cols], start=False,
                                                 stop=j == ph.groups - 1 and c == ph.kpg - 1)
                            else:
                                pe.matmul(o, hi[:, kc, tokens], whi[:, s, cols], start=j == 0 and c == 0,
                                          stop=False)
                                pe.matmul(o, lo[:, kc, tokens], whi[:, s, cols], start=False, stop=False)
                last.then_inc(group_used, 1)

            for ph in plan:
                if ph.kind == "norm":
                    if ph.post:
                        pe.wait_ge(done["acc"], base(ph, "acc"))
                        stat(ph, 0)
                    else:
                        shift_products()
                    if ph.pre:
                        pe.wait_ge(done["acc"], base(ph, "acc") + KC)
                        stat(ph, 1 if ph.post else 0)
                    if not ph.post:
                        pe.wait_ge(consts_made, 2 + 2 * LAYERS)
                        pe.wait_ge(done["refined"], 1)
                        pe.matmul(ps[:, STAT, 0:2 * LAYERS], ones[0:64, :],
                                  dprod[:, :, :].rearrange("p l n -> p (l n)"), start=True, stop=True)\
                          .then_inc(lam_sum, 1)
                elif ph.kind == "latnorm":
                    wait(pe, done["pt"], base(ph, "pt"))
                    wait(pe, done["refined"], base(ph, "inv"))
                    for c in range(QC + KVC):
                        pe.wait_ge(done["lsq"], base(ph, "lsq") + c + 1)
                        pe.matmul(ps[:, 4 if c < QC else 5, :], ones[:, :], tmp[:, c % 2, :],
                                  start=c in (0, QC), stop=c in (QC - 1, QC + KVC - 1)).then_inc(done["stat"], 1)
                elif ph.kind == "attn":
                    pe_attention(pe, ph)
                elif ph.iters:
                    wait(pe, done["exp"], base(ph, "exp"))
                    if ph.kind == "v":
                        def body(i, ph=ph):
                            for j in range(ph.groups):
                                token_products(ph, i, j)
                    else:
                        def body(i, ph=ph):
                            for j in range(ph.groups):
                                group_products(ph, i, j)

                    run(pe, ph, body)



def blocked(w):
    *lead, k, m = w.shape
    n = len(lead)
    w = w.reshape(*lead, k // P, P, m // P, P)
    w = w.transpose(*range(n), n + 2, n + 1, n, n + 3)
    return w.reshape(*lead, m // P, P, k)


def by_rows(w, cols, kpg):
    l, k, m = w.shape
    w = w.reshape(l, k // P // kpg, kpg, P, m // cols, cols)
    return w.transpose(0, 4, 1, 3, 2, 5).reshape(l, -1, P, kpg * cols)


def layout(x, c, ctx, c_ctx, ada_w, ada_b, norm_g, ffn_w_in, ffn_w_out, mix_w_in, diff_lambda, diff_subln_g,
           win_sink, mla_q_norm_g, mla_kv_norm_g, mla_w_uq, mla_w_ukv, branch_w, mix_w_out):
    L = LAYERS
    a = {}
    a["x"] = np.concatenate([x[0], ctx[0]], 0).T.reshape(KC, P, T).transpose(1, 0, 2)
    a["cvec"] = np.stack([c[0], c_ctx], -1).reshape(KC, P, 2).transpose(1, 0, 2)
    a["c_rows"] = np.concatenate([c[0], c_ctx])[None, :]
    a["shift_w"] = blocked(ada_w[0][:, :D]).reshape(-1, ADA_PAIR, P, D).transpose(0, 2, 1, 3)
    a["scale_w"] = ada_w[0][:, D:2 * D].T.reshape(-1, ADA_PAIR, P, D).transpose(0, 2, 1, 3)
    a["ada_rows"] = ada_w.transpose(0, 2, 1).reshape(-1, P, D)[FIRST_ADA * KC:]
    a["ada_b"] = np.repeat(ada_b.reshape(L, N_MOD, KC, P).transpose(3, 0, 1, 2)[..., None], 2, -1)
    a["norm_g"] = np.repeat(norm_g.reshape(L, 6, KC, P).transpose(3, 0, 1, 2)[..., None], 2, -1)
    ab = blocked(ffn_w_in).reshape(L, 2, 2, FC, P, D).transpose(0, 1, 3, 2, 4, 5)
    a["ffn_in"] = ab.reshape(L, 2, 2 * FC, P, D)
    a["ffn_out"] = blocked(ffn_w_out)
    cuts = np.cumsum([D, D, D, D, 256, 256, Q_RANK, KV_RANK, ROPE])
    aq, ak, av, bq, bk, bv, cq, ckv, ckr, gates = np.split(mix_w_in, cuts, axis=-1)
    a["qk_a"] = np.concatenate([blocked(aq), blocked(ak)], 1)
    a["v_a"] = by_rows(av, 512, 2)
    bq = bq.reshape(L, D, 2, 2, 4, 64).transpose(0, 1, 2, 4, 3, 5).reshape(L, D, D)
    a["qk_b"] = np.concatenate([blocked(bq), blocked(bk)], 1)
    a["v_b"] = by_rows(bv, 256, 4)
    a["c_lat"] = np.concatenate([blocked(cq), blocked(ckv), blocked(np.concatenate([ckr, ckr], -1))], 1)
    uq = mla_w_uq.reshape(L, Q_RANK, 8, 192)
    uq = np.concatenate([uq[..., :128].reshape(L, Q_RANK, D), uq[..., 128:].reshape(L, Q_RANK, 512)], -1)
    a["uq"] = blocked(uq).reshape(L, 6, 2, P, Q_RANK).transpose(0, 1, 3, 2, 4).reshape(L, 6, P, 2 * Q_RANK)
    ukv = mla_w_ukv.reshape(L, KV_RANK, 8, 256)
    uk = blocked(ukv[..., :128].reshape(L, KV_RANK, D))
    a["uk"] = uk.reshape(L, 2, 4, P, KV_RANK).transpose(0, 1, 3, 2, 4).reshape(L, 2, P, 4 * KV_RANK)
    a["uv"] = by_rows(ukv[..., 128:].reshape(L, KV_RANK, D), 512, 2)
    bw = branch_w.reshape(L, 3, D, D)
    win = bw[:, 1].reshape(L, 2, 2, 4, 64, D).transpose(0, 1, 3, 2, 4, 5).reshape(L, D, D)
    bw = np.stack([bw[:, 0], win, bw[:, 2]], 1)
    gates = gates.reshape(L, D, 3, D).transpose(0, 2, 1, 3)
    a["merge"] = np.stack([blocked(gates), blocked(bw)], 3).reshape(L, 3, 2 * KC, P, D)
    a["wo"] = blocked(mix_w_out)
    a["subg"] = diff_subln_g.T
    lat_g = np.concatenate([mla_q_norm_g, mla_kv_norm_g], -1)
    a["lat_g"] = lat_g.reshape(L, QC + KVC, P).transpose(2, 0, 1)
    a["dlam"] = diff_lambda.transpose(2, 0, 1)
    a["sink"] = win_sink.reshape(L, 2, 2, 4).transpose(0, 1, 3, 2).reshape(1, L * 16)

    token = np.arange(S)
    quarter = ROPE // 4
    freq = (1.0 / (np.float32(10000.0) ** (np.arange(quarter, dtype=np.float32) / np.float32(quarter))))
    freq = freq.astype(np.float32)
    row, col = (token // GRID_W).astype(np.float32), (token % GRID_W).astype(np.float32)
    angles = np.concatenate([freq[:, None] * row] * 2 + [freq[:, None] * col] * 2, 0).astype(np.float32)
    sign = np.where(np.arange(ROPE) // quarter % 2 == 0, -1.0, 1.0)[:, None].astype(np.float32)
    a["cos"] = np.concatenate([np.cos(angles)] * 2, 0).astype(np.float32)
    a["sin"] = np.concatenate([np.sin(angles) * sign] * 2, 0).astype(np.float32)
    a["ident"] = np.eye(P, dtype=np.float32)
    i = np.arange(P)
    later, earlier = i[None, :] > i[:, None], i[None, :] < i[:, None]
    a["mask"] = np.where(np.stack([later, earlier], 1), np.float32(NEG), np.float32(0.0)).astype(np.float32)
    return {name: np.ascontiguousarray(t) for name, t in a.items()}


def kernel(**inputs):
    import concourse.bacc as bacc
    from concourse.bass_utils import run_bass_kernel_spmd

    arrays = layout(**{name: np.asarray(t) for name, t in inputs.items()})
    nc = bacc.Bacc("TRN2", target_bir_lowering=False, num_devices=1)
    io = {name: nc.dram_tensor(f"in_{name}", t.shape, F32, kind="ExternalInput").ap()
          for name, t in arrays.items()}
    out = nc.dram_tensor("out", (P, KC, S), F32, kind="ExternalOutput").ap()
    silu_rows = nc.dram_tensor("silu_rows", (1, 2 * D), F32).ap()
    build(nc, io, silu_rows, out)
    r = run_bass_kernel_spmd(nc, [{f"in_{name}": t for name, t in arrays.items()}], core_ids=[0])
    y = r.results[0]["out"]
    return y.transpose(2, 1, 0).reshape(1, S, D)
```

```python
from contextlib import ExitStack

import numpy as np

import concourse.bass as bass
from concourse import mybir

F32 = mybir.dt.float32
F32R = mybir.dt.float32r
ALU = mybir.AluOpType
ACT = mybir.ActivationFunctionType
AX_X = mybir.AxisListType.X

P = 128
D = 1024
KC = D // P
S = 256
T = 512
LAYERS = 2
FFN = 2816
FC = FFN // P
N_MOD = 9
GRID_W = 64
ROPE = 64
EPS = 1e-6
NEG = -1e30
WINDOW = 128
Q_RANK, KV_RANK = 384, 256
QC, KVC = Q_RANK // P, KV_RANK // P
HEAD_SCALE = 64 ** -0.5
MLA_SCALE = (128 + 64) ** -0.5
LN_EXP = "natural_log_exp_and_others"
SILU = "silu_and_others"
SIGMOID = "sigmoid_and_others"

RAW = 4
SPLIT = 2
BANKS = 4
STAT, ADA_BANK = 5, 6
GROUP = 1024
FIRST_ADA = 2
ADA_PAIR = 2
POOL_CHUNKS = (1, 3, 5)
ADA_RING = 2


class Idx:

    def __init__(self, c, step, i):
        self.c, self.step, self.i = c, step, i

    def plus(self, k):
        return Idx(self.c + k, self.step, self.i)

    def val(self, extra=0):
        if isinstance(self.i, int):
            return self.c + self.i * self.step + extra
        return self.i * self.step + (self.c + extra)

    def ring(self, size):
        if isinstance(self.i, int):
            return (self.c + self.i * self.step) % size
        assert self.step % size == 0
        return self.c % size

    def lap(self, size, extra=0):
        if isinstance(self.i, int):
            return (self.c + self.i * self.step) // size + extra
        assert self.step % size == 0
        return self.i * (self.step // size) + (self.c // size + extra)


def wait(eng, sem, value):
    if isinstance(value, int) and value <= 0:
        return
    eng.wait_ge(sem, value)


class Phase:

    def __init__(self, kind, layer, src=None, tokens=None, first=0, iters=0, groups=0, tiles=0, adds=None,
                 sub=None, post=None, pre=None, vectors=(), per_tile=1, dst=None, cols=0, x=None,
                 kpg=0, mode=None, blocks=0, nq=0, r=0):
        self.kind, self.layer, self.src, self.tokens, self.first = kind, layer, src, tokens, first
        self.iters, self.groups, self.tiles, self.adds = iters, groups, tiles, dict(adds or {})
        self.sub, self.post, self.pre, self.vectors = sub, post, pre, vectors
        self.per_tile, self.dst, self.cols, self.x, self.kpg = per_tile, dst, cols, x, kpg
        self.mode, self.blocks, self.nq, self.r = mode, blocks, nq, r
        self.peel_first = self.peel_last = False


def make_plan():
    plan = []

    def add(kind, layer, **kw):
        plan.append(Phase(kind, layer=layer, **kw))

    def norm(layer, post, pre, tokens):
        adds = {"stat": int(bool(post)), "inv": bool(post) + bool(pre)}
        if post:
            adds.update(gated=KC, x=KC - len(POOL_CHUNKS), xp=len(POOL_CHUNKS))
        if pre:
            adds.update(xsq=KC, xsum=KC, scaled=KC, shifted=KC, xhi=KC, xlo=KC)
        add("norm", layer, post=post, pre=pre, tokens=tokens, adds=adds)

    norm(0, None, (0, 0), T)
    vectors = {
        (0, 0): [(0, 2), (0, 3), (0, 4), (0, 5), (0, 6)],
        (0, "v"): [(0, 7)],
        (1, "v"): [],
        (0, 2): [(0, 8), (1, 0), (1, 1), (1, 2)],
        (1, 0): [(1, 3), (1, 4), (1, 5), (1, 6), (1, 7)],
        (1, 2): [(1, 8)],
    }
    for layer in range(LAYERS):
        last = layer == LAYERS - 1
        nq = S if last else T

        def ffn(sub, tokens):
            made = vectors[(layer, sub)]
            add("ffn_in", layer, sub=sub, tokens=tokens, iters=FC // 2, groups=4, tiles=4, vectors=made,
                adds={"ghi": FC, "glo": FC, "made": sum(m % 3 > 0 for _, m in made)})
            add("y", layer, src="ffn_out", sub=sub, tokens=tokens, iters=KC // 4, groups=12, tiles=4,
                per_tile=3, adds={"sq": KC, "acc": KC})

        ffn(0, T)
        norm(layer, (layer, 0), (layer, 1), T)
        if last:
            add("rope", layer, src="qk_a", dst="q", first=0, tokens=nq, iters=2, groups=4, tiles=4,
                adds={"rope": 8})
            add("rope", layer, src="qk_a", dst="k", first=8, tokens=T, iters=2, groups=4, tiles=4,
                adds={"rope": 8})
        else:
            add("rope", layer, src="qk_a", dst="qk", first=0, tokens=T, iters=4, groups=4, tiles=4,
                adds={"rope": 16})
        made = vectors[(layer, "v")]
        add("v", layer, src="v_a", cols=512, x="x", kpg=2, iters=2, groups=4, tiles=4, vectors=made,
            adds={"made": sum(m % 3 > 0 for _, m in made)})
        add("attn", layer, mode="a", blocks=8, nq=nq)
        add("merge", layer, r=0, tokens=nq, iters=4, groups=4, tiles=4)
        add("rope", layer, src="qk_b", dst="q", first=0, tokens=nq, iters=2, groups=4, tiles=4,
            adds={"rope": 8})
        add("rope", layer, src="qk_b", dst="k", first=8, tokens=T, iters=1, groups=2, tiles=2,
            adds={"rope": 2})
        add("v", layer, src="v_b", cols=256, x="x", kpg=4, iters=1, groups=2, tiles=4)
        add("attn", layer, mode="b", blocks=8, nq=nq)
        add("merge", layer, r=1, tokens=nq, iters=4, groups=4, tiles=4, adds={"m": KC})
        add("plain", layer, src="c_lat", dst="lat", tokens=T, iters=1, groups=QC + KVC, tiles=QC + KVC)
        add("rope", layer, src="c_lat", dst="kr", first=QC + KVC, tokens=T, iters=1, groups=1, tiles=1,
            adds={"rope": 1})
        add("latnorm", layer, adds={"lsq": QC + KVC, "stat": QC + KVC, "inv": 2, "lt": QC + KVC,
                                    "lhi": QC + KVC, "llo": QC + KVC})
        add("plain", layer, src="uq", dst="qn", tokens=nq, iters=1, groups=4, tiles=8)
        add("rope", layer, src="uq", dst="qr", first=8, tokens=nq, iters=1, groups=2, tiles=4,
            adds={"rope": 4})
        add("plain", layer, src="uk", dst="kn", tokens=T, iters=1, groups=2, tiles=8)
        add("v", layer, src="uv", cols=512, x="lat", kpg=2, iters=2, groups=1, tiles=4)
        add("attn", layer, mode="c", blocks=4, nq=nq)
        add("merge", layer, r=2, tokens=nq, iters=4, groups=4, tiles=4, adds={"m": KC})
        add("msplit", layer, tokens=nq, adds={"mhi": KC, "mlo": KC})
        add("y", layer, src="wo", sub=1, tokens=nq, iters=2, groups=4, tiles=4, per_tile=1,
            adds={"sq": KC, "acc": KC})
        norm(layer, (layer, 1), (layer, 2), nq)
        ffn(2, nq)
        norm(layer, (layer, 2), None if last else (layer + 1, 0), nq)

    at = {}
    g = n = 0
    for ph in plan:
        ph.g, ph.n, ph.at = g, n, dict(at)
        g += ph.groups * ph.iters
        n += ph.tiles * ph.iters
        if ph.kind == "attn":
            qts = list(range(ph.nq // P))
            ph.units = [(b, qt) for b in range(ph.blocks) for qt in qts]
            ph.per_block = len(qts)
            u = len(ph.units)
            ph.adds = {"score": u, "bias": u, "exp": u, "prob": u, "turned": u, "pt": u, "pv": u,
                       "yhi": ph.blocks, "ylo": ph.blocks}
            if ph.mode == "a":
                ph.adds.update(asq=ph.blocks, stat=ph.blocks, inv=ph.blocks, residue=ph.blocks, ynorm=ph.blocks)
        for k, v in ph.adds.items():
            at[k] = at.get(k, 0) + v
    products = [ph for ph in plan if ph.iters]
    products[0].peel_first = True
    next(ph for ph in products if ph.kind == "rope").peel_first = True
    products[-1].peel_last = True
    return plan, g


def build(nc, io, silu_rows, out):
    plan, all_groups = make_plan()
    lambda_init = [0.8 - 0.6 * float(np.exp(-0.3 * l)) for l in range(LAYERS)]

    with ExitStack() as ctx:
        def sb(name, shape, dt=F32):
            return ctx.enter_context(nc.sbuf_tensor(name, shape, dt))

        x = sb("x", [P, KC, T])
        work = sb("work", [P, KC, T])
        xhi = sb("xhi", [P, KC, T], F32R)
        xlo = sb("xlo", [P, KC, T], F32R)
        raw = sb("raw", [P, RAW, GROUP])
        whi = sb("whi", [P, SPLIT, GROUP], F32R)
        wlo = sb("wlo", [P, SPLIT, GROUP], F32R)
        ada = sb("ada", [P, ADA_RING, D])
        cos = sb("cos", [P, S])
        sin = sb("sin", [P, S])
        ident = sb("ident", [P, P])
        mask = sb("mask", [P, 2, P])
        ones = sb("ones", [P, P])
        inv = sb("inv", [P, T])
        tmp = sb("tmp", [P, 2, T])
        acc = sb("acc", [P, T])
        mods = sb("mods", [P, LAYERS, N_MOD, KC, 2])
        ada_b = sb("ada_b", [P, LAYERS, N_MOD, KC, 2])
        norm_g = sb("norm_g", [P, LAYERS, 6, KC, 2])
        cvec = sb("cvec", [P, KC, 2])
        subg = sb("subg", [P, LAYERS])
        lat_g = sb("lat_g", [P, LAYERS, QC + KVC])
        dlam = sb("dlam", [64, LAYERS, 4])
        dprod = sb("dprod", [64, LAYERS, 2])
        elam = sb("elam", [P, LAYERS, 2])
        lam = sb("lam", [P, LAYERS])
        nsink = sb("nsink", [P, LAYERS, 16])
        sink = sb("sink", [P, LAYERS, 16])
        eps = sb("eps", [P, 1])
        mx = sb("mx", [P, 2, 2])
        nb = sb("nb", [P, 2, 2])
        sd = sb("sd", [P, 2, 2])
        se = sb("se", [P, 2, 2])
        sm = sb("sm", [P, 2, 2])
        rc = sb("rc", [P, 2, 2])

        arena_bytes = 2 * FC * T * 4
        arena_at = (nc.sbuf_usable_end - arena_bytes) // 32 * 32
        assert nc.sbuf_base <= arena_at, (nc.sbuf_base, arena_at)

        def at(name, shape, offset, dt=F32):
            assert offset + int(np.prod(shape[1:])) * 4 <= arena_bytes, name
            return nc.alloc_sbuf_tensor_at(name, shape, dt, offset=arena_at + offset)

        KB = 1024
        shift_w = at("shift_w", [P, KC, D], 0)
        scale_w = at("scale_w", [P, KC, D], 32 * KB)
        ghi = at("ghi", [P, FC, T], 0, F32R)
        glo = at("glo", [P, FC, T], FC * T * 4, F32R)
        qk = at("qk", [P, 16, T], 0)
        q = qk[:, 0:8, :]
        k = qk[:, 8:16, :]
        yhi = at("yhi", [P, 8, T], 0, F32R)
        v = at("v", [P, 4, D], 32 * KB)
        ylo = at("ylo", [P, 8, T], 48 * KB, F32R)
        lat = at("lat", [P, QC + KVC, T], 78 * KB)
        lhi = at("lhi", [P, QC + KVC, T], 48 * KB, F32R)
        llo = at("llo", [P, QC + KVC, T], 58 * KB, F32R)
        qr = at("qr", [P, 4, T], 68 * KB)
        kr = at("kr", [P, T], 76 * KB)
        sub_v = at("sub_v", [P, T], 68 * KB)
        prob = at("prob", [P, 2, 2, T], 78 * KB)

        ps = ctx.enter_context(nc.psum_tensor("ps", [P, 8, 512], F32))

        def sem(name):
            return ctx.enter_context(nc.semaphore(name))

        raw_loaded = [sem(f"raw_loaded{s}") for s in range(RAW)]
        shift_w_loaded = [sem(f"shift_w_loaded{s}") for s in range(KC // ADA_PAIR)]
        scale_w_loaded = [sem(f"scale_w_loaded{s}") for s in range(KC // ADA_PAIR)]
        ada_loaded = [sem(f"ada_loaded{s}") for s in range(ADA_RING)]
        x_loaded = sem("x_loaded")
        c_loaded = sem("c_loaded")
        consts_loaded = sem("consts_loaded")
        consts_made = sem("consts_made")
        silu_c = sem("silu_c")
        silu_rows_made = sem("silu_rows_made")
        silu_rows_stored = sem("silu_rows_stored")
        c_all_loaded = sem("c_all_loaded")
        c_spread = sem("c_spread")
        hi_ready = sem("hi_ready")
        lo_ready = sem("lo_ready")
        group_used = sem("group_used")
        bank_free = [sem(f"bank_free{b}") for b in range(BANKS)]
        first_shift = sem("first_shift")
        ada_dot = sem("ada_dot")
        done = {name: sem(f"{name}_done") for name in (
            "ghi", "glo", "gated", "xp", "xsq", "xsum", "sq", "acc", "stat", "inv", "x", "scaled", "shifted", "xhi", "xlo", "rope", "m", "mhi",
            "mlo", "lsq", "lt", "lhi", "llo", "score", "bias", "exp", "prob", "turned", "pt", "pv",
            "yhi", "ylo", "asq", "ynorm", "ln", "refined", "residue", "made")}
        rope_mul = sem("rope_mul")
        half_residue = sem("half_residue")
        acc_zero = sem("acc_zero")
        lam_sum = sem("lam_sum")
        lam_exp = sem("lam_exp")
        dve_step = sem("dve_step")
        stored = sem("stored")

        block = ctx.enter_context(nc.Block())

        def run(eng, ph, body):
            first = 1 if ph.peel_first else 0
            last = 1 if ph.peel_last else 0
            if ph.iters == 1 or ph.groups % RAW:
                for i in range(ph.iters):
                    body(i)
                return
            for i in range(first):
                body(i)
            if ph.iters - first - last > 1:
                with eng.Fori(first, ph.iters - last) as i:
                    body(i)
            else:
                for i in range(first, ph.iters - last):
                    body(i)
            for i in range(ph.iters - last, ph.iters):
                body(i)

        def base(ph, name):
            return ph.at.get(name, 0)

        def residual(ph, c):
            if c in POOL_CHUNKS:
                return "xp", base(ph, "xp") + POOL_CHUNKS.index(c) + 1
            return "x", base(ph, "x") + c + 1 - sum(p < c for p in POOL_CHUNKS)

        def streams(tokens):
            return range(tokens // S)

        def sl(s):
            return slice(s * S, (s + 1) * S)

        def source(ph, i, j):
            w = io[ph.src or ph.kind][ph.layer]

            def pick(ap, index):
                if isinstance(index, int):
                    return ap[index]
                return ap[bass.ds(index, 1)].rearrange("o p n -> (o p) n")

            if ph.kind == "ffn_in":
                return pick(w[ph.sub // 2], i * 4 + j), GROUP
            if ph.kind == "merge":
                return pick(w[ph.r], i * 4 + j), GROUP
            if ph.src == "ffn_out":
                tile, part = divmod(j, 3)
                n = GROUP if part < 2 else (FC - 16) * P
                return pick(w[ph.sub // 2], i * 4 + tile)[:, part * GROUP:part * GROUP + n], n
            first = 4 if (ph.src, ph.kind) == ("uq", "rope") else ph.first
            n = w.shape[-1]
            return pick(w, i * ph.groups + (first + j)), n

        def last_group(ph, i, j):
            if ph.kind == "v":
                own = ph.groups - 1
            elif ph.src == "ffn_out":
                own = 3 * j + 2
            else:
                own = j * ph.groups // ph.tiles
            return Idx(ph.g + own, ph.groups, i)

        def bank(ph, i, j):
            return Idx(ph.n + j, ph.tiles, i)

        def tiles_before(ph, b):
            return (ph.n - b + BANKS - 1) // BANKS

        def chunk(t, c, tokens):
            if isinstance(c.i, int):
                return t[:, c.val(), 0:tokens]
            return t[:, bass.ds(c.val(), 1), 0:tokens].rearrange("p o n -> p (o n)")

        def split_ahead(split, ph, i, j):
            per_group = ph.tiles // ph.groups
            if j % per_group == 0:
                split(Idx(ph.g + j // per_group + 1, ph.groups, i))

        def rope_dst(ph, i, j, cols):
            if ph.dst == "kr":
                return kr[:, cols]
            t = {"q": q, "k": k, "qk": qk, "qr": qr}[ph.dst]
            if isinstance(i, int):
                return t[:, i * ph.tiles + j, cols]
            return t[:, bass.ds(i * ph.tiles + j, 1), cols].rearrange("p o n -> p (o n)")

        ada_order = [lm for ph in plan for lm in ph.vectors]
        assert ada_order == [divmod(n, N_MOD) for n in range(FIRST_ADA, LAYERS * N_MOD)]

        c_all = work[:, 0:4, :].rearrange("p c n -> p (c n)")
        products = work[:, 4:8, :].rearrange("p (s c) n -> p s (c n)", s=2)
        mods_flat = mods[:, :, :, :, :].rearrange("p l m c s -> p (l m c s)")
        ada_b_flat = ada_b[:, :, :, :, :].rearrange("p l m c s -> p (l m c s)")

        def scale_or_gate(eng, l, m):
            sub, part = divmod(m, 3)
            g = norm_g[:, l, 2 * sub + part - 1, :, :]
            factor, op = (1.0, ALU.add) if part == 1 else (1.0 if sub == 1 else 0.5, ALU.mult)
            dst = mods[:, l, m, :, :]
            return eng.scalar_tensor_tensor(dst, dst, factor, g, op, ALU.mult)

        def newton_start(dve, ln, bank_, tokens, width, v):
            dve.wait_ge(done["ln"], ln)
            dve.tensor_scalar(v, ps[:, bank_, 0:tokens], -0.5 / width, -0.5 * EPS, ALU.mult, ALU.add)\
               .then_inc(done["refined"], 1)

        def newton_end(step, dve, dst, v):
            step(dve.scalar_tensor_tensor(dst, v, 1.5, dst, ALU.add, ALU.mult))

        def newton(step, dve, count, bank_, width, dst, v):
            newton_start(dve, count, bank_, dst.shape[-1], width, v)
            dve.wait_ge(done["refined"], count)
            dve.wait_ge(done["inv"], count)
            step(dve.tensor_tensor(v, v, dst, ALU.mult))
            step(dve.tensor_tensor(v, v, dst, ALU.mult))
            newton_end(step, dve, dst, v)

        def last_unit(ph, b):
            return (b + 1) * ph.per_block - 1

        def keys(qt):
            return 0 if qt < S // P else S // P

        def turns(ph):
            return 1 if ph.mode == "a" else 2

        def turned(ph, u, n):
            if ph.mode == "a":
                return tmp[:, u % 2, :]
            return (acc, inv)[n][:, :] if u % 2 else tmp[:, n, :]

        def outputs(ph, b):
            if ph.mode == "b":
                return [(b, ps[:, 6 + b % 2, 0:ph.nq])]
            return [(2 * b + n, ps[:, 6 + n, 0:ph.nq]) for n in range(2)]

        def act_attention(act, ph, inverse):
            units, nq = ph.units, ph.nq
            scale = MLA_SCALE if ph.mode == "c" else HEAD_SCALE

            def exp(u):
                e, nk = u % 2, T - keys(units[u][1]) * P
                act.wait_ge(done["bias"], base(ph, "bias") + u + 1)
                wait(act, done["turned"], base(ph, "turned") + u - 1 if u >= 2 else 0)
                if ph.mode == "b":
                    act.activation(se[:, e, :], sd[:, e, :], ACT.Exp)
                for n in range(2):
                    last = act.activation(prob[:, e, n, 0:nk], ps[:, 2 * e + n, 0:nk], ACT.Exp,
                                          bias=nb[:, e, n:n + 1], scale=scale, accum_out=sm[:, e, n:n + 1])
                last.then_inc(done["exp"], 1)

            def turned_copy(u):
                nk = T - keys(units[u][1]) * P
                act.wait_ge(done["turned"], base(ph, "turned") + u + 1)
                wait(act, done["pv"], base(ph, "pv") + u - 1 if u >= 2 else 0)
                for n in range(turns(ph)):
                    last = act.activation(turned(ph, u, n)[:, 0:nk], ps[:, 4 + n, 0:nk], ACT.Copy)
                last.then_inc(done["pt"], 1)

            def output_high(s):
                for b in range(ph.blocks):
                    if s == last_unit(ph, b) + 2:
                        act.wait_ge(done["pv"], base(ph, "pv") + last_unit(ph, b) + 1)
                        for c, src in outputs(ph, b):
                            last = act.activation(yhi[:, c, 0:nq], src, ACT.Copy)
                        last.then_inc(done["yhi"], 1)

            exp(0)
            exp(1)
            for s in range(len(units) + 4):
                if ph.mode == "c":
                    output_high(s)
                if s < len(units):
                    turned_copy(s)
                for b in range(ph.blocks):
                    if ph.mode == "a" and s == last_unit(ph, b) + 4:
                        act.wait_ge(done["ynorm"], base(ph, "ynorm") + b + 1)
                        act.activation(yhi[:, b, 0:nq], acc[:, 0:nq], ACT.Copy).then_inc(done["yhi"], 1)
                    if ph.mode == "a" and s == last_unit(ph, b) + 2:
                        act.wait_ge(done["pv"], base(ph, "pv") + last_unit(ph, b) + 1)
                        wait(act, done["ylo"], base(ph, "ylo") + b)
                        act.activation(acc[:, 0:nq], ps[:, 6 + b % 2, 0:nq], ACT.Square).then_inc(done["asq"], 1)
                    if ph.mode == "a" and s == last_unit(ph, b) + 3:
                        inverse(inv[:, 0:nq], STAT, nq, P, base(ph, "stat") + b + 1)
                if s + 2 < len(units):
                    exp(s + 2)
                if ph.mode == "b":
                    output_high(s)

        def dve_attention(dve, ph, step):
            units, nq, l = ph.units, ph.nq, ph.layer
            scale = MLA_SCALE if ph.mode == "c" else HEAD_SCALE

            def biases(u):
                b, qt = units[u]
                e, nk = u % 2, T - keys(qt) * P
                dve.wait_ge(done["score"], base(ph, "score") + u + 1)
                step(dve.tensor_reduce(mx[:, e, :], ps[:, 2 * e:2 * e + 2, 0:nk], AX_X, ALU.max, negate=True))
                if ph.mode == "b":
                    negs = nsink[:, l, 2 * b:2 * b + 2]
                    step(dve.scalar_tensor_tensor(nb[:, e, :], mx[:, e, :], scale, negs, ALU.mult, ALU.min))
                    dve.tensor_tensor(sd[:, e, :], sink[:, l, 2 * b:2 * b + 2], nb[:, e, :], ALU.add)\
                       .then_inc(done["bias"], 1)
                else:
                    dve.tensor_scalar(nb[:, e, :], mx[:, e, :], scale, None, ALU.mult).then_inc(done["bias"], 1)

            def normalize(u):
                e, nk = u % 2, T - keys(units[u][1]) * P
                dve.wait_ge(done["exp"], base(ph, "exp") + u + 1)
                if ph.mode == "b":
                    step(dve.tensor_tensor(sm[:, e, :], sm[:, e, :], se[:, e, :], ALU.add))
                step(dve.reciprocal(rc[:, e, :], sm[:, e, :]))
                p0, p1 = prob[:, e, 0, 0:nk], prob[:, e, 1, 0:nk]
                if ph.mode == "a":
                    step(dve.tensor_scalar(p1, p1, rc[:, e, 1:2], lam[:, l:l + 1], ALU.mult, ALU.mult))
                    dve.scalar_tensor_tensor(p0, p0, rc[:, e, 0:1], p1, ALU.mult, ALU.subtract)\
                       .then_inc(done["prob"], 1)
                else:
                    dve.tensor_scalar(p0, p0, rc[:, e, 0:1], None, ALU.mult)
                    dve.tensor_scalar(p1, p1, rc[:, e, 1:2], None, ALU.mult).then_inc(done["prob"], 1)

            def output_low(s):
                for b in range(ph.blocks):
                    if s == last_unit(ph, b) + 2:
                        dve.wait_ge(done["yhi"], base(ph, "yhi") + b + 1)
                        for c, src in outputs(ph, b):
                            last = dve.tensor_tensor(ylo[:, c, 0:nq], src, yhi[:, c, 0:nq].bitcast(F32),
                                                     ALU.subtract)
                        last.then_inc(done["ylo"], 1)

            biases(0)
            biases(1)
            normalize(0)
            for s in range(len(units) + 4):
                if ph.mode == "c":
                    output_low(s)
                if s + 1 < len(units):
                    normalize(s + 1)
                ended = [b for b in range(ph.blocks) if ph.mode == "a" and s == last_unit(ph, b) + 3]
                dst, var = inv[:, 0:nq], sub_v[:, 0:nq]
                for b in ended:
                    newton_start(dve, base(ph, "inv") + b + 1, STAT, nq, P, var)
                if s + 2 < len(units):
                    biases(s + 2)
                if ph.mode == "b":
                    output_low(s)
                for b in ended:
                    dve.wait_ge(done["residue"], base(ph, "residue") + b + 1)
                    newton_end(step, dve, dst, var)
                    dve.scalar_tensor_tensor(acc[:, 0:nq], ps[:, 6 + b % 2, 0:nq], subg[:, l:l + 1],
                                             inv[:, 0:nq], ALU.mult, ALU.mult).then_inc(done["ynorm"], 1)

        def pe_attention(pe, ph):
            units = ph.units
            for b in range(BANKS):
                pe.wait_ge(bank_free[b], tiles_before(ph, b))
            pe.wait_ge(done["rope"], base(ph, "rope"))
            wait(pe, done["refined"], base(ph, "inv"))
            wait(pe, done["pt"], base(ph, "pt"))

            def scores(u):
                b, qt = units[u]
                e, kc = u % 2, keys(units[u][1])
                nk = T - kc * P
                cols, ks = slice(qt * P, (qt + 1) * P), slice(kc * P, T)
                wait(pe, done["exp"], base(ph, "exp") + u - 1 if u >= 2 else 0)
                for n in range(2):
                    o = ps[:, 2 * e + n, 0:nk]
                    half = slice(64 * n, 64 * n + 64)
                    if ph.mode == "c":
                        pe.matmul(o, q[:, 2 * b + n, cols], k[:, 2 * b + n, ks], start=True, stop=False)
                        last = pe.matmul(o, qr[half, b, cols], kr[half, ks], start=False, stop=True)
                    else:
                        kb = b if ph.mode == "a" else b // 4
                        masked = ph.mode == "b" and kc == 0
                        last = pe.matmul(o, q[half, b, cols], k[half, kb, ks], start=True, stop=not masked)
                        if masked:
                            other = (1 - qt) * P
                            last = pe.matmul(ps[:, 2 * e + n, other:other + P], ident[:, :], mask[:, qt, :],
                                             start=False, stop=True)
                last.then_inc(done["score"], 1)

            def turn(u):
                e, nk = u % 2, T - keys(units[u][1]) * P
                pe.wait_ge(done["prob"], base(ph, "prob") + u + 1)
                wait(pe, done["pt"], base(ph, "pt") + u if u else 0)
                for n in range(turns(ph)):
                    for c in range(nk // P):
                        cs = slice(c * P, (c + 1) * P)
                        last = pe.transpose(ps[:, 4 + n, cs], prob[:, e, n, cs], ident[:, :])
                last.then_inc(done["turned"], 1)

            def weighted(u):
                b, qt = units[u]
                kc0 = keys(qt)
                pe.wait_ge(done["pt"], base(ph, "pt") + u + 1)
                if qt == 0:
                    if ph.mode == "a":
                        wait(pe, done["ynorm"], base(ph, "ynorm") + b - 1 if b >= 2 else base(ph, "ynorm"))
                        wait(pe, done["ylo"], base(ph, "ylo") if b < 2 else 0)
                    else:
                        before = b if ph.mode == "c" else b - 1
                        wait(pe, done["ylo"], base(ph, "ylo") + before if before > 0 else base(ph, "ylo"))
                for n in range(turns(ph)):
                    to = 6 + (n if ph.mode == "c" else b % 2)
                    rows = slice(64 * n, 64 * n + 64) if ph.mode == "b" else slice(0, P)
                    first = {"a": b, "b": b // 4, "c": 2 * b + n}[ph.mode] * P + rows.start
                    vs = slice(first, first + rows.stop - rows.start)
                    for kc in range(kc0, T // P):
                        last = pe.matmul(ps[rows, to, qt * P:(qt + 1) * P], v[:, kc, vs],
                                         turned(ph, u, n)[:, (kc - kc0) * P:(kc - kc0 + 1) * P],
                                         start=kc == kc0, stop=kc == T // P - 1)
                last.then_inc(done["pv"], 1)

            scores(0)
            scores(1)
            for s in range(len(units) + 3):
                if s < len(units):
                    turn(s)
                if s + 2 < len(units):
                    scores(s + 2)
                if 1 <= s <= len(units):
                    weighted(s - 1)
                for b in range(ph.blocks):
                    if ph.mode == "a" and s == last_unit(ph, b) + 2:
                        pe.wait_ge(done["asq"], base(ph, "asq") + b + 1)
                        wait(pe, done["refined"], base(ph, "inv") + b)
                        pe.matmul(ps[:, STAT, 0:ph.nq], ones[:, :], acc[:, 0:ph.nq], start=True, stop=True)\
                          .then_inc(done["stat"], 1)

        def pool_attention(pool, ph):
            dst, v = inv[:, 0:ph.nq], sub_v[:, 0:ph.nq]
            for b in range(ph.blocks):
                pool.wait_ge(done["refined"], base(ph, "inv") + b + 1)
                pool.wait_ge(done["inv"], base(ph, "inv") + b + 1)
                pool.tensor_tensor(v, v, dst, ALU.mult).then_inc(half_residue, 1)
                pool.wait_ge(half_residue, base(ph, "residue") + b + 1)
                pool.tensor_tensor(v, v, dst, ALU.mult).then_inc(done["residue"], 1)
                pool.wait_ge(done["yhi"], base(ph, "yhi") + b + 1)
                pool.tensor_tensor(ylo[:, b, 0:ph.nq], acc[:, 0:ph.nq], yhi[:, b, 0:ph.nq].bitcast(F32),
                                   ALU.subtract).then_inc(done["ylo"], 1)

        @block.sync
        def _(sp):
            sp.dma_start(cvec[:, :, :], io["cvec"]).then_inc(c_loaded, 16)
            sp.dma_start(c_all[:, :], io["c_rows"].to_broadcast([P, 2 * D])).then_inc(c_all_loaded, 16)

            def load_shift_w(pair):
                some = slice(pair * ADA_PAIR, (pair + 1) * ADA_PAIR)
                sp.dma_start(shift_w[:, some, :], io["shift_w"][pair]).then_inc(shift_w_loaded[pair], 16)

            def load_scale_w(pair):
                some = slice(pair * ADA_PAIR, (pair + 1) * ADA_PAIR)
                sp.dma_start(scale_w[:, some, :], io["scale_w"][pair]).then_inc(scale_w_loaded[pair], 16)

            load_shift_w(0)
            load_scale_w(0)
            small = [(ada_b, "ada_b"), (norm_g, "norm_g"), (dlam, "dlam"), (subg, "subg"), (lat_g, "lat_g"),
                     (cos, "cos"), (sin, "sin"), (ident, "ident"), (mask, "mask")]
            for dst, name in small:
                sp.dma_start(dst[tuple([slice(None)] * len(dst.shape))], io[name]).then_inc(consts_loaded, 16)
            sp.dma_start(sink[:, :, :].rearrange("p l n -> p (l n)"),
                         io["sink"].to_broadcast([P, LAYERS * 16])).then_inc(consts_loaded, 16)
            load_shift_w(1)
            sp.dma_start(x[:, :, :], io["x"]).then_inc(x_loaded, 16)
            load_scale_w(1)
            for pair in range(2, KC // ADA_PAIR):
                load_shift_w(pair)
                load_scale_w(pair)
            sp.wait_ge(silu_rows_made, 1)
            sp.dma_start(silu_rows, c_all[0:1, :]).then_inc(silu_rows_stored, 16)

            def group_loads(ph, i):
                for j in range(ph.groups):
                    g = Idx(ph.g + j, ph.groups, i)
                    wait(sp, lo_ready, g.val(1 - RAW))
                    src, n = source(ph, i, j)
                    sp.dma_start(raw[:, g.ring(RAW), 0:n], src).then_inc(raw_loaded[g.ring(RAW)], 16)

            for ph in plan:
                if ph.iters:
                    run(sp, ph, lambda i, ph=ph: group_loads(ph, i))
            for c in range(KC):
                name, count = residual(plan[-1], c)
                sp.wait_ge(done[name], count)
            sp.dma_start(out, x[:, :, 0:S]).then_inc(stored, 16)
            sp.wait_ge(stored, 16)

        @block.gpsimd
        def _(pool):
            def add_square(n, number, tokens):
                pool.wait_ge(done["sq"], n.val(1))
                wait(pool, done["acc"], n.val())
                pool.tensor_tensor(acc[:, 0:tokens], acc[:, 0:tokens], tmp[:, number, 0:tokens], ALU.add)\
                    .then_inc(done["acc"], 1)

            def load_ada(block):
                index = block.val()
                src = io["ada_rows"][index] if isinstance(index, int) else \
                    io["ada_rows"][bass.ds(index, 1)].rearrange("o p n -> (o p) n")
                slot = block.ring(ADA_RING)
                pool.dma_start(ada[:, slot, :], src).then_inc(ada_loaded[slot], 16)

            def feed_modulation_vectors(ph):
                pool.wait_ge(done["xlo"], base(ph, "xlo"))
                pool.wait_ge(silu_rows_stored, 16)
                pool.dma_start(c_all[:, :], silu_rows.to_broadcast([P, 2 * D])).then_inc(c_spread, 16)
                first = ada_order.index(ph.vectors[0]) * KC

                def body(i):
                    for j in range(ADA_RING):
                        block = Idx(first + j, ADA_RING, i)
                        pool.wait_ge(ada_dot, Idx(2 * (first + j + 1), 2 * ADA_RING, i).val())
                        load_ada(block.plus(ADA_RING))

                pairs = len(ph.vectors) * KC // ADA_RING
                final = ph.vectors[-1] == ada_order[-1]
                with pool.Fori(0, pairs - final) as i:
                    body(i)

            for j in range(ADA_RING):
                load_ada(Idx(j, 0, 0))
            zeros = 0
            for ph in plan:
                if ph.vectors:
                    feed_modulation_vectors(ph)
                if ph.kind == "norm" and ph.post:
                    for n, c in enumerate(POOL_CHUNKS):
                        pool.wait_ge(done["gated"], base(ph, "gated") + c + 1)
                        pool.tensor_tensor(x[:, c, 0:ph.tokens], x[:, c, 0:ph.tokens], work[:, c, 0:ph.tokens],
                                           ALU.add).then_inc(done["xp"], 1)
                if ph.kind == "y":
                    pool.wait_ge(done["stat"], base(ph, "stat"))
                    if "ylo" in ph.at:
                        pool.wait_ge(done["ylo"], base(ph, "ylo"))
                    pool.memset(acc[:, :], 0.0).then_inc(acc_zero, 1)
                    zeros += 1
                    pool.wait_ge(acc_zero, zeros)

                    def body(i, ph=ph):
                        for j in range(ph.tiles):
                            add_square(Idx(base(ph, "sq") + j, ph.tiles, i), j % 2, ph.tokens)

                    run(pool, ph, body)
                if ph.kind == "attn" and ph.mode == "a":
                    pool_attention(pool, ph)
                if ph.kind == "rope":
                    def body(i, ph=ph):
                        for j in range(ph.tiles):
                            n = Idx(ph.n + j, ph.tiles, i)
                            r = Idx(base(ph, "rope") + j, ph.tiles, i)
                            pool.wait_ge(bank_free[n.ring(BANKS)], n.lap(BANKS, 1))
                            wait(pool, done["rope"], r.val(-1))
                            pool.tensor_tensor(acc[:, r.ring(2) * S:(r.ring(2) + 1) * S],
                                               tmp[:, r.ring(2), 0:S], cos[:, :], ALU.mult).then_inc(rope_mul, 1)

                    if base(ph, "rope") == 0:
                        pool.wait_ge(consts_loaded, 160)
                    run(pool, ph, body)

        @block.scalar
        def _(act):
            steps = 0
            table = None

            def use_table(name):
                nonlocal table
                if table != name:
                    act.preload_act_table_set(name)
                    table = name

            def split_hi(g):
                if isinstance(g.i, int) and g.val() >= all_groups:
                    return
                act.wait_ge(raw_loaded[g.ring(RAW)], g.lap(RAW, 1) * 16)
                wait(act, group_used, g.val(1 - SPLIT))
                act.activation(whi[:, g.ring(SPLIT), :], raw[:, g.ring(RAW), :], ACT.Copy).then_inc(hi_ready, 1)

            def inverse(dst, bank, tokens, width, stat, name="stat"):
                nonlocal steps
                act.wait_ge(done[name], stat)
                act.activation(dst, ps[:, bank, 0:tokens], ACT.Ln, bias=eps[:, 0:1], scale=1.0 / width)\
                   .then_inc(done["ln"], 1)
                steps += 1
                act.wait_ge(done["ln"], steps)
                act.activation(dst, dst, ACT.Exp, scale=-0.5).then_inc(done["inv"], 1)

            def square(src, number, tokens, n):
                wait(act, done["acc"], n.val(-1))
                act.activation(tmp[:, number, 0:tokens], src, ACT.Square).then_inc(done["sq"], 1)

            use_table(SILU)
            act.wait_ge(c_loaded, 16)
            act.activation(cvec[:, :, :], cvec[:, :, :], ACT.Silu).then_inc(silu_c, 1)
            act.wait_ge(c_all_loaded, 16)
            act.activation(c_all[:, :], c_all[:, :], ACT.Silu).then_inc(silu_rows_made, 1)
            use_table(LN_EXP)
            act.wait_ge(consts_made, 2)

            for ph in plan:
                tk = ph.tokens
                if ph.kind == "norm":
                    if ph.post:
                        inverse(inv[:, 0:tk], STAT, tk, D, base(ph, "stat") + 1)
                    if ph.pre:
                        for c in range(KC):
                            if ph.post:
                                name, count = residual(ph, c)
                                act.wait_ge(done[name], count)
                            elif c == 0:
                                act.wait_ge(x_loaded, 16)
                            if c < 2:
                                wait(act, done["acc"], base(ph, "acc"))
                            else:
                                act.wait_ge(done["xsum"], base(ph, "xsum") + c - 1)
                            act.activation(tmp[:, c % 2, 0:tk], x[:, c, 0:tk], ACT.Square)\
                               .then_inc(done["xsq"], 1)
                        if not ph.post:
                            split_hi(Idx(0, 0, 0))
                        inverse(inv[:, 0:tk], STAT, tk, D, base(ph, "xsum") + KC, "xsum")
                        l, sub = ph.pre

                        def shifted(c):
                            act.wait_ge(done["scaled"], base(ph, "scaled") + c + 1)
                            for s in streams(tk):
                                last = act.activation(work[:, c, sl(s)], work[:, c, sl(s)], ACT.Identity,
                                                      scale=mods[:, l, 3 * sub + 1, c, s:s + 1],
                                                      bias=mods[:, l, 3 * sub, c, s:s + 1])
                            last.then_inc(done["shifted"], 1)

                        shifted(0)
                        for c in range(KC):
                            if c + 1 < KC:
                                shifted(c + 1)
                            act.wait_ge(done["shifted"], base(ph, "shifted") + c + 1)
                            act.activation(xhi[:, c, 0:tk], work[:, c, 0:tk], ACT.Copy).then_inc(done["xhi"], 1)
                    if not ph.post:
                        act.wait_ge(lam_sum, 1)
                        act.activation(elam[:, :, :], ps[:, STAT, 0:2 * LAYERS].rearrange("p (l n) -> p l n", n=2),
                                       ACT.Exp).then_inc(lam_exp, 1)
                elif ph.kind == "ffn_in":
                    use_table(SILU)

                    def body(i, ph=ph, tk=tk):
                        for j in range(2):
                            g = Idx(ph.g + 2 * j, ph.groups, i)
                            n = Idx(ph.n + 2 * j, ph.tiles, i)
                            p = Idx(base(ph, "ghi") + j, 2, i)
                            split_hi(g.plus(1))
                            split_hi(g.plus(2))
                            a, b = n, n.plus(1)
                            act.wait_ge(group_used, last_group(ph, i, 2 * j).val(1))
                            act.activation(tmp[:, 0, 0:tk], ps[:, a.ring(BANKS), 0:tk], ACT.Silu)\
                               .then_inc(bank_free[a.ring(BANKS)], 1)
                            act.wait_ge(bank_free[b.ring(BANKS)], b.lap(BANKS, 1))
                            act.activation(chunk(ghi, Idx(j, 2, i), tk), tmp[:, 1, 0:tk], ACT.Copy)\
                               .then_inc(done["ghi"], 1)

                    run(act, ph, body)
                elif ph.kind == "y":
                    use_table(LN_EXP)
                    if ph.src == "ffn_out":
                        act.wait_ge(done["glo"], base(ph, "glo"))
                        act.wait_ge(done["made"], base(ph, "made"))

                    def body(i, ph=ph, tk=tk):
                        for j in range(ph.tiles):
                            g = Idx(ph.g + ph.per_tile * j, ph.groups, i)
                            n = Idx(ph.n + j, ph.tiles, i)
                            for t in range(ph.per_tile):
                                split_hi(g.plus(1 + t))
                            act.wait_ge(group_used, last_group(ph, i, j).val(1))
                            square(ps[:, n.ring(BANKS), 0:tk], j % 2, tk,
                                   Idx(base(ph, "sq") + j, ph.tiles, i))
                            c = i * ph.tiles + j
                            for s in streams(tk):
                                last = act.activation(work[:, c, sl(s)], ps[:, n.ring(BANKS), sl(s)], ACT.Identity,
                                                      scale=mods[:, ph.layer, 3 * ph.sub + 2, c, s:s + 1])
                            last.then_inc(bank_free[n.ring(BANKS)], 1)

                    for i in range(ph.iters):
                        body(i)
                elif ph.kind == "rope":
                    for b in range(BANKS):
                        act.wait_ge(bank_free[b], tiles_before(ph, b))
                    wait(act, done["m"], base(ph, "m"))

                    def body(i, ph=ph, tk=tk):
                        for j in range(ph.tiles):
                            split_ahead(split_hi, ph, i, j)
                            n = Idx(ph.n + j, ph.tiles, i)
                            r = Idx(base(ph, "rope") + j, ph.tiles, i)
                            act.wait_ge(group_used, last_group(ph, i, j).val(1))
                            wait(act, done["rope"], r.val(-1))
                            last = act.activation(tmp[:, r.ring(2), 0:S], ps[:, n.ring(BANKS), 0:S], ACT.Copy)
                            if tk == T:
                                last = act.activation(rope_dst(ph, i, j, slice(S, T)),
                                                      ps[:, n.ring(BANKS), S:T], ACT.Copy)
                            last.then_inc(bank_free[n.ring(BANKS)], 1)

                    run(act, ph, body)
                elif ph.kind == "plain":
                    i = 0
                    for j in range(ph.tiles):
                        split_ahead(split_hi, ph, i, j)
                        n = bank(ph, i, j)
                        act.wait_ge(group_used, last_group(ph, i, j).val(1))
                        dst = {"lat": lat, "qn": q, "kn": k}[ph.dst]
                        act.activation(dst[:, j, 0:tk], ps[:, n.ring(BANKS), 0:tk], ACT.Copy)\
                           .then_inc(bank_free[n.ring(BANKS)], 1)
                elif ph.kind == "v":
                    def body(i, ph=ph):
                        for j in range(ph.groups):
                            split_hi(Idx(ph.g + j + 1, ph.groups, i))
                        for t in range(ph.tiles):
                            n = bank(ph, i, t)
                            act.wait_ge(group_used, last_group(ph, i, t).val(1))
                            col = i * ph.cols
                            dst = v[:, t, col:col + ph.cols] if isinstance(i, int) else \
                                v[:, t, bass.ds(col, ph.cols)]
                            act.activation(dst, ps[:, n.ring(BANKS), 0:ph.cols], ACT.Copy)\
                               .then_inc(bank_free[n.ring(BANKS)], 1)

                    run(act, ph, body)
                elif ph.kind == "merge":
                    use_table(SIGMOID)

                    def body(i, ph=ph, tk=tk):
                        for j in range(2):
                            g = Idx(ph.g + 2 * j, ph.groups, i)
                            gate = Idx(ph.n + 2 * j, ph.tiles, i)
                            split_hi(g.plus(1))
                            split_hi(g.plus(2))
                            act.wait_ge(group_used, last_group(ph, i, 2 * j).val(1))
                            before = gate.plus(-1)
                            if j or not (isinstance(i, int) and i == 0):
                                act.wait_ge(bank_free[before.ring(BANKS)], before.lap(BANKS, 1))
                            act.activation(tmp[:, 0, 0:tk], ps[:, gate.ring(BANKS), 0:tk], ACT.Sigmoid)\
                               .then_inc(bank_free[gate.ring(BANKS)], 1)

                    run(act, ph, body)
                elif ph.kind == "msplit":
                    for c in range(KC):
                        act.wait_ge(done["m"], base(ph, "m") - KC + c + 1)
                        if c == 0:
                            act.wait_ge(group_used, ph.g)
                        act.activation(yhi[:, c, 0:tk], work[:, c, 0:tk], ACT.Copy).then_inc(done["mhi"], 1)
                elif ph.kind == "latnorm":
                    use_table(LN_EXP)
                    for c in range(QC + KVC):
                        if c == 0:
                            act.wait_ge(done["rope"], base(ph, "rope"))
                        if c >= 2:
                            act.wait_ge(done["stat"], base(ph, "stat") + c - 1)
                        act.activation(tmp[:, c % 2, :], lat[:, c, :], ACT.Square).then_inc(done["lsq"], 1)
                    inverse(inv[:, :], 4, T, Q_RANK, base(ph, "stat") + QC)
                    inverse(acc[:, :], 5, T, KV_RANK, base(ph, "stat") + QC + KVC)
                    for c in range(QC + KVC):
                        act.wait_ge(done["lt"], base(ph, "lt") + c + 1)
                        act.activation(lhi[:, c, :], lat[:, c, :], ACT.Copy).then_inc(done["lhi"], 1)
                elif ph.kind == "attn":
                    use_table(LN_EXP)
                    act_attention(act, ph, inverse)

        @block.vector
        def _(dve):
            steps = 0

            def split_lo(g):
                if isinstance(g.i, int) and g.val() >= all_groups:
                    return
                dve.wait_ge(hi_ready, g.val(1))
                dve.tensor_tensor(wlo[:, g.ring(SPLIT), :], raw[:, g.ring(RAW), :],
                                  whi[:, g.ring(SPLIT), :].bitcast(F32), ALU.subtract).then_inc(lo_ready, 1)

            def step(ins):
                nonlocal steps
                ins.then_inc(dve_step, 1)
                steps += 1
                dve.wait_ge(dve_step, steps)

            def first_modulations():
                dve.wait_ge(silu_rows_made, 1)
                for block in range(KC):
                    if block % ADA_PAIR == 0:
                        dve.wait_ge(scale_w_loaded[block // ADA_PAIR], 16)
                    for s in range(2):
                        step(dve.scalar_tensor_tensor(products[:, s, :], scale_w[:, block, :], 1.0,
                                                      c_all[:, s * D:(s + 1) * D], ALU.mult, ALU.mult,
                                                      accum_out=mods[:, 0, 1, block, s:s + 1]))
                dve.wait_ge(consts_loaded, 160)
                step(dve.tensor_tensor(mods[:, 0, 1, :, :], mods[:, 0, 1, :, :], ada_b[:, 0, 1, :, :], ALU.add))
                step(scale_or_gate(dve, 0, 1))
                dve.wait_ge(first_shift, 2)
                src = ps[:, ADA_BANK, 0:2 * KC].rearrange("p (c n) -> p c n", n=2)
                step(dve.tensor_tensor(mods[:, 0, 0, :, :], src, ada_b[:, 0, 0, :, :], ALU.add))

            spreads = 0

            def ada_block(block):
                slot = block.ring(ADA_RING)
                dve.wait_ge(c_spread, 16 * spreads)
                dve.wait_ge(ada_loaded[slot], block.lap(ADA_RING, 1) * 16)
                for s in range(2):
                    dot = Idx(2 * block.c + s, 2 * block.step, block.i)
                    wait(dve, ada_dot, dot.val(-1))
                    to = dot.val(2 * FIRST_ADA * KC)
                    to = mods_flat[:, to:to + 1] if isinstance(to, int) else mods_flat[:, bass.ds(to, 1)]
                    dve.scalar_tensor_tensor(products[:, s, :], ada[:, slot, :], 1.0, c_all[:, s * D:(s + 1) * D],
                                             ALU.mult, ALU.mult, accum_out=to).then_inc(ada_dot, 1)

            def blocks_per_body(ph):
                left = len(ph.vectors) * KC - ADA_RING
                counts = []
                for bodies in range(ph.iters - 1, 0, -1):
                    even = left // bodies // ADA_RING * ADA_RING
                    counts.append(min(left, max(even, ADA_RING)))
                    left -= counts[-1]
                assert not left
                return counts + [ADA_RING]

            def finish_vectors(ph):
                first = ada_order.index(ph.vectors[0]) * KC
                last = first + len(ph.vectors) * KC
                dve.wait_ge(ada_dot, 2 * last)
                span = slice(2 * (FIRST_ADA * KC + first), 2 * (FIRST_ADA * KC + last))
                step(dve.tensor_tensor(mods_flat[:, span], mods_flat[:, span], ada_b_flat[:, span], ALU.add))
                for l, m in ph.vectors:
                    if m % 3:
                        scale_or_gate(dve, l, m).then_inc(done["made"], 1)

            dve.memset(ones[:, :], 1.0).then_inc(consts_made, 1)
            dve.memset(eps[:, :], EPS).then_inc(consts_made, 1)
            first_modulations()
            for l in range(LAYERS):
                for n in range(2):
                    dve.tensor_tensor(dprod[:, l, n:n + 1], dlam[:, l, 2 * n:2 * n + 1],
                                      dlam[:, l, 2 * n + 1:2 * n + 2], ALU.mult).then_inc(consts_made, 1)
            for l in range(LAYERS):
                step(dve.tensor_scalar(subg[:, l:l + 1], subg[:, l:l + 1], 1.0 - lambda_init[l], None, ALU.mult))
            step(dve.tensor_scalar(nsink[:, :, :], sink[:, :, :], -1.0, None, ALU.mult))


            for ph in plan:
                tk = ph.tokens
                if ph.kind == "norm":
                    if ph.post:
                        l, sub = ph.post
                        newton(step, dve, base(ph, "inv") + 1, STAT, D, inv[:, 0:tk], tmp[:, 0, 0:tk])
                        dve.wait_ge(done["made"], base(ph, "made"))

                        def gated(c):
                            dve.tensor_tensor(work[:, c, 0:tk], work[:, c, 0:tk], inv[:, 0:tk], ALU.mult)\
                               .then_inc(done["gated"], 1)

                        gated(0)
                        for c in range(KC):
                            if c + 1 < KC:
                                gated(c + 1)
                            if c not in POOL_CHUNKS:
                                dve.wait_ge(done["gated"], base(ph, "gated") + c + 1)
                                dve.tensor_tensor(x[:, c, 0:tk], x[:, c, 0:tk], work[:, c, 0:tk], ALU.add)\
                                   .then_inc(done["x"], 1)
                    if ph.pre:
                        l, sub = ph.pre
                        if not ph.post:
                            split_lo(Idx(0, 0, 0))
                        newton(step, dve, base(ph, "inv") + (2 if ph.post else 1), STAT, D, inv[:, 0:tk],
                               tmp[:, 0, 0:tk])

                        for c in POOL_CHUNKS if ph.post else ():
                            dve.wait_ge(done["xp"], residual(ph, c)[1])

                        def scaled(c):
                            dve.tensor_tensor(work[:, c, 0:tk], x[:, c, 0:tk], inv[:, 0:tk], ALU.mult)\
                               .then_inc(done["scaled"], 1)

                        scaled(0)
                        scaled(1)
                        for c in range(KC):
                            if c + 2 < KC:
                                scaled(c + 2)
                            dve.wait_ge(done["xhi"], base(ph, "xhi") + c + 1)
                            dve.tensor_tensor(xlo[:, c, 0:tk], work[:, c, 0:tk], xhi[:, c, 0:tk].bitcast(F32),
                                              ALU.subtract).then_inc(done["xlo"], 1)
                    if not ph.post:
                        dve.wait_ge(lam_exp, 1)
                        for l in range(LAYERS):
                            step(dve.scalar_tensor_tensor(lam[:, l:l + 1], elam[:, l, 0:1], lambda_init[l],
                                                          elam[:, l, 1:2], ALU.add, ALU.subtract))
                elif ph.kind == "ffn_in":
                    def body(i, count, first, ph=ph, tk=tk):
                        for j in range(2):
                            g = Idx(ph.g + 2 * j, ph.groups, i)
                            a, b = bank(ph, i, 2 * j), bank(ph, i, 2 * j + 1)
                            p = Idx(base(ph, "ghi") + j, 2, i)
                            split_lo(g.plus(1))
                            split_lo(g.plus(2))
                            dve.wait_ge(bank_free[a.ring(BANKS)], a.lap(BANKS, 1))
                            dve.wait_ge(group_used, last_group(ph, i, 2 * j + 1).val(1))
                            dve.tensor_tensor(tmp[:, 1, 0:tk], tmp[:, 0, 0:tk], ps[:, b.ring(BANKS), 0:tk],
                                              ALU.mult).then_inc(bank_free[b.ring(BANKS)], 1)
                            for n in range(count // 2):
                                ada_block(Idx(first + j * count // 2 + n, count, i))
                            dve.wait_ge(done["ghi"], p.val(1))
                            c = Idx(j, 2, i)
                            dve.tensor_tensor(chunk(glo, c, tk), tmp[:, 1, 0:tk], chunk(ghi, c, tk).bitcast(F32),
                                              ALU.subtract).then_inc(done["glo"], 1)

                    counts = blocks_per_body(ph)
                    spreads += 1
                    start, block = 0, ada_order.index(ph.vectors[0]) * KC
                    while start < ph.iters:
                        end = start + 1
                        while end < ph.iters and counts[end] == counts[start] and not (ph.peel_first and start == 0):
                            end += 1
                        count = counts[start]
                        if end - start > 1:
                            with dve.Fori(start, end) as i:
                                body(i, count, block - start * count)
                        else:
                            body(start, count, block - start * count)
                        block += (end - start) * count
                        start = end
                    finish_vectors(ph)
                elif ph.kind == "y":
                    def body(i, ph=ph):
                        for j in range(ph.groups):
                            split_lo(Idx(ph.g + j + 1, ph.groups, i))

                    run(dve, ph, body)
                elif ph.kind == "rope":
                    start = steps

                    def body(i, ph=ph, start=start):
                        for j in range(ph.tiles):
                            split_ahead(split_lo, ph, i, j)
                            n = bank(ph, i, j)
                            r = Idx(base(ph, "rope") + j, ph.tiles, i)
                            st = Idx(start + 2 * j, 2 * ph.tiles, i)
                            a = tmp[:, r.ring(2), 0:S]
                            b = tmp[:, r.ring(2), S:T]
                            dve.wait_ge(bank_free[n.ring(BANKS)], n.lap(BANKS, 1))
                            dve.stream_shuffle(b, a, [(m + 16) % 32 for m in range(32)]).then_inc(dve_step, 1)
                            dve.wait_ge(dve_step, st.val(1))
                            dve.tensor_tensor(b, b, sin[:, :], ALU.mult).then_inc(dve_step, 1)
                            dve.wait_ge(dve_step, st.val(2))
                            dve.wait_ge(rope_mul, r.val(1))
                            dve.tensor_tensor(rope_dst(ph, i, j, slice(0, S)),
                                              acc[:, r.ring(2) * S:(r.ring(2) + 1) * S], b, ALU.add)\
                               .then_inc(done["rope"], 1)

                    for i in range(ph.iters):
                        body(i)
                    steps += 2 * ph.tiles * ph.iters
                elif ph.kind == "plain":
                    for j in range(ph.tiles):
                        split_ahead(split_lo, ph, 0, j)
                elif ph.kind == "v":
                    spreads += bool(ph.vectors)
                    first = ada_order.index(ph.vectors[0]) * KC if ph.vectors else 0
                    assert len(ph.vectors) * KC in (0, ph.iters * ph.groups)

                    def body(i, ph=ph, first=first):
                        for j in range(ph.groups):
                            split_lo(Idx(ph.g + j + 1, ph.groups, i))
                            if ph.vectors:
                                ada_block(Idx(first + j, ph.groups, i))

                    run(dve, ph, body)
                    if ph.vectors:
                        finish_vectors(ph)
                elif ph.kind == "merge":
                    def body(i, ph=ph, tk=tk):
                        for j in range(2):
                            g = Idx(ph.g + 2 * j, ph.groups, i)
                            a, b = bank(ph, i, 2 * j), bank(ph, i, 2 * j + 1)
                            split_lo(g.plus(1))
                            split_lo(g.plus(2))
                            dve.wait_ge(bank_free[a.ring(BANKS)], a.lap(BANKS, 1))
                            dve.wait_ge(group_used, last_group(ph, i, 2 * j + 1).val(1))
                            c = Idx(j, 2, i)
                            dst = chunk(work, c, tk) if ph.r == 0 else tmp[:, 1, 0:tk]
                            dve.tensor_tensor(dst, tmp[:, 0, 0:tk], ps[:, b.ring(BANKS), 0:tk], ALU.mult)\
                               .then_inc(bank_free[b.ring(BANKS)], 1)
                            if ph.r:
                                dve.wait_ge(bank_free[b.ring(BANKS)], b.lap(BANKS, 1))
                                dve.tensor_tensor(chunk(work, c, tk), chunk(work, c, tk), tmp[:, 1, 0:tk], ALU.add)\
                                   .then_inc(done["m"], 1)

                    run(dve, ph, body)
                elif ph.kind == "msplit":
                    for c in range(KC):
                        dve.wait_ge(done["mhi"], base(ph, "mhi") + c + 1)
                        dve.tensor_tensor(ylo[:, c, 0:tk], work[:, c, 0:tk], yhi[:, c, 0:tk].bitcast(F32),
                                          ALU.subtract).then_inc(done["mlo"], 1)
                elif ph.kind == "latnorm":
                    dve.wait_ge(done["stat"], base(ph, "stat") + QC + KVC)
                    count = base(ph, "inv") + 1
                    rms = [(inv[:, :], tmp[:, 0, :], 4, Q_RANK), (acc[:, :], tmp[:, 1, :], 5, KV_RANK)]
                    for n, (dst, var, bank_, width) in enumerate(rms):
                        newton(step, dve, count + n, bank_, width, dst, var)

                    def normed(c):
                        dve.scalar_tensor_tensor(lat[:, c, :], lat[:, c, :], lat_g[:, ph.layer, c:c + 1],
                                                 (inv if c < QC else acc)[:, :], ALU.mult, ALU.mult)\
                           .then_inc(done["lt"], 1)

                    normed(0)
                    for c in range(QC + KVC):
                        if c + 1 < QC + KVC:
                            normed(c + 1)
                        dve.wait_ge(done["lhi"], base(ph, "lhi") + c + 1)
                        dve.tensor_tensor(llo[:, c, :], lat[:, c, :], lhi[:, c, :].bitcast(F32), ALU.subtract)\
                           .then_inc(done["llo"], 1)
                elif ph.kind == "attn":
                    dve_attention(dve, ph, step)

        @block.tensor
        def _(pe):
            def shift_products(blocks):
                pe.wait_ge(silu_c, 1)
                for block in blocks:
                    if block % ADA_PAIR == 0:
                        pe.wait_ge(shift_w_loaded[block // ADA_PAIR], 16)
                    for c in range(KC):
                        last = pe.matmul(ps[:, ADA_BANK, 2 * block:2 * block + 2],
                                         shift_w[:, block, c * P:(c + 1) * P], cvec[:, c, :],
                                         start=c == 0, stop=c == KC - 1)
                last.then_inc(first_shift, 1)

            def stat(ph, before):
                wait(pe, done["refined"], base(ph, "inv") + before)
                wait(pe, done["pt"], base(ph, "pt"))
                pe.matmul(ps[:, STAT, 0:ph.tokens], ones[:, :], acc[:, 0:ph.tokens], start=True, stop=True)\
                  .then_inc(done["stat"], 1)

            def group_pieces(ph, j):
                if ph.src == "ffn_out":
                    tile, part = divmod(j, 3)
                    n = KC if part < 2 else FC - 2 * KC
                    return [(tile, KC * part + c, c * P, part == 0 and c == 0, part == 2 and c == n - 1)
                            for c in range(n)]
                per, depth = ph.tiles // ph.groups, {"uq": QC, "uk": KVC}.get(ph.src, KC)
                return [(per * j + t, c, (t * depth + c) * P, c == 0, c == depth - 1)
                        for t in range(per) for c in range(depth)]

            def moving(ph, tile):
                tk, j = ph.tokens, tile
                if ph.kind == "merge" and j % 2:
                    return yhi, ylo, 0, "ylo", None
                if ph.src == "ffn_out":
                    return ghi, glo, 0, "glo", FC
                if ph.src == "wo":
                    return yhi, ylo, 0, "mlo", KC
                if ph.src == "uq":
                    return lhi, llo, 0, "llo", QC + KVC
                if ph.src == "uk":
                    return lhi, llo, QC, "llo", QC + KVC
                return xhi, xlo, 0, "xlo", KC

            def group_products(ph, i, j):
                g = Idx(ph.g + j, ph.groups, i)
                s = g.ring(SPLIT)
                pieces = group_pieces(ph, j)
                tk = ph.tokens
                for tile, c, col, start, stop in pieces:
                    hi, lo, first, ready, chunks = moving(ph, tile)
                    n = bank(ph, i, tile)
                    if start:
                        wait(pe, bank_free[n.ring(BANKS)], n.lap(BANKS))
                    if tile == 0 or (ph.kind == "merge" and tile == 1 and c == 0):
                        pe.wait_ge(done[ready], base(ph, ready) if chunks is None else
                                   base(ph, ready) - chunks + first + c + 1)
                    if (tile, c) == pieces[0][:2]:
                        pe.wait_ge(hi_ready, g.val(1))
                    o = ps[:, n.ring(BANKS), 0:tk]
                    w = whi[:, s, col:col + P]
                    pe.matmul(o, w, hi[:, first + c, 0:tk], start=start, stop=False)
                    pe.matmul(o, w, lo[:, first + c, 0:tk], start=False, stop=False)
                pe.wait_ge(lo_ready, g.val(1))
                for tile, c, col, start, stop in pieces:
                    hi, lo, first, _, _ = moving(ph, tile)
                    n = bank(ph, i, tile)
                    last = pe.matmul(ps[:, n.ring(BANKS), 0:tk], wlo[:, s, col:col + P], hi[:, first + c, 0:tk],
                                     start=False, stop=stop)
                last.then_inc(group_used, 1)

            def token_products(ph, i, j):
                g = Idx(ph.g + j, ph.groups, i)
                s = g.ring(SPLIT)
                hi, lo, first = (lhi, llo, QC) if ph.x == "lat" else (xhi, xlo, 0)
                pe.wait_ge(hi_ready, g.val(1))
                for low in range(2):
                    if low:
                        pe.wait_ge(lo_ready, g.val(1))
                    for t in range(T // P):
                        n = bank(ph, i, t)
                        if j == 0 and not low:
                            wait(pe, bank_free[n.ring(BANKS)], n.lap(BANKS))
                        o = ps[:, n.ring(BANKS), 0:ph.cols]
                        for c in range(ph.kpg):
                            kc = first + j * ph.kpg + c
                            cols = slice(c * ph.cols, (c + 1) * ph.cols)
                            tokens = slice(t * P, (t + 1) * P)
                            if low:
                                last = pe.matmul(o, hi[:, kc, tokens], wlo[:, s, cols], start=False,
                                                 stop=j == ph.groups - 1 and c == ph.kpg - 1)
                            else:
                                pe.matmul(o, hi[:, kc, tokens], whi[:, s, cols], start=j == 0 and c == 0,
                                          stop=False)
                                pe.matmul(o, lo[:, kc, tokens], whi[:, s, cols], start=False, stop=False)
                last.then_inc(group_used, 1)

            for ph in plan:
                if ph.kind == "norm":
                    if ph.post:
                        pe.wait_ge(done["acc"], base(ph, "acc"))
                        stat(ph, 0)
                    else:
                        shift_products(range(KC - ADA_PAIR))
                    if ph.pre:
                        wait(pe, done["refined"], base(ph, "inv") + (1 if ph.post else 0))
                        for c in range(KC):
                            pe.wait_ge(done["xsq"], base(ph, "xsq") + c + 1)
                            pe.matmul(ps[:, STAT, 0:ph.tokens], ones[:, :], tmp[:, c % 2, 0:ph.tokens],
                                      start=c == 0, stop=c == KC - 1).then_inc(done["xsum"], 1)
                    if not ph.post:
                        shift_products(range(KC - ADA_PAIR, KC))
                        pe.wait_ge(consts_made, 2 + 2 * LAYERS)
                        pe.wait_ge(done["refined"], 1)
                        pe.matmul(ps[:, STAT, 0:2 * LAYERS], ones[0:64, :],
                                  dprod[:, :, :].rearrange("p l n -> p (l n)"), start=True, stop=True)\
                          .then_inc(lam_sum, 1)
                elif ph.kind == "latnorm":
                    wait(pe, done["pt"], base(ph, "pt"))
                    wait(pe, done["refined"], base(ph, "inv"))
                    for c in range(QC + KVC):
                        pe.wait_ge(done["lsq"], base(ph, "lsq") + c + 1)
                        pe.matmul(ps[:, 4 if c < QC else 5, :], ones[:, :], tmp[:, c % 2, :],
                                  start=c in (0, QC), stop=c in (QC - 1, QC + KVC - 1)).then_inc(done["stat"], 1)
                elif ph.kind == "attn":
                    pe_attention(pe, ph)
                elif ph.iters:
                    wait(pe, done["exp"], base(ph, "exp"))
                    if ph.kind == "v":
                        def body(i, ph=ph):
                            for j in range(ph.groups):
                                token_products(ph, i, j)
                    else:
                        def body(i, ph=ph):
                            for j in range(ph.groups):
                                group_products(ph, i, j)

                    run(pe, ph, body)



def blocked(w):
    *lead, k, m = w.shape
    n = len(lead)
    w = w.reshape(*lead, k // P, P, m // P, P)
    w = w.transpose(*range(n), n + 2, n + 1, n, n + 3)
    return w.reshape(*lead, m // P, P, k)


def by_rows(w, cols, kpg):
    l, k, m = w.shape
    w = w.reshape(l, k // P // kpg, kpg, P, m // cols, cols)
    return w.transpose(0, 4, 1, 3, 2, 5).reshape(l, -1, P, kpg * cols)


def layout(x, c, ctx, c_ctx, ada_w, ada_b, norm_g, ffn_w_in, ffn_w_out, mix_w_in, diff_lambda, diff_subln_g,
           win_sink, mla_q_norm_g, mla_kv_norm_g, mla_w_uq, mla_w_ukv, branch_w, mix_w_out):
    L = LAYERS
    a = {}
    a["x"] = np.concatenate([x[0], ctx[0]], 0).T.reshape(KC, P, T).transpose(1, 0, 2)
    a["cvec"] = np.stack([c[0], c_ctx], -1).reshape(KC, P, 2).transpose(1, 0, 2)
    a["c_rows"] = np.concatenate([c[0], c_ctx])[None, :]
    a["shift_w"] = blocked(ada_w[0][:, :D]).reshape(-1, ADA_PAIR, P, D).transpose(0, 2, 1, 3)
    a["scale_w"] = ada_w[0][:, D:2 * D].T.reshape(-1, ADA_PAIR, P, D).transpose(0, 2, 1, 3)
    a["ada_rows"] = ada_w.transpose(0, 2, 1).reshape(-1, P, D)[FIRST_ADA * KC:]
    a["ada_b"] = np.repeat(ada_b.reshape(L, N_MOD, KC, P).transpose(3, 0, 1, 2)[..., None], 2, -1)
    a["norm_g"] = np.repeat(norm_g.reshape(L, 6, KC, P).transpose(3, 0, 1, 2)[..., None], 2, -1)
    ab = blocked(ffn_w_in).reshape(L, 2, 2, FC, P, D).transpose(0, 1, 3, 2, 4, 5)
    a["ffn_in"] = ab.reshape(L, 2, 2 * FC, P, D)
    a["ffn_out"] = blocked(ffn_w_out)
    cuts = np.cumsum([D, D, D, D, 256, 256, Q_RANK, KV_RANK, ROPE])
    aq, ak, av, bq, bk, bv, cq, ckv, ckr, gates = np.split(mix_w_in, cuts, axis=-1)
    a["qk_a"] = np.concatenate([blocked(aq), blocked(ak)], 1)
    a["v_a"] = by_rows(av, 512, 2)
    bq = bq.reshape(L, D, 2, 2, 4, 64).transpose(0, 1, 2, 4, 3, 5).reshape(L, D, D)
    a["qk_b"] = np.concatenate([blocked(bq), blocked(bk)], 1)
    a["v_b"] = by_rows(bv, 256, 4)
    a["c_lat"] = np.concatenate([blocked(cq), blocked(ckv), blocked(np.concatenate([ckr, ckr], -1))], 1)
    uq = mla_w_uq.reshape(L, Q_RANK, 8, 192)
    uq = np.concatenate([uq[..., :128].reshape(L, Q_RANK, D), uq[..., 128:].reshape(L, Q_RANK, 512)], -1)
    a["uq"] = blocked(uq).reshape(L, 6, 2, P, Q_RANK).transpose(0, 1, 3, 2, 4).reshape(L, 6, P, 2 * Q_RANK)
    ukv = mla_w_ukv.reshape(L, KV_RANK, 8, 256)
    uk = blocked(ukv[..., :128].reshape(L, KV_RANK, D))
    a["uk"] = uk.reshape(L, 2, 4, P, KV_RANK).transpose(0, 1, 3, 2, 4).reshape(L, 2, P, 4 * KV_RANK)
    a["uv"] = by_rows(ukv[..., 128:].reshape(L, KV_RANK, D), 512, 2)
    bw = branch_w.reshape(L, 3, D, D)
    win = bw[:, 1].reshape(L, 2, 2, 4, 64, D).transpose(0, 1, 3, 2, 4, 5).reshape(L, D, D)
    bw = np.stack([bw[:, 0], win, bw[:, 2]], 1)
    gates = gates.reshape(L, D, 3, D).transpose(0, 2, 1, 3)
    a["merge"] = np.stack([blocked(gates), blocked(bw)], 3).reshape(L, 3, 2 * KC, P, D)
    a["wo"] = blocked(mix_w_out)
    a["subg"] = diff_subln_g.T
    lat_g = np.concatenate([mla_q_norm_g, mla_kv_norm_g], -1)
    a["lat_g"] = lat_g.reshape(L, QC + KVC, P).transpose(2, 0, 1)
    a["dlam"] = diff_lambda.transpose(2, 0, 1)
    a["sink"] = win_sink.reshape(L, 2, 2, 4).transpose(0, 1, 3, 2).reshape(1, L * 16)

    token = np.arange(S)
    quarter = ROPE // 4
    freq = (1.0 / (np.float32(10000.0) ** (np.arange(quarter, dtype=np.float32) / np.float32(quarter))))
    freq = freq.astype(np.float32)
    row, col = (token // GRID_W).astype(np.float32), (token % GRID_W).astype(np.float32)
    angles = np.concatenate([freq[:, None] * row] * 2 + [freq[:, None] * col] * 2, 0).astype(np.float32)
    sign = np.where(np.arange(ROPE) // quarter % 2 == 0, -1.0, 1.0)[:, None].astype(np.float32)
    a["cos"] = np.concatenate([np.cos(angles)] * 2, 0).astype(np.float32)
    a["sin"] = np.concatenate([np.sin(angles) * sign] * 2, 0).astype(np.float32)
    a["ident"] = np.eye(P, dtype=np.float32)
    i = np.arange(P)
    later, earlier = i[None, :] > i[:, None], i[None, :] < i[:, None]
    a["mask"] = np.where(np.stack([later, earlier], 1), np.float32(NEG), np.float32(0.0)).astype(np.float32)
    return {name: np.ascontiguousarray(t) for name, t in a.items()}


def kernel(**inputs):
    import concourse.bacc as bacc
    from concourse.bass_utils import run_bass_kernel_spmd

    arrays = layout(**{name: np.asarray(t) for name, t in inputs.items()})
    nc = bacc.Bacc("TRN2", target_bir_lowering=False, num_devices=1)
    io = {name: nc.dram_tensor(f"in_{name}", t.shape, F32, kind="ExternalInput").ap()
          for name, t in arrays.items()}
    out = nc.dram_tensor("out", (P, KC, S), F32, kind="ExternalOutput").ap()
    silu_rows = nc.dram_tensor("silu_rows", (1, 2 * D), F32).ap()
    build(nc, io, silu_rows, out)
    r = run_bass_kernel_spmd(nc, [{f"in_{name}": t for name, t in arrays.items()}], core_ids=[0])
    y = r.results[0]["out"]
    return y.transpose(2, 1, 0).reshape(1, S, D)
```
